# Optimizing a Trainium2 kernel written in Bass

```python
import math
import jax, jax.numpy as jnp
from jax import lax
import numpy as np

D_MODEL = 1024
BATCH = 1
SEQ = 512
DEPTH = 2
DEC_BATCH = 8
DEC_SEQ = 1
PAST_LEN = 4096
PAGE_SIZE = 128

D_MIX = D_MODEL
N_MIXERS = 4
W_GROUP = D_MIX // N_MIXERS
N_HEADS = 4
HEAD_DIM = W_GROUP // N_HEADS
GDN_CONV = 4
SC_CONV = 3
GLA_RANK = 16
GLA_NORMALIZER = 16.0
CHUNK = 64
D_FF = 2816
N_EXPERTS = 8
TOP_K = 2
D_FF_EXPERT = 1408
N_DENSE = (DEPTH + 1) // 2
N_MOE = DEPTH // 2
EPS = 1e-6
N_STATE = 7

SPLIT_SIZES = (
    [W_GROUP] * 4 + [N_HEADS] * 2 +
    [W_GROUP] * 4 + [N_HEADS] * 2 +
    [W_GROUP] * 3 +
    [W_GROUP] * 4 + [GLA_RANK]
)
D_IN = sum(SPLIT_SIZES)

kernel_name = 'hybrid_mlstm_gdn_conv_gla_step'

def _split(z, sizes):
    idx, acc = [], 0
    for s in sizes[:-1]:
        acc += s
        idx.append(acc)
    return jnp.split(z, idx, axis=-1)

def _rmsnorm(x, g):
    xf = x.astype(jnp.float32)
    xf = xf * lax.rsqrt(jnp.mean(xf * xf, axis=-1, keepdims=True) + EPS)
    return (xf * g.astype(jnp.float32)).astype(x.dtype)

def _headnorm(o, w):
    o = o * lax.rsqrt(jnp.mean(o * o, axis=-1, keepdims=True) + EPS)
    b, h, l, d = o.shape
    return o.transpose(0, 2, 1, 3).reshape(b, l, h * d) * w.astype(jnp.float32)

def _l2norm(x):
    return x * lax.rsqrt(jnp.sum(x * x, axis=-1, keepdims=True) + EPS)

def _causal_conv(u, buf, w):
    width = w.shape[-1]
    L = u.shape[1]
    w = w.astype(u.dtype)
    xp = jnp.concatenate([buf, u], axis=1)
    y = xp[:, 0:L] * w[:, 0]
    for j in range(1, width):
        y = y + xp[:, j:j + L] * w[:, j]
    return y, xp[:, L:]

def _to_chunks(a, c):
    b, h, L = a.shape[:3]
    a = a.reshape(b, h, L // c, c, *a.shape[3:])
    return jnp.moveaxis(a, 2, 0)

def _from_chunks(a):
    a = jnp.moveaxis(a, 0, 2)
    return a.reshape(a.shape[0], a.shape[1], -1, a.shape[-1])

def _mlstm(q, k, v, ig, fg, C0, n0, m0):
    L = q.shape[2]
    c = math.gcd(L, CHUNK)
    k = k * HEAD_DIM ** -0.5
    logf = jax.nn.log_sigmoid(fg)
    incl = jnp.tril(jnp.ones((c, c), dtype=bool))

    def step(carry, inp):
        C, n, m = carry
        qc, kc, vc, ic, lf = inp
        b = jnp.cumsum(lf, axis=-1)
        a = b + m[..., None]
        D = jnp.where(incl, b[..., :, None] - b[..., None, :] + ic[..., None, :], -jnp.inf)
        mt = jnp.maximum(a, jnp.max(D, axis=-1))
        w_int = jnp.exp(a - mt)
        s = jnp.einsum('bhtd,bhsd->bhts', qc, kc) * jnp.exp(D - mt[..., None])
        num = w_int[..., None] * jnp.einsum('bhtd,bhde->bhte', qc, C) + jnp.einsum('bhts,bhse->bhte', s, vc)
        den = w_int * jnp.einsum('bhtd,bhd->bht', qc, n) + jnp.sum(s, axis=-1)
        h = num / jnp.maximum(jnp.abs(den), jnp.exp(-mt))[..., None]
        a_end = b[..., -1] + m
        g = b[..., -1:] - b + ic
        m_new = jnp.maximum(a_end, jnp.max(g, axis=-1))
        wg = jnp.exp(g - m_new[..., None])
        dec = jnp.exp(a_end - m_new)
        C_new = dec[..., None, None] * C + jnp.einsum('bhs,bhsd,bhse->bhde', wg, kc, vc)
        n_new = dec[..., None] * n + jnp.einsum('bhs,bhsd->bhd', wg, kc)
        return (C_new, n_new, m_new), h

    (C, n, m), hs = lax.scan(step, (C0, n0, m0),
                             (_to_chunks(q, c), _to_chunks(k, c), _to_chunks(v, c),
                              _to_chunks(ig, c), _to_chunks(logf, c)))
    return _from_chunks(hs), C, n, m

def _gated_delta(q, k, v, g, beta, S0):
    L = q.shape[2]
    c = math.gcd(L, CHUNK)
    q = q * HEAD_DIM ** -0.5
    dv = v.shape[-1]
    incl = jnp.tril(jnp.ones((c, c), dtype=bool))
    strict = jnp.tril(jnp.ones((c, c), dtype=bool), k=-1)

    def step(S, inp):
        qc, kc, vc, gc, bc = inp
        G = jnp.cumsum(gc, axis=-1)
        Lw = jnp.exp(jnp.where(incl, G[..., :, None] - G[..., None, :], -jnp.inf))
        kk = jnp.einsum('bhtd,bhsd->bhts', kc, kc)
        A = jnp.where(strict, bc[..., :, None] * kk * Lw, 0.0)
        rhs = jnp.concatenate([bc[..., None] * vc, (bc * jnp.exp(G))[..., None] * kc], axis=-1)
        sol = lax.linalg.triangular_solve(A, rhs, left_side=True, lower=True, unit_diagonal=True)
        U, W = sol[..., :dv], sol[..., dv:]
        Vn = U - jnp.einsum('bhtd,bhde->bhte', W, S)
        qk = jnp.einsum('bhtd,bhsd->bhts', qc, kc) * Lw
        o = jnp.einsum('bhtd,bhde->bhte', qc * jnp.exp(G)[..., None], S) + jnp.einsum('bhts,bhse->bhte', qk, Vn)
        G_last = G[..., -1]
        S_new = jnp.exp(G_last)[..., None, None] * S + jnp.einsum(
            'bhsd,bhse->bhde', kc * jnp.exp(G_last[..., None] - G)[..., None], Vn)
        return S_new, o

    S, os_ = lax.scan(step, S0, (_to_chunks(q, c), _to_chunks(k, c), _to_chunks(v, c),
                                 _to_chunks(g, c), _to_chunks(beta, c)))
    return _from_chunks(os_), S

def _gla(q, k, v, gk, S0):
    L = q.shape[2]
    c = math.gcd(L, CHUNK)
    q = q * HEAD_DIM ** -0.5
    incl = jnp.tril(jnp.ones((c, c), dtype=bool))[..., None]

    def step(S, inp):
        qc, kc, vc, gc = inp
        G = jnp.cumsum(gc, axis=2)
        dec = jnp.exp(jnp.where(incl, G[:, :, :, None, :] - G[:, :, None, :, :], -jnp.inf))
        A = jnp.einsum('bhtd,bhsd,bhtsd->bhts', qc, kc, dec)
        o = jnp.einsum('bhtd,bhde->bhte', qc * jnp.exp(G), S) + jnp.einsum('bhts,bhse->bhte', A, vc)
        G_last = G[:, :, -1]
        S_new = jnp.exp(G_last)[..., None] * S + jnp.einsum(
            'bhsd,bhse->bhde', kc * jnp.exp(G_last[:, :, None] - G), vc)
        return S_new, o

    S, os_ = lax.scan(step, S0, (_to_chunks(q, c), _to_chunks(k, c), _to_chunks(v, c), _to_chunks(gk, c)))
    return _from_chunks(os_), S

def _mix(h, st, w_in, mlstm_b_i, mlstm_b_f, mlstm_norm, gdn_conv_w, gdn_a_log, gdn_dt_bias, gdn_norm,
         sc_conv_w, gla_w_gate, gla_b_gate, gla_norm, w_out):
    f32 = jnp.float32
    dt = h.dtype
    bn, L = h.shape[:2]
    C0, n0, m0, Sg0, gbuf0, sbuf0, Sl0 = [s.astype(f32) for s in st]
    z = jnp.einsum('bld,de->ble', h, w_in).astype(f32)
    (mq, mk, mv, mo, mi, mf, gq, gk, gv, gz, ga, gb, sb, sc, sh, lq, lk, lv, lr, lg) = _split(z, SPLIT_SIZES)

    def heads(a):
        return a.reshape(bn, L, N_HEADS, -1).transpose(0, 2, 1, 3)

    def per_head(a):
        return a.transpose(0, 2, 1)

    hm, C1, n1, m1 = _mlstm(heads(mq), heads(mk), heads(mv), per_head(mi + mlstm_b_i.astype(f32)),
                            per_head(mf + mlstm_b_f.astype(f32)), C0, n0, m0)
    y_a = jax.nn.sigmoid(mo) * _headnorm(hm, mlstm_norm)

    qkv, gbuf1 = _causal_conv(jnp.concatenate([gq, gk, gv], axis=-1), gbuf0, gdn_conv_w)
    cq, ck, cv = jnp.split(jax.nn.silu(qkv), 3, axis=-1)
    decay = -jnp.exp(gdn_a_log.astype(f32)) * jax.nn.softplus(ga + gdn_dt_bias.astype(f32))
    ho, Sg1 = _gated_delta(_l2norm(heads(cq)), _l2norm(heads(ck)), heads(cv), per_head(decay),
                           per_head(jax.nn.sigmoid(gb)), Sg0)
    y_b = _headnorm(ho, gdn_norm) * jax.nn.silu(gz)

    cu, sbuf1 = _causal_conv(sc * sh, sbuf0, sc_conv_w)
    y_c = sb * cu

    gate_log = jax.nn.log_sigmoid(lg @ gla_w_gate.astype(f32) + gla_b_gate.astype(f32)) / GLA_NORMALIZER
    hl, Sl1 = _gla(heads(lq), heads(lk), heads(lv), heads(gate_log), Sl0)
    y_d = _headnorm(hl, gla_norm) * jax.nn.silu(lr)

    y = jnp.concatenate([y_a, y_b, y_c, y_d], axis=-1).astype(dt)
    y = jnp.einsum('ble,ed->bld', y, w_out)
    new = (C1, n1, m1, Sg1, gbuf1, sbuf1, Sl1)
    return y, [s.astype(dt) for s in new]

def _swiglu(h, wg, wu, wd):
    return (jax.nn.silu(h @ wg) * (h @ wu)) @ wd

def _moe(h, w_router, b_router, w_g, w_u, w_d):
    logits = (h @ w_router).astype(jnp.float32) + b_router.astype(jnp.float32)
    probs = jax.nn.softmax(logits, axis=-1)
    topv, topi = lax.top_k(probs, TOP_K)
    topv = topv / jnp.sum(topv, axis=-1, keepdims=True)
    gates = jnp.sum(jax.nn.one_hot(topi, N_EXPERTS, dtype=jnp.float32) * topv[..., None], axis=-2)
    y = jnp.zeros(h.shape, jnp.float32)
    for e in range(N_EXPERTS):
        y = y + gates[..., e:e + 1] * _swiglu(h, w_g[e], w_u[e], w_d[e]).astype(jnp.float32)
    return y.astype(h.dtype)

def _trunk(x, states, params):
    (w_in, g_mix, mlstm_b_i, mlstm_b_f, mlstm_norm, gdn_conv_w, gdn_a_log, gdn_dt_bias, gdn_norm,
     sc_conv_w, gla_w_gate, gla_b_gate, gla_norm, w_out, g_ffn, ffn_w_gate, ffn_w_up, ffn_w_down,
     moe_w_router, moe_b_router, moe_w_gate, moe_w_up, moe_w_down, g_final) = params
    per_layer = []
    for l in range(DEPTH):
        h = _rmsnorm(x, g_mix[l])
        y, st = _mix(h, [s[l] for s in states], w_in[l], mlstm_b_i[l], mlstm_b_f[l], mlstm_norm[l],
                     gdn_conv_w[l], gdn_a_log[l], gdn_dt_bias[l], gdn_norm[l], sc_conv_w[l],
                     gla_w_gate[l], gla_b_gate[l], gla_norm[l], w_out[l])
        x = x + y
        h = _rmsnorm(x, g_ffn[l])
        j = l // 2
        if l % 2 == 0:
            x = x + _swiglu(h, ffn_w_gate[j], ffn_w_up[j], ffn_w_down[j])
        else:
            x = x + _moe(h, moe_w_router[j], moe_b_router[j], moe_w_gate[j], moe_w_up[j], moe_w_down[j])
        per_layer.append(st)
    new_states = [jnp.stack([st[i] for st in per_layer]) for i in range(N_STATE)]
    return _rmsnorm(x, g_final), new_states

def _zero_states(bn, dtype):
    return [jnp.zeros((DEPTH, bn, N_HEADS, HEAD_DIM, HEAD_DIM), dtype),
            jnp.zeros((DEPTH, bn, N_HEADS, HEAD_DIM), dtype),
            jnp.zeros((DEPTH, bn, N_HEADS), dtype),
            jnp.zeros((DEPTH, bn, N_HEADS, HEAD_DIM, HEAD_DIM), dtype),
            jnp.zeros((DEPTH, bn, GDN_CONV - 1, 3 * W_GROUP), dtype),
            jnp.zeros((DEPTH, bn, SC_CONV - 1, W_GROUP), dtype),
            jnp.zeros((DEPTH, bn, N_HEADS, HEAD_DIM, HEAD_DIM), dtype)]

def setup_inputs(seed: int = 0) -> dict:
    key = jax.random.key(seed)
    keys = jax.random.split(key, 64)
    counter = [0]
    f32 = jnp.float32

    def nk():
        counter[0] += 1
        return keys[counter[0] - 1]

    def nrm(shape, scale):
        return scale * jax.random.normal(nk(), shape, f32)

    def gain(shape):
        return 1.0 + nrm(shape, 0.02)

    inp = {}
    inp['x_prompt'] = nrm((BATCH, SEQ, D_MODEL), 1.0)
    inp['x_sample'] = nrm((DEC_BATCH, DEC_SEQ, D_MODEL), 1.0)
    inp['state_mlstm_C'] = nrm((DEPTH, DEC_BATCH, N_HEADS, HEAD_DIM, HEAD_DIM), 1.0)
    inp['state_mlstm_n'] = nrm((DEPTH, DEC_BATCH, N_HEADS, HEAD_DIM), 1.0)
    inp['state_mlstm_m'] = nrm((DEPTH, DEC_BATCH, N_HEADS), 1.0)
    inp['state_gdn_S'] = nrm((DEPTH, DEC_BATCH, N_HEADS, HEAD_DIM, HEAD_DIM), 0.1)
    inp['state_gdn_conv'] = nrm((DEPTH, DEC_BATCH, GDN_CONV - 1, 3 * W_GROUP), 1.0)
    inp['state_sc_conv'] = nrm((DEPTH, DEC_BATCH, SC_CONV - 1, W_GROUP), 1.0)
    inp['state_gla_S'] = nrm((DEPTH, DEC_BATCH, N_HEADS, HEAD_DIM, HEAD_DIM), 0.5)
    inp['w_in'] = nrm((DEPTH, D_MODEL, D_IN), D_MODEL ** -0.5)
    inp['g_mix'] = gain((DEPTH, D_MODEL))
    inp['mlstm_b_i'] = nrm((DEPTH, N_HEADS), 0.1)
    inp['mlstm_b_f'] = jnp.linspace(3.0, 6.0, N_HEADS, dtype=f32)[None, :] + nrm((DEPTH, N_HEADS), 0.1)
    inp['mlstm_norm'] = gain((DEPTH, W_GROUP))
    inp['gdn_conv_w'] = nrm((DEPTH, 3 * W_GROUP, GDN_CONV), GDN_CONV ** -0.5)
    inp['gdn_a_log'] = jnp.log(jax.random.uniform(nk(), (DEPTH, N_HEADS), f32, 1.0, 16.0))
    dt0 = jnp.exp(jax.random.uniform(nk(), (DEPTH, N_HEADS), f32, math.log(1e-3), math.log(1e-1)))
    inp['gdn_dt_bias'] = dt0 + jnp.log(-jnp.expm1(-dt0))
    inp['gdn_norm'] = gain((DEPTH, W_GROUP))
    inp['sc_conv_w'] = nrm((DEPTH, W_GROUP, SC_CONV), SC_CONV ** -0.5)
    inp['gla_w_gate'] = nrm((DEPTH, GLA_RANK, W_GROUP), GLA_RANK ** -0.5)
    inp['gla_b_gate'] = nrm((DEPTH, W_GROUP), 0.1)
    inp['gla_norm'] = gain((DEPTH, W_GROUP))
    inp['w_out'] = nrm((DEPTH, D_MIX, D_MODEL), D_MIX ** -0.5)
    inp['g_ffn'] = gain((DEPTH, D_MODEL))
    inp['ffn_w_gate'] = nrm((N_DENSE, D_MODEL, D_FF), D_MODEL ** -0.5)
    inp['ffn_w_up'] = nrm((N_DENSE, D_MODEL, D_FF), D_MODEL ** -0.5)
    inp['ffn_w_down'] = nrm((N_DENSE, D_FF, D_MODEL), D_FF ** -0.5)
    inp['moe_w_router'] = nrm((N_MOE, D_MODEL, N_EXPERTS), D_MODEL ** -0.5)
    inp['moe_b_router'] = nrm((N_MOE, N_EXPERTS), 0.01)
    inp['moe_w_gate'] = nrm((N_MOE, N_EXPERTS, D_MODEL, D_FF_EXPERT), D_MODEL ** -0.5)
    inp['moe_w_up'] = nrm((N_MOE, N_EXPERTS, D_MODEL, D_FF_EXPERT), D_MODEL ** -0.5)
    inp['moe_w_down'] = nrm((N_MOE, N_EXPERTS, D_FF_EXPERT, D_MODEL), D_FF_EXPERT ** -0.5)
    inp['g_final'] = gain((D_MODEL,))
    return inp

def reference(x_prompt, x_sample, state_mlstm_C, state_mlstm_n, state_mlstm_m, state_gdn_S, state_gdn_conv,
              state_sc_conv, state_gla_S, w_in, g_mix, mlstm_b_i, mlstm_b_f, mlstm_norm, gdn_conv_w, gdn_a_log,
              gdn_dt_bias, gdn_norm, sc_conv_w, gla_w_gate, gla_b_gate, gla_norm, w_out, g_ffn, ffn_w_gate,
              ffn_w_up, ffn_w_down, moe_w_router, moe_b_router, moe_w_gate, moe_w_up, moe_w_down, g_final):
    params = (w_in, g_mix, mlstm_b_i, mlstm_b_f, mlstm_norm, gdn_conv_w, gdn_a_log, gdn_dt_bias, gdn_norm,
              sc_conv_w, gla_w_gate, gla_b_gate, gla_norm, w_out, g_ffn, ffn_w_gate, ffn_w_up, ffn_w_down,
              moe_w_router, moe_b_router, moe_w_gate, moe_w_up, moe_w_down, g_final)
    y_prompt, sp = _trunk(x_prompt, _zero_states(x_prompt.shape[0], x_prompt.dtype), params)
    ss_in = [state_mlstm_C, state_mlstm_n, state_mlstm_m, state_gdn_S, state_gdn_conv, state_sc_conv, state_gla_S]
    y_sample, ss = _trunk(x_sample, ss_in, params)
    p_mC, p_mn, p_mm, p_gS, p_gconv, p_sconv, p_lS = sp
    s_mC, s_mn, s_mm, s_gS, s_gconv, s_sconv, s_lS = ss
    return (y_prompt, y_sample, p_mC, s_mC, p_mn, s_mn, p_mm, s_mm, p_gS, s_gS,
            p_gconv, s_gconv, p_sconv, s_sconv, p_lS, s_lS)


_drawn_inputs = setup_inputs


def setup_inputs(seed=0):
    import zlib

    import numpy as np

    out = dict(_drawn_inputs(seed))
    spreads = {}
    factors = {'mlstm_norm': 9.968,
     'gdn_norm': 13.933,
     'gla_norm': 9.582,
     'moe_b_router': 11.286,
     'g_final': 20.323,
     'g_ffn': 2.755}
    for name, (base, spread) in spreads.items():
        noise = np.random.default_rng([zlib.crc32(name.encode()), seed]).standard_normal(out[name].shape)
        drawn = base * np.exp(spread * noise) if base else spread * noise
        out[name] = __import__('jax').numpy.asarray(drawn.astype(out[name].dtype))
    for name, factor in factors.items():
        out[name] = (out[name] * factor).astype(out[name].dtype)
    return out
```

```python
from contextlib import ExitStack

import numpy as np

import concourse.bass as bass
from concourse import mybir

F32 = mybir.dt.float32
F32R = mybir.dt.float32r
ALU = mybir.AluOpType
ACT = mybir.ActivationFunctionType
AX = mybir.AxisListType

P = 128
D = 1024
KT = D // P
T, NB = 512, 8
TOK = T + NB
HALF = TOK // 2
LAYERS = 2
HEADS, DH = 4, 64
C = 128
NC_ = T // C
SUB = 32
NSUB = C // SUB
EPS = 1e-6
GEXP, GF = 10, 11
EXPERTS = 8
ZU, OU = 31, 8
EU = 2 * GF + KT
RAW, SPLIT = 3, 2
UNITS = [ZU + OU + 2 * EU, ZU + OU + EXPERTS * EU]
KCH, KSC = 4, 3
CW = T + KCH - 1 + NB * KCH + 1
CV = T + KCH - 1 + NB * KCH - KCH + 1
SW = T + KSC - 1 + NB * KSC + 1
SV = T + KSC - 1 + NB * KSC - KSC + 1

PAR = {}
_n = 0
for _name, _w in (("g_mix", 8), ("g_ffn", 8), ("g_final", 8), ("n_mlstm", 2), ("n_gdn", 2), ("n_gla", 2),
                  ("conv", 24), ("sconv", 6), ("gla_b", 2), ("gate_b", 1), ("a_log", 1), ("m0", 8),
                  ("wgate", 256), ("router", 64), ("router_b", 8)):
    PAR[_name] = (_n, _n + _w)
    _n += _w
PARW = _n

CON = {}
_n = 0
for _name, _w in (("ident", 128), ("neg", 128), ("tri", 128), ("lvl", 896), ("bones", 128), ("ones", 128),
                  ("onesh", 256), ("irep", 64), ("sel", 512), ("ehp", 256), ("reset", 512),
                  ("rev", 8), ("eps", 1), ("ln8", 1), ("one", 1)):
    CON[_name] = (_n, _n + _w)
    _n += _w
CONW = _n


def constants():
    c = np.zeros((P, CONW), np.float32)

    def put(name, a):
        c[:, CON[name][0]:CON[name][1]] = a.reshape(P, -1)

    s, t = np.arange(P)[:, None], np.arange(P)[None, :]
    put("ident", (s == t).astype(np.float32))
    put("neg", np.where(s <= t, 0.0, -1e30).astype(np.float32))
    put("tri", (s <= t).astype(np.float32))
    lv = [((s // (2 * b) == t // (2 * b)) & (s % (2 * b) < b) & (t % (2 * b) >= b)) for b in (1, 2, 4, 8, 16, 32, 64)]
    put("lvl", np.stack(lv, 1).astype(np.float32))
    put("bones", (s // DH == t // DH).astype(np.float32))
    put("ones", np.ones((P, P), np.float32))
    put("onesh", np.stack([np.broadcast_to(t // DH == h, (P, P)) for h in range(2)], 1).astype(np.float32))
    put("irep", (s % DH == np.arange(DH)[None, :]).astype(np.float32))
    h = np.arange(HEADS)[None, :, None]
    put("sel", np.broadcast_to(s[:, :, None] % 32 == h, (P, HEADS, P)).astype(np.float32))
    hp = np.arange(2)[None, :, None]
    put("ehp", (s[:, :, None] % 32 == 2 * hp + t[:, None, :] // DH).astype(np.float32))
    put("reset", np.broadcast_to((np.arange(T) % C != 0)[None, :], (P, T)).astype(np.float32))
    put("rev", np.broadcast_to(np.arange(8, 0, -1, dtype=np.float32)[None, :], (P, 8)))
    put("eps", np.full((P, 1), EPS, np.float32))
    put("ln8", np.full((P, 1), -0.5 * np.log(DH), np.float32))
    put("one", np.ones((P, 1), np.float32))
    return c


N = dict(
    at_v=4, beta_p=1, conv_v=24, ct_g=12, da_a=1, dec_v=3, dx_p=7, dx_v=7, eb_v=4, ebx_a=4, em_v=4, emx_a=4,
    gate_a=2, glog_p=4, gsd_p=4, gst_p=3, gtok_p=4, gtok_v=12, hn_p=3, hn_v=9, hrs_a=3, hsq_a=3, ki0_g=1,
    ki_v=5, kind_g=1, l2_p=2, l2_v=2, lcum_v=1, leg_a=1, lg_p=1, lk_a=1, lkd_a=4, lke_v=1, llog_p=4, ln2_a=2,
    lpm_v=4, lqe_v=1, lsp_a=1, lsub_a=5, lsub_v=5, ltok_p=4, mbc_a=3, mbc_p=3, mkd_v=4, mlog_p=4, mo_v=1,
    mpm_v=4, mtok_p=4, nd_a=1, nq_p=1, nq_v=1, nsn_v=1, nso_a=3, o_a=4, out_p=6, pm_v=4, qe_a=1, qe_p=1,
    qe_v=1, qw_v=1, rex_a=6, rows_v=1, rpre_v=1, rs2_a=2, rsp_a=2, sc_v=2, scu_v=1, silu_a=3, so_a=6, so_g=3,
    spad_g=2, sq2_a=2, st_v=48, stail_a=2, tail_a=2, tq_a=2, tq_p=2, up_p=8, uw_p=2, uw_v=6, vn_v=4, vp_a=24,
    wo_add=8, xm_a=2, xt0_v=2, xtr_p=2, xtu_v=12, xu_v=10, y_p=12, ys_a=12, z_evac=31, z_p=10, zero_g=4,
    zt_p=12,
)


def build(nc, A, O):
    with ExitStack() as ctx:
        def sb(name, shape, dt=F32, stack=ctx):
            return stack.enter_context(nc.sbuf_tensor("sb_" + name, shape, dt))

        X = sb("x", [P, KT, TOK])
        Hhi, Hlo = sb("h_hi", [P, KT, TOK], F32R), sb("h_lo", [P, KT, TOK], F32R)
        Wraw = sb("w_raw", [P, RAW, GF * P])
        Whi, Wlo = sb("w_hi", [P, SPLIT, GF * P], F32R), sb("w_lo", [P, SPLIT, GF * P], F32R)
        con = sb("con", [P, CONW])
        par = sb("par", [P, PARW])
        mixers = ExitStack()
        Y = sb("y", [P, KT, TOK], stack=mixers)
        GA = sb("ga", [P, 6 * CW + 2 * TOK], stack=mixers)
        GB = sb("gb", [P, 8, TOK], stack=mixers)
        S = sb("s", [P, 14522], stack=mixers)
        mixers.close()
        ffn = ExitStack()
        Ahi, Alo = sb("a_hi", [P, GF, TOK], F32R, ffn), sb("a_lo", [P, GF, TOK], F32R, ffn)
        GT = sb("gate_bc", [P, EXPERTS, TOK], stack=ffn)
        SG = sb("silu_g", [P, 2, TOK], stack=ffn)
        AF = sb("act_f", [P, 2, TOK], stack=ffn)
        RTK = sb("router_tok", [P, 8, 5, 8], stack=ffn)
        RG = sb("router_g", [8, TOK], stack=ffn)
        RWhi, RWlo = sb("rw_hi", [P, 64], F32R, ffn), sb("rw_lo", [P, 64], F32R, ffn)
        RC = sb("router_c", [P, 4, 5], stack=ffn)
        SEL8 = sb("sel8", [8, EXPERTS * P], stack=ffn)
        ffn.close()
        PS = ctx.enter_context(nc.psum_tensor("ps", [P, 8, 512], F32))

        sem = {}

        def new(*names):
            for name in names:
                sem[name] = ctx.enter_context(nc.semaphore(name))

        new("a_ord", "af_v", "ahi_a", "at_v", "beta_p", "conv_v", "ct_g", "da_a", "dec_v", "down_v", "dx_p",
            "dx_v", "eb_v", "ebx_a", "em_v", "emx_a", "gate_a", "glog_p", "glu_v", "gsd_p", "gst_p", "gt_a", "gt_p",
            "gtok_p", "gtok_v", "h_f", "h_hi", "h_lo", "hist_d", "hn_p", "hn_v", "hrs_a", "hsq_a", "ki0_g", "ki_v",
            "kind_g", "l2_p", "l2_v", "lcum_v", "leg_a", "lg_p", "lk_a", "lkd_a", "lke_v", "llog_p", "ln2_a",
            "load_con", "load_par", "load_x", "lpm_v", "lqe_v", "lsp_a", "lsub_a", "lsub_v", "ltok_p", "m_v",
            "mbc_a", "mbc_p", "mkd_v", "mlog_p", "mo_v", "mpm_v", "mtok_p", "nd_a", "nq_p", "nq_v", "nsn_v", "nso_a",
            "o_a", "out_p", "pm_v", "qe_a", "qe_p", "qe_v", "qw_v", "rex_a", "rexp_a", "rg_v", "rgt_a", "rl_v",
            "rows_v", "rpre_v", "rs2_a", "rs_a", "rsp_a", "rt_p", "rwhi_a", "rwlo_v", "sc_v", "scu_v", "sel8_d",
            "shist_d", "silu_a", "silu_g", "so_a", "so_g", "spad_g", "sq2_a", "sq_a", "ssq_p", "st_v", "stail_a",
            "state_d", "stored", "stored_g", "tail_a", "tq_a", "tq_p", "unit_done", "up_p", "uw_p", "uw_v", "v_ord",
            "vn_v", "vp_a", "w_hi", "w_lo", "wo_add", "xm_a", "xt0_v", "xtr_p", "xtu_v", "xu_v", "y_p", "y_stored",
            "ys_a", "z_evac", "z_p", "zero_g", "zt_p")
        new(*[f"w_raw{i}" for i in range(RAW)])
        count = dict.fromkeys(sem, 0)

        def inc(ins, name):
            ins.then_inc(sem[name], 1)
            count[name] += 1
            return ins

        def own(eng, name):
            if count[name]:
                eng.wait_ge(sem[name], count[name])

        def looped(before, times):
            for name in count:
                count[name] += (times - 1) * (count[name] - before[name])

        def W(eng, name, l, k=None):
            value = l * N[name] + (N[name] if k is None else k)
            if value:
                eng.wait_ge(sem[name], value)

        def cn(name, rows=None):
            a, b = CON[name]
            return con[:, a:b] if rows is None else con[rows, a:b]

        ident, ones, bones, tri, neg = cn("ident"), cn("ones"), cn("bones"), cn("tri"), cn("neg")
        lvl = cn("lvl").rearrange("p (l t) -> p l t", l=7)
        onesh = cn("onesh").rearrange("p (h m) -> p h m", h=2)
        irep = cn("irep")
        reset = cn("reset")
        EPSC, LN8 = cn("eps"), cn("ln8")
        sel = cn("sel").rearrange("p (h m) -> p h m", h=HEADS)
        ehp = cn("ehp").rearrange("p (h m) -> p h m", h=2)

        def pr(name, rows=slice(0, P)):
            a, b = PAR[name]
            return par[rows, a:b]

        def cut(o, *shape):
            n = int(np.prod(shape))
            v = S[:, o:o + n]
            names = "abcde"[:len(shape)]
            if len(shape) == 1:
                return v
            return v.rearrange(f"p ({' '.join(names)}) -> p {' '.join(names)}",
                               **{x: w for x, w in zip(names[1:], shape[1:])})

        VP = cut(0, NC_, HEADS, P)
        ST = cut(2048, NC_ + 1, 2, 2, P)
        KD = cut(4608, NC_, 256)
        PM = cut(5632, HEADS, NC_, P)
        R0 = 7680
        QA, QB, RA = cut(R0 + 4160, TOK), cut(R0 + 4680, TOK), cut(R0 + 5200, TOK)
        RM = cut(R0 + 5720, TOK)
        TQ = cut(R0 + 6240, NC_, 8, 4)
        SM = cut(R0 + 6368, 7, 16)
        TAIL = cut(R0 + 6480, 6, 27)
        STAIL = cut(R0 + 6642, 2, 18)
        SO = cut(R0 + 6678, 2, DH)
        NS = cut(R0 + 6806, 2, NB)
        NSO = cut(R0 + 6822, 2, NB + 1)
        EA, SMZ = cut(R0 + 6840, 1)[0:4], cut(R0 + 6841, 1)
        TN, TH, RS = cut(R0, 2, TOK), cut(R0 + 1040, 2, TOK), cut(R0 + 2080, TOK)
        YO = Y
        ri, rf, ra, rb, fa, aa, _, gg = (GB[0:4, i, :] for i in range(8))
        t1, t2, t3, t4, t5 = (cut(R0 + TOK * i, TOK)[0:4] for i in range(5))
        CB = GA[:, 0:6 * CW].rearrange("p (j w) -> p j w", j=6)
        GZ = GA[:, 6 * CW:].rearrange("p (j w) -> p j w", j=2)
        CY = cut(R0, 6, CV)
        LS = cut(R0, 4, TOK)
        AT, XM, XT, YS = (cut(R0 + 1024 * i, 2, NC_, P) for i in range(4))
        EB = cut(R0 + 3072, 2, NC_, P)
        yflat = Y[:].rearrange("p k t -> p (k t)")

        def ycut(o, *shape):
            n = int(np.prod(shape))
            names = "abcde"[:len(shape)]
            return yflat[:, o:o + n].rearrange(f"p ({' '.join(names)}) -> p {' '.join(names)}",
                                               **{x: w for x, w in zip(names[1:], shape[1:])})
        CT = ycut(0, 2, NC_, P)
        BK, BV = ycut(1040, NC_, 256), ycut(2064, NC_, 256)
        U = ycut(3120, NC_, 256)
        VN = cut(R0, NC_, 256)
        QE = cut(R0 + 1024, 2, NC_, P)
        OG = cut(R0 + 2048, 2, TOK)
        SQG = EGB = cut(R0 + 3088, 2, TOK)
        WI, EMN, OM = cut(R0, 2, TOK), cut(R0 + 1040, 2, TOK), cut(R0 + 2080, 2, TOK)
        DA = Y[:, 4:6, :]
        EM = ycut(3120, 2, NC_, P)
        GG, EG, QI = Y[:, 4:6, :], Y[:, 6:8, :], GB[:, 6:8, :]
        KI = [cut(R0 + 1024 * i, 2, NC_, P) for i in range(NSUB)]
        OL, SQL = cut(R0, 2, TOK), cut(R0 + 1040, 2, TOK)
        LA = GA[:, 0:8 * TOK].rearrange("p (j w) -> p j w", j=8)
        SD, DX = cut(5632, 2, NB, DH), cut(6656, 2, NB, DH)
        SCB = cut(R0, 2, SW)
        SCY = cut(R0 + 2 * SW, 2, SV)

        def halves(ap):
            return ap.rearrange("p (a b) -> p a b", a=2)

        def slot(i):
            return PS[:, 2 * i:2 * i + 2, 0:HALF]

        M = [PS[:, 4 + i, :] for i in range(4)]
        DOWN_SLOT = [0, 3, 1, 2, 1, 2, 0, 3]

        def kind_of(u):
            if u < ZU + OU:
                return KT
            return KT if (u - ZU - OU) % EU < 2 * GF else GF

        UB = [0, UNITS[0]]
        LAST = sum(UNITS)

        ORDER = (["rnm"] + [("z", u) for u in range(7)] +
                 ["rows", ("z", 7), "tq", ("z", 8), "conv", ("z", 9), "l2", ("z", 10), "gtok", ("z", 11),
                  ("glog", 0), ("z", 12), ("inv", 0), ("uw", 0), ("z", 13), ("glog", 1), ("z", 14),
                  ("inv", 1), ("uw", 1), "qe", ("z", 15), "gst", "gout", ("z", 16), "gd", ("hn", 0),
                  "mbc", ("z", 17), "mtok", ("z", 18), "mst", ("z", 19), "mlog", ("z", 20), "mout",
                  ("z", 21), "md", ("z", 22), ("hn", 1), ("z", 23), ("z", 24),
                  "lg", ("z", 25), "lk", "ltok", ("z", 26), "lst", "lsub", ("z", 27), "llog", ("z", 28), "lout",
                  ("z", 29), "ld", ("z", 30), ("hn", 2), "sc", "ysp"] + [("o", m) for m in range(OU)] + ["rnf"])

        NG = [2, EXPERTS]
        GROUPS_BEFORE = [0, 2]

        block = ctx.enter_context(nc.Block())

        @block.sync
        def _(sp):
            for k in range(KT):
                sp.dma_start(X[:, k, :], A["xT"][k]).then_inc(sem["load_x"], 16)

            def load(u, k, src):
                if not isinstance(u, int) or u >= RAW:
                    sp.wait_ge(sem["w_lo"], u - RAW + 1)
                return sp.dma_start(Wraw[:, k[1], 0:k[0] * P], src).then_inc(sem[f"w_raw{k[1]}"], 16)

            for l in range(LAYERS):
                for i in range(ZU):
                    load(UB[l] + i, (KT, (UB[l] + i) % RAW), A["wz"][l, i])
                for i in range(OU):
                    u = UB[l] + ZU + i
                    load(u, (KT, u % RAW), A["wo"][l, i])
                base = UB[l] + ZU + OU
                with sp.Fori(0, NG[l]) as e:
                    g = e + GROUPS_BEFORE[l]
                    for i in range(2 * GF):
                        load(e * EU + (base + i), (KT, (base + i) % RAW),
                             A["wgu"][bass.ds(g, 1), i, :, :].rearrange("g p n -> (g p) n"))
                    for i in range(KT):
                        load(e * EU + (base + 2 * GF + i), (GF, (base + 2 * GF + i) % RAW),
                             A["wd"][bass.ds(g, 1), i, :, :].rearrange("g p n -> (g p) n"))
            for k in range(KT):
                sp.wait_ge(sem["h_f"], 8 * 4 + k + 1)
                sp.dma_start(O["y"][k], YO[:, k, :]).then_inc(sem["y_stored"], 16)
            sp.wait_ge(sem["y_stored"], 16 * KT)

        @block.gpsimd
        def _(pool):
            pool.dma_start(con[:, :], A["con"]).then_inc(sem["load_con"], 16)
            stored = [0]

            def store(dst, src):
                pool.dma_start(dst, src).then_inc(sem["stored"], 16)
                stored[0] += 16

            def coupling(l, hp):
                W(pool, "at_v", l, 2 * hp + 2)
                for v in range(1, 7):
                    if v == 1:
                        W(pool, "xt0_v", l, hp + 1)
                    else:
                        W(pool, "y_p", l, 6 * hp + v - 1)
                    inc(pool.tensor_tensor(CT.rearrange("p h c t -> p (h c) t"), AT.rearrange("p h c t -> p (h c) t"),
                                           lvl[:, v:v + 1, :].broadcast_to([P, 8, P]), ALU.mult), "ct_g")

            def state_in(l, i, name):
                W(pool, "out_p", l, 2 * (i + 1))
                if i:
                    W(pool, "hn_v", l, 3 * i)
                pool.dma_start(SD, A[name][l]).then_inc(sem["state_d"], 16)

            def state_out(l, i, name):
                W(pool, "so_a", l, 2 * (i + 1))
                store(O[name + "_p"][l], SO)
                W(pool, "dec_v", l, i + 1)
                store(O[name + "_s"][l], SD)
                pool.wait_ge(sem["stored"], stored[0])
                inc(pool.memset(SMZ, 0.0), "so_g")

            for l in range(LAYERS):
                if l:
                    pool.wait_ge(sem["down_v"], KT * NG[0])
                pool.dma_start(par[:, :], A["par"][l]).then_inc(sem["load_par"], 16)
                inc(pool.memset(S[:, 0:4608], 0.0), "zero_g")
                inc(pool.memset(S[:, R0 + 4160:R0 + 5720], 0.0), "zero_g")
                inc(pool.memset(CB[:, :, 0:KCH - 1], 0.0), "zero_g")
                inc(pool.memset(CB[:, :, CW - 1:CW], 0.0), "zero_g")
                for j in range(6):
                    pool.dma_start(CB[:, j, T + KCH - 1:CW - 1].rearrange("p (b w) -> p b w", w=KCH)[:, :, 0:KCH - 1],
                                   A["gconv"][l, j]).then_inc(sem["hist_d"], 16)
                W(pool, "rows_v", l)
                store(O["mm"][l], RM[0:4, :])
                W(pool, "tail_a", l, 2)
                store(O["gtail"][l], TAIL)
                pool.wait_ge(sem["load_con"], 16)
                coupling(l, 0)
                coupling(l, 1)
                state_in(l, 0, "gS")
                state_out(l, 0, "gS")
                W(pool, "gst_p", l)
                inc(pool.memset(ST[:, :, :, 1, :], 0.0), "kind_g")
                state_in(l, 1, "mC")
                W(pool, "out_p", l, 4)
                pool.dma_start(NS, A["mn"][l]).then_inc(sem["state_d"], 16)
                state_out(l, 1, "mC")
                W(pool, "nso_a", l)
                store(O["mn"][l], NSO)
                W(pool, "ltok_p", l)
                for i in range(NSUB - 1):
                    last = pool.memset(KI[i][:, :, :, (i + 1) * SUB:], 0.0)
                inc(last, "ki0_g")
                state_in(l, 2, "lS")
                state_out(l, 2, "lS")
                W(pool, "hn_v", l, 9)
                inc(pool.memset(SCB[:, :, 0:KSC - 1], 0.0), "spad_g")
                inc(pool.memset(SCB[:, :, SW - 1:SW], 0.0), "spad_g")
                for j in range(2):
                    pool.dma_start(SCB[:, j, T + KSC - 1:SW - 1].rearrange("p (b w) -> p b w", w=KSC)[:, :, 0:KSC - 1],
                                   A["sconv"][l, j]).then_inc(sem["shist_d"], 16)
                W(pool, "stail_a", l)
                store(O["stail"][l], STAIL)
                pool.wait_ge(sem["stored"], stored[0])
                inc(pool.memset(SMZ, 0.0), "stored_g")
                if l == 1:
                    pool.wait_ge(sem["h_lo"], 24 + 16)
                    pool.dma_start(SEL8[:, :], A["sel8"]).then_inc(sem["sel8_d"], 16)
            pool.wait_ge(sem["stored"], stored[0])
        @block.tensor
        def _(pe):
            def mm(out, lhsT, rhs, start=True, stop=True):
                return pe.matmul(out, lhsT, rhs, start=start, stop=stop, skip_group_check=True)

            def unit(s, banks, k, hi, lo, last_tile=None):
                for j in range(k):
                    if last_tile is not None and j == k - 1:
                        pe.wait_ge(sem["glu_v"], last_tile)
                    for h in range(2):
                        out, t = banks[:, h, :], slice(h * HALF, (h + 1) * HALF)
                        w = slice(j * P, (j + 1) * P)
                        mm(out, Whi[:, s, w], hi[:, j, t], j == 0, False)
                        mm(out, Whi[:, s, w], lo[:, j, t], False, False)
                        last = mm(out, Wlo[:, s, w], hi[:, j, t], False, j == k - 1)
                return last

            def z(l, u):
                if u == 0:
                    pe.wait_ge(sem["h_lo"], l * 24 + 8)
                    if l:
                        pe.wait_ge(sem["down_v"], KT * NG[0])
                if u >= 2:
                    W(pe, "z_evac", l, u - 1)
                g = UB[l] + u
                pe.wait_ge(sem["w_lo"], g + 1)
                inc(unit(g % SPLIT, slot(u % 2), KT, Hhi, Hlo), "unit_done")

            def o(l, m):
                if m == 0:
                    pe.wait_ge(sem["h_lo"], l * 24 + 16)
                    W(pe, "z_evac", l)
                if m >= 2:
                    W(pe, "wo_add", l, m - 1)
                g = UB[l] + ZU + m
                pe.wait_ge(sem["w_lo"], g + 1)
                inc(unit(g % SPLIT, slot(m % 2), KT, Hhi, Hlo), "unit_done")

            def rn(l, n):
                for k in range(KT):
                    pe.wait_ge(sem["sq_a"], n * KT + k + 1)
                    for h in range(2):
                        last = mm(M[h][:, 0:HALF], ones, TN[:, k % 2, h * HALF:(h + 1) * HALF], k == 0, k == KT - 1)
                    inc(last, "ssq_p")

            def tq(l):
                W(pe, "rows_v", l)
                W(pe, "rex_a", l)
                for i, q in enumerate((QA, QB)):
                    for c in range(NC_):
                        last = pe.transpose(M[i][:, c * P:(c + 1) * P], q[:, c * C:(c + 1) * C], ident)
                    inc(last, "tq_p")

            def pair_bc(lo, hi_, rows, at, name):
                for hp in range(2):
                    for h in range(2):
                        last = mm(M[2 * hp + h][:, 0:HALF], ehp[lo:hi_, hp, :], rows[lo:hi_, h * HALF:(h + 1) * HALF])
                inc(last, name)

            def head_sums(src, name):
                for j in range(2):
                    for h in range(2):
                        last = mm(M[2 * j + h][:, 0:HALF], bones, src[:, j, h * HALF:(h + 1) * HALF])
                inc(last, name)

            def l2(l):
                for i in range(2):
                    W(pe, "sq2_a", l, i + 1)
                    if i:
                        W(pe, "ln2_a", l, i)
                    else:
                        W(pe, "tq_a", l)
                    head_sums(LS[:, 2 * i:2 * i + 2, :], "l2_p")

            def tok(l, keys, values, name, free):
                for c in range(NC_):
                    for i, src in enumerate((keys[0], keys[1], values[0], values[1])):
                        last = pe.transpose(M[c][:, i * P:(i + 1) * P], src[:, c * C:(c + 1) * C], ident)
                    inc(last, name)

            def gtok(l):
                W(pe, "l2_v", l)
                W(pe, "silu_a", l)
                tok(l, (CB[:, 2, :], CB[:, 3, :]), (CB[:, 4, :], CB[:, 5, :]), "gtok_p", None)

            def glog(l, hp):
                for h in range(2):
                    head = 2 * hp + h
                    if head == 0:
                        W(pe, "gtok_v", l)
                    elif head == 2:
                        W(pe, "uw_v", l, 3)
                    else:
                        W(pe, "at_v", l, head)
                    rows = slice(DH * h, DH * h + DH)
                    mm(M[0], sel[64:68, head, :], QB[64:68, 0:T])
                    mm(M[3], sel[0:4, head, :], QB[0:4, 0:T])
                    for c in range(NC_):
                        t = slice(c * C, (c + 1) * C)
                        mm(M[1][:, t], CB[rows, 2 + hp, t], CB[rows, 2 + hp, t])
                        last = mm(M[2][:, t], CB[rows, 2 + hp, t], CB[rows, hp, t])
                    inc(last, "glog_p")

            def inv(l, hp):
                W(pe, "xt0_v", l, hp + 1)
                W(pe, "at_v", l, 2 * hp + 2)
                for h in range(2):
                    for c in range(NC_):
                        last = pe.transpose(M[h][:, c * P:(c + 1) * P], XT[:, h, c, :], ident)
                inc(last, "xtr_p")
                W(pe, "xm_a", l, hp + 1)
                for v in range(1, 7):
                    W(pe, "ct_g", l, 6 * hp + v)
                    if v > 1:
                        W(pe, "xu_v", l, 5 * hp + v - 1)
                        W(pe, "xtu_v", l, 6 * hp + v - 1)
                    for h in range(2):
                        for c in range(NC_):
                            last = mm(M[h][:, c * P:(c + 1) * P], CT[:, h, c, :], XM[:, h, c, :])
                    inc(last, "y_p")
                    W(pe, "ys_a", l, 6 * hp + v)
                    if v < 6:
                        for h in range(2):
                            for c in range(NC_):
                                last = mm(M[2 + h][:, c * P:(c + 1) * P], XT[:, h, c, :], YS[:, h, c, :])
                        inc(last, "z_p")
                    for h in range(2):
                        for c in range(NC_):
                            last = mm(M[h][:, c * P:(c + 1) * P], YS[:, h, c, :], XT[:, h, c, :])
                    inc(last, "zt_p")

            def uw(l, hp):
                W(pe, "xtu_v", l, 6 * hp + 6)
                for h in range(2):
                    for c in range(NC_):
                        a = hp * P + h * DH
                        mm(M[0][:, (h * NC_ + c) * DH:(h * NC_ + c + 1) * DH], XT[:, h, c, :], BV[:, c, a:a + DH])
                        last = mm(M[1 + h][:, c * P:(c + 1) * P], BK[:, c, hp * P:(hp + 1) * P], XT[:, h, c, :])
                inc(last, "uw_p")

            def qe(l):
                W(pe, "uw_v", l)
                pair_bc(96, 100, QB, None, "qe_p")

            def gst(l):
                W(pe, "qe_v", l)
                for c in range(NC_):
                    if c:
                        W(pe, "st_v", l, 4 * c)
                        for hp in range(2):
                            last = mm(M[0][:, hp * P:(hp + 1) * P], ST[:, c, hp, 1, :], ST[:, c, hp, 0, :])
                        inc(last, "gst_p")
                    W(pe, "vn_v", l, c + 1)
                    for hp in range(2):
                        last = mm(M[1][:, hp * P:(hp + 1) * P], KD[:, c, hp * P:(hp + 1) * P],
                                  VN[:, c, hp * P:(hp + 1) * P])
                    inc(last, "gsd_p")

            def outs(l, i, q):
                W(pe, "st_v", l, 16 * (i + 1))
                W(pe, "vp_a", l, 8 * (i + 1))
                for hp in range(2):
                    for c in range(NC_):
                        t = slice(c * P, (c + 1) * P)
                        mm(M[hp][:, t], ST[:, c, hp, 0, :], q[:, hp, t], True, False)
                        for h in range(2):
                            last = mm(M[hp][:, t], VP[:, c, 2 * hp + h, :], PM[:, 2 * hp + h, c, :], False, h == 1)
                    if i == 1:
                        for c in range(NC_):
                            t = slice(c * P, (c + 1) * P)
                            mm(M[2 + hp][:, t], ST[:, c, hp, 1, :], q[:, hp, t], True, False)
                            for h in range(2):
                                last = mm(M[2 + hp][:, t], onesh[:, h, :], PM[:, 2 * hp + h, c, :], False, h == 1)
                    inc(last, "out_p")

            def dx(l, n):
                W(pe, "dx_v", l, n)
                for hp in range(2):
                    last = mm(M[hp], bones, DX[:, hp, :, :].rearrange("p b e -> p (b e)"))
                inc(last, "dx_p")

            def gd(l):
                W(pe, "o_a", l, 2)
                for hp in range(2):
                    last = mm(M[2][:, hp * NB:(hp + 1) * NB], ehp[0:4, hp, :], QB[0:4, T:TOK])
                inc(last, "beta_p")
                for n in range(3):
                    dx(l, n + 1)

            def hn(l, i):
                W(pe, "hsq_a", l, i + 1)
                W(pe, "dec_v", l, i + 1)
                head_sums((SQG, DA, SQL)[i], "hn_p")

            def mbc(l):
                W(pe, "hrs_a", l, 1)
                pair_bc(32, 36, RA, None, "mbc_p")
                W(pe, "mbc_a", l, 1)
                pair_bc(64, 68, RA, None, "mbc_p")
                W(pe, "mbc_a", l, 2)
                for hp in range(2):
                    last = mm(M[0][:, hp * NB:(hp + 1) * NB], ehp[32:36, hp, :], QA[32:36, T:TOK])
                inc(last, "mbc_p")

            def mtok(l):
                W(pe, "mbc_a", l)
                W(pe, "z_evac", l, 15)
                tok(l, (GB[:, 2, :], GB[:, 3, :]), (GB[:, 4, :], GB[:, 5, :]), "mtok_p", None)

            def updates(l, i):
                for c in range(NC_):
                    W(pe, ("", "mkd_v", "lkd_a")[i], l, c + 1)
                    W(pe, "vp_a", l, 8 * i + 2 * c + 2)
                    for hp in range(2):
                        k = KD[:, c, hp * P:(hp + 1) * P]
                        a = hp * 256 if i == 1 else hp * P
                        mm(M[c][:, a:a + P], k, VP[:, c, 2 * hp, :], True, False)
                        last = mm(M[c][:, a:a + P], k, VP[:, c, 2 * hp + 1, :], False, True)
                        if i == 1:
                            last = mm(M[c][:, a + P:a + 2 * P], k, ones)
                    inc(last, "up_p")

            def mlog(l):
                W(pe, "st_v", l, 32)
                for head in range(HEADS):
                    hp, h = head // 2, head % 2
                    rows = slice(DH * h, DH * h + DH)
                    if head >= 2:
                        W(pe, "mpm_v", l, head - 1)
                    a = 2 * (head % 2)
                    mm(M[a], sel[0:4, head, :], RA[0:4, 0:T])
                    for c in range(NC_):
                        t = slice(c * C, (c + 1) * C)
                        last = mm(M[a + 1][:, t], GB[rows, 2 + hp, t], GB[rows, hp, t])
                    inc(last, "mlog_p")

            def mout(l):
                W(pe, "mpm_v", l)
                W(pe, "qw_v", l)
                outs(l, 1, GB)

            def md(l):
                W(pe, "mo_v", l)
                dx(l, 4)
                W(pe, "nq_v", l)
                inc(mm(M[2][:, 0:2 * NB], bones, SM[:, 3, :]), "nq_p")
                dx(l, 5)

            def lg(l):
                W(pe, "hrs_a", l, 2)
                for hp in range(2):
                    for h in range(2):
                        a = PAR["wgate"][0] + hp * P
                        last = mm(M[2 * hp + h][:, 0:HALF], par[96:128, a:a + P], RA[96:128, h * HALF:(h + 1) * HALF])
                inc(last, "lg_p")

            def ltok(l):
                W(pe, "lke_v", l)
                W(pe, "z_evac", l, 23)
                tok(l, (KI[0][:, 0, :, :].rearrange("p c t -> p (c t)"), KI[0][:, 1, :, :].rearrange("p c t -> p (c t)")),
                    (LA[:, 4, :], LA[:, 5, :]), "ltok_p", None)

            def llog(l):
                W(pe, "ki_v", l)
                W(pe, "ki0_g", l)
                W(pe, "st_v", l, 48)
                for head in range(HEADS):
                    hp, h = head // 2, head % 2
                    rows = slice(DH * h, DH * h + DH)
                    for c in range(NC_):
                        for i in range(NSUB):
                            t = slice(c * C + i * SUB, c * C + (i + 1) * SUB)
                            last = mm(M[head][:, t], KI[i][rows, hp, c, :], QI[rows, hp, t])
                    inc(last, "llog_p")

            def lout(l):
                W(pe, "lpm_v", l)
                W(pe, "lqe_v", l)
                outs(l, 2, LA)

            def ld(l):
                W(pe, "o_a", l, 4)
                dx(l, 6)
                dx(l, 7)

            def router(l):
                pe.wait_ge(sem["h_lo"], l * 24 + 24)
                pe.wait_ge(sem["rwlo_v"], 1)
                for i in range(5):
                    n = P if i < 4 else NB
                    t = slice(i * P, i * P + n)
                    for k in range(KT):
                        w = slice(k * 8, k * 8 + 8)
                        out = M[0][0:n, i * 8:i * 8 + 8]
                        mm(out, Hhi[:, k, t], RWhi[:, w], k == 0, False)
                        mm(out, Hlo[:, k, t], RWhi[:, w], False, False)
                        last = mm(out, Hhi[:, k, t], RWlo[:, w], False, k == KT - 1)
                inc(last, "rt_p")
                pe.wait_ge(sem["rg_v"], 1)
                for i in range(5):
                    n = P if i < 4 else NB
                    out = M[1][0:8, i * P:i * P + n] if i < 4 else M[2][0:8, 0:NB]
                    last = pe.transpose(out, RTK[0:n, 7, i, :], ident[0:n, 0:n])
                inc(last, "rt_p")
                pe.wait_ge(sem["rgt_a"], 2)
                pe.wait_ge(sem["sel8_d"], 16)
                for e in range(EXPERTS):
                    if e >= 2:
                        pe.wait_ge(sem["gt_a"], e - 1)
                    for h in range(2):
                        last = mm(slot(2 + e % 2)[:, h, :], SEL8[:, e * P:(e + 1) * P], RG[:, h * HALF:(h + 1) * HALF])
                    inc(last, "gt_p")

            pe.wait_ge(sem["load_con"], 16)
            STEPS = dict(tq=tq, l2=l2, gtok=gtok, glog=glog, inv=inv, uw=uw, qe=qe, gst=gst, gd=gd, hn=hn,
                         mbc=mbc, mtok=mtok, mlog=mlog, mout=mout, md=md, lg=lg, ltok=ltok, llog=llog,
                         lout=lout, ld=ld)

            for l in range(LAYERS):
                for step in ORDER:
                    name, arg = step if isinstance(step, tuple) else (step, None)
                    if name == "z":
                        z(l, arg)
                    elif name == "o":
                        o(l, arg)
                    elif name == "rnm":
                        rn(l, 2 * l)
                    elif name == "rnf":
                        rn(l, 2 * l + 1)
                    elif name == "gout":
                        W(pe, "pm_v", l)
                        outs(l, 0, QE.rearrange("p h c t -> p h (c t)"))
                    elif name == "mst":
                        updates(l, 1)
                    elif name == "lst":
                        updates(l, 2)
                    elif name in STEPS:
                        STEPS[name](l) if arg is None else STEPS[name](l, arg)
                if l == 1:
                    router(l)
                base = UB[l] + ZU + OU
                pe.wait_ge(sem["h_lo"], l * 24 + 24)
                W(pe, "wo_add", l)
                if l == 1:
                    pe.wait_ge(sem["gt_a"], EXPERTS)
                GB0, DB0 = GF * GROUPS_BEFORE[l], KT * GROUPS_BEFORE[l]

                def group(e, first):
                    for f in range(GF):
                        if f >= 2:
                            pe.wait_ge(sem["glu_v"], e * GF + (GB0 + f - 1))
                        elif not first:
                            pe.wait_ge(sem["down_v"], e * KT + (DB0 - 2 + 2 * f))
                        for j in range(2):
                            i = 2 * f + j
                            pe.wait_ge(sem["w_lo"], e * EU + (base + i + 1))
                            s = slot((1 - f % 2) if j == 0 else (2 + f % 2))
                            inc(unit((base + i) % SPLIT, s, KT, Hhi, Hlo), "unit_done")
                    for m in range(KT):
                        pe.wait_ge(sem["w_lo"], e * EU + (base + 2 * GF + m + 1))
                        if m == 0:
                            pe.wait_ge(sem["glu_v"], e * GF + (GB0 + GF - 1))
                        elif m >= 4:
                            pe.wait_ge(sem["down_v"], e * KT + (DB0 + (3, 4, 4, 4)[m - 4]))
                        inc(unit((base + 2 * GF + m) % SPLIT, slot(DOWN_SLOT[m]), GF, Ahi, Alo,
                                 e * GF + (GB0 + GF) if m == 0 else None), "unit_done")

                group(0, True)
                before = dict(count)
                with pe.Fori(1, NG[l]) as e:
                    group(e, False)
                looped(before, NG[l] - 1)
            rn(LAYERS, 4)

        @block.scalar
        def _(act):
            def split(g, k, s, raw, value):
                act.wait_ge(sem[f"w_raw{raw}"], value)
                if not isinstance(g, int) or g >= SPLIT:
                    act.wait_ge(sem["unit_done"], g - SPLIT + 1)
                inc(act.activation(Whi[:, s, 0:k * P], Wraw[:, raw, 0:k * P], ACT.Copy), "w_hi")

            def split_at(g):
                if g < UB[1] + UNITS[1]:
                    l = int(g >= UB[1])
                    split(g, kind_of(g - UB[l]), g % SPLIT, g % RAW, 16 * (g // RAW + 1))

            def ex(out, in_, func, name="a_ord", **kw):
                return inc(act.activation(out, in_, func, **kw), name)

            def z(l, u):
                split_at(UB[l] + u + 2)
                act.wait_ge(sem["unit_done"], UB[l] + u + 1)
                ps = slot(u % 2)
                if u == 0:
                    if l:
                        act.wait_ge(sem["down_v"], KT * NG[0])
                    W(act, "zero_g", l, 4)
                    act.wait_ge(sem["load_par"], 16 * (l + 1))
                    act.activation(halves(ri), ps[0:4], ACT.Identity, bias=pr("gate_b", slice(0, 4)))
                    act.activation(halves(rf), ps[32:36], ACT.Identity, bias=pr("gate_b", slice(32, 36)))
                    act.activation(halves(ra), ps[64:68], ACT.Identity, bias=pr("gate_b", slice(64, 68)))
                    act.activation(halves(rb), ps[96:100], ACT.Copy)
                    ex(halves(RA[96:128, :]), ps[0:32], ACT.Copy, "z_evac")
                elif u < 7:
                    j = u - 1
                    act.activation(CB[:, j, 3:3 + HALF], ps[:, 0, :], ACT.Copy)
                    act.activation(CB[:, j, 3 + HALF:3 + T], ps[:, 1, 0:T - HALF], ACT.Copy)
                    ex(CB[:, j, T + KCH - 1:CW - 1].rearrange("p (b w) -> p b w", w=KCH)[:, :, KCH - 1],
                       ps[:, 1, T - HALF:HALF], ACT.Copy, "z_evac")
                elif u < 9:
                    ex(halves(GZ[:, u - 7, :]), ps, ACT.Copy, "z_evac")
                elif u < 17:
                    if u == 9:
                        W(act, "rows_v", l)
                        own(act, "rex_a")
                    ex(halves(GB[:, u - 9, :]), ps, ACT.Copy, "z_evac", scale=DH ** -0.5 if u in (11, 12) else 1.0)
                elif u < 25:
                    if u == 17:
                        W(act, "hn_v", l, 3)
                    ex(halves(LA[:, u - 17, :]), ps, ACT.Copy, "z_evac", scale=DH ** -0.5 if u < 19 else 1.0)
                else:
                    if u == 25:
                        W(act, "hn_v", l, 6)
                    ex(halves(GB[:, u - 25, :]), ps, ACT.Copy, "z_evac")

            def rn(l, n):
                if n == 0:
                    act.wait_ge(sem["load_x"], 16 * KT)
                elif n % 2:
                    W(act, "wo_add", l)
                else:
                    act.wait_ge(sem["down_v"], KT * sum(NG[:n // 2]))
                for k in range(KT):
                    if k >= 2:
                        act.wait_ge(sem["ssq_p"], n * KT + k - 1)
                    ex(TN[:, k % 2, :], X[:, k, :], ACT.Square, "sq_a")
                act.wait_ge(sem["ssq_p"], n * KT + KT)
                ex(halves(RS), PS[:, 4:6, 0:HALF], ACT.Ln, scale=1.0 / D, bias=EPSC)
                own(act, "a_ord")
                ex(RS, RS, ACT.Exp, "rs_a", scale=-0.5)
                if n < 2 * LAYERS:
                    for k in range(KT):
                        act.wait_ge(sem["h_f"], n * KT + k + 1)
                        if k == 0:
                            act.wait_ge(sem["unit_done"], UB[l] + (0 if n % 2 == 0 else ZU + OU))
                        ex(Hhi[:, k, :], TH[:, k % 2, :], ACT.Copy, "h_hi")

            def rows(l):
                own(act, "z_evac")
                ex(fa, rf, ACT.Abs)
                ex(aa, ra, ACT.Abs)
                own(act, "a_ord")
                ex(fa, fa, ACT.Exp, scale=-1.0)
                ex(aa, aa, ACT.Exp, scale=-1.0)
                ex(rb, rb, ACT.Exp, scale=-1.0)
                ex(EA, pr("a_log", slice(0, 4)), ACT.Exp)
                own(act, "a_ord")
                ex(fa, fa, ACT.Ln, "rsp_a", bias=cn("one", slice(0, 4)))
                ex(aa, aa, ACT.Ln, "rsp_a", bias=cn("one", slice(0, 4)))
                W(act, "rpre_v", l)
                ex(RA[32:36, :], t1, ACT.Exp, "rex_a")
                ex(RA[64:68, :], RM[0:4, :], ACT.Exp, "rex_a", scale=-1.0)
                ex(QA[32:36, :], t3, ACT.Exp, "rex_a")
                ex(QA[96:100, 0:T], t4[:, 0:T], ACT.Exp, "rex_a")
                ex(t5, gg, ACT.Exp, "rex_a")
                ex(QB[96:100, :], gg, ACT.Exp, "rex_a")

            def tq(l):
                for i in range(2):
                    W(act, "tq_p", l, i + 1)
                    ex(TQ[:, :, 4 * i:4 * i + 4, :],
                       M[i].rearrange("p (c j h) -> p c j h", c=NC_, j=4)[:, :, :, 0:4], ACT.Copy, "tq_a")

            def tails(l):
                act.wait_ge(sem["hist_d"], 96 * (l + 1))
                own(act, "z_evac")
                ex(TAIL[:, :, 0:3], CB[:, :, T:T + 3], ACT.Copy, "tail_a")
                for j in range(6):
                    last = act.activation(TAIL[:, j, 3:27].rearrange("p (b w) -> p b w", w=3),
                                          CB[:, j, T + KCH - 1:CW - 1].rearrange("p (b w) -> p b w", w=KCH)[:, :, 1:4],
                                          ACT.Copy)
                inc(last, "tail_a")
                W(act, "conv_v", l)
                own(act, "tail_a")
                ex(CB[:, :, 0:T], CY[:, :, 0:T], ACT.Silu, "silu_a")
                ex(CB[:, :, T:TOK], CY[:, :, T + KCH - 1:CV:KCH], ACT.Silu, "silu_a")
                ex(GZ, GZ, ACT.Silu, "silu_a")

            def l2(l):
                own(act, "silu_a")
                for i in range(2):
                    ex(LS[:, 2 * i:2 * i + 2, :], CB[:, 2 * i:2 * i + 2, 0:TOK], ACT.Square, "sq2_a")
                for i in range(2):
                    W(act, "l2_p", l, i + 1)
                    ls = LS[:, 2 * i:2 * i + 2, :].rearrange("p j w -> p (j w)")
                    ex(ls.rearrange("p (a b) -> p a b", a=4), PS[:, 4:8, 0:HALF], ACT.Ln, "ln2_a", bias=EPSC)
                    own(act, "ln2_a")
                    ex(ls, ls, ACT.Exp, "rs2_a", scale=-0.5, bias=LN8 if i == 0 else 0.0)

            def glog(l, hp):
                for h in range(2):
                    head = 2 * hp + h
                    W(act, "eb_v", l, head + 1)
                    for c in range(NC_):
                        last = act.activation(EB[:, h, c, :], EB[:, h, c, :], ACT.Exp,
                                              bias=TQ[:, c, 2, head:head + 1])
                    inc(last, "ebx_a")

            def inv(l, hp):
                W(act, "xtr_p", l, hp + 1)
                ex(XM.rearrange("p h c t -> p h (c t)"), PS[:, 4:6, :], ACT.Copy, "xm_a")
                for v in range(1, 7):
                    W(act, "y_p", l, 6 * hp + v)
                    if v > 1:
                        W(act, "zt_p", l, 6 * hp + v - 1)
                    ex(YS.rearrange("p h c t -> p h (c t)"), PS[:, 4:6, :], ACT.Copy, "ys_a")

            def qe(l):
                W(act, "qe_p", l)
                ex(EGB.rearrange("p j w -> p (j w)").rearrange("p (a b) -> p a b", a=4), PS[:, 4:8, 0:HALF],
                   ACT.Copy, "qe_a")

            def pad_values(l, c, src):
                vp = VP[:, c, :, :].rearrange("p (a b) e -> p a b e", b=2)
                for h in range(2):
                    ex(vp[:, :, h, h * DH:(h + 1) * DH], src[:, :, h, :], ACT.Copy, "vp_a")

            def state_out(l, i):
                W(act, "so_g", l, i)
                for h in range(2):
                    r = slice(h * DH, (h + 1) * DH)
                    ex(SO[r, :, :], ST[r, NC_, :, 0, h * DH:(h + 1) * DH], ACT.Copy, "so_a")

            def gst(l):
                for c in range(NC_):
                    W(act, "vn_v", l, c + 1)
                    pad_values(l, c, VN[:, c, :].rearrange("p (a b e) -> p a b e", a=2, b=2))
                W(act, "st_v", l, 16)
                state_out(l, 0)

            def outs(l, i, o_):
                for hp in range(2):
                    W(act, "out_p", l, 2 * i + hp + 1)
                    ex(o_[:, hp, 0:T], M[hp], ACT.Copy, "o_a")

            def hn(l, i):
                o_, sq = ((OG, SQG), (OM, DA), (OL, SQL))[i]
                if i == 1:
                    own(act, "z_evac")
                    ex(GB[:, 6:8, :], GB[:, 6:8, :], ACT.Sigmoid, "gate_a")
                elif i == 2:
                    own(act, "z_evac")
                    ex(LA[:, 6:8, :], LA[:, 6:8, :], ACT.Silu, "gate_a")
                W(act, "dec_v", l, i + 1)
                if i != 1:
                    own(act, "o_a")
                ex(sq, o_, ACT.Square, "hsq_a")
                W(act, "hn_p", l, i + 1)
                sf = sq.rearrange("p j w -> p (j w)") if i != 1 else yflat[:, 4 * TOK:6 * TOK]
                ex(sf.rearrange("p (a b) -> p a b", a=4), PS[:, 4:8, 0:HALF], ACT.Ln, scale=1.0 / DH, bias=EPSC)
                own(act, "a_ord")
                ex(sf, sf, ACT.Exp, "hrs_a", scale=-0.5)

            def mbc(l):
                W(act, "hn_v", l, 3)
                for i, dst in enumerate((WI, EMN)):
                    W(act, "mbc_p", l, i + 1)
                    ex(dst.rearrange("p j w -> p (j w)").rearrange("p (a b) -> p a b", a=4), PS[:, 4:8, 0:HALF],
                       ACT.Copy, "mbc_a")
                W(act, "mbc_p", l, 3)
                ex(SM[:, 2, :], M[0][:, 0:2 * NB], ACT.Copy, "mbc_a")

            def mtok(l):
                for c in range(NC_):
                    W(act, "mtok_p", l, c + 1)
                    pad_values(l, c, M[c][:, 256:512].rearrange("p (a b e) -> p a b e", a=2, b=2))

            def mst(l):
                W(act, "st_v", l, 32)
                state_out(l, 1)
                if l:
                    act.wait_ge(sem["stored_g"], l)
                for h in range(2):
                    r = slice(h * DH, (h + 1) * DH)
                    ex(NSO[r, :, 0], ST[r, NC_, :, 1, h * DH], ACT.Copy, "nso_a")

            def mlog(l):
                for head in range(HEADS):
                    W(act, "em_v", l, head + 1)
                    for c in range(NC_):
                        last = act.activation(EM[:, head % 2, c, :], EM[:, head % 2, c, :], ACT.Exp,
                                              bias=TQ[:, c, 0, head:head + 1])
                    inc(last, "emx_a")

            def mout(l):
                W(act, "out_p", l, 4)
                ex(DA[:, :, 0:T], PS[:, 6:8, :], ACT.Abs, "da_a")

            def md(l):
                W(act, "nsn_v", l)
                ex(NSO[:, :, 1:9], NS, ACT.Copy, "nso_a")
                W(act, "nq_p", l)
                ex(SM[:, 5, :], M[2][:, 0:2 * NB], ACT.Abs, "nd_a")

            def lg(l):
                W(act, "lg_p", l)
                W(act, "hn_v", l, 6)
                for hp in range(2):
                    a = PAR["gla_b"][0] + hp
                    ex(halves(GG[:, hp, :]), PS[:, 4 + 2 * hp:6 + 2 * hp, 0:HALF], ACT.Identity, bias=par[:, a:a + 1])
                own(act, "a_ord")
                ex(EG, GG, ACT.Abs)
                own(act, "a_ord")
                ex(EG, EG, ACT.Exp, scale=-1.0)
                own(act, "a_ord")
                ex(EG, EG, ACT.Ln, "lsp_a", bias=cn("one"))
                W(act, "lcum_v", l)
                ex(GG, EG, ACT.Exp, "leg_a")

            def lk(l):
                for hp in range(2):
                    for c in range(NC_):
                        e = c * C + C - 1
                        last = act.activation(KI[0][:, hp, c, :], EG[:, hp, c * C:(c + 1) * C], ACT.Exp, scale=-1.0,
                                              bias=EG[:, hp, e:e + 1])
                inc(last, "lk_a")

            def ltok(l):
                for c in range(NC_):
                    W(act, "ltok_p", l, c + 1)
                    ex(KD[:, c, :], M[c][:, 0:256], ACT.Copy, "lkd_a")
                    pad_values(l, c, M[c][:, 256:512].rearrange("p (a b e) -> p a b e", a=2, b=2))

            def lst(l):
                W(act, "st_v", l, 48)
                state_out(l, 2)

            def lsub(l):
                W(act, "lsub_v", l, 1)
                ex(QI[:, :, 0:T], QI[:, :, 0:T], ACT.Exp, "lsub_a")
                for i in range(NSUB):
                    W(act, "lsub_v", l, i + 2)
                    k = KI[i][:, :, :, 0:(i + 1) * SUB]
                    ex(k, k, ACT.Exp, "lsub_a")

            def sc(l):
                W(act, "scu_v", l)
                act.wait_ge(sem["shist_d"], 32 * (l + 1))
                ex(STAIL[:, :, 0:2], SCB[:, :, T:T + 2], ACT.Copy, "stail_a")
                for j in range(2):
                    last = act.activation(STAIL[:, j, 2:18].rearrange("p (b w) -> p b w", w=2),
                                          SCB[:, j, T + KSC - 1:SW - 1].rearrange("p (b w) -> p b w", w=KSC)[:, :, 1:3],
                                          ACT.Copy)
                inc(last, "stail_a")

            def ysp(l):
                act.wait_ge(sem["unit_done"], UB[l] + ZU)
                W(act, "hn_v", l)
                W(act, "sc_v", l)
                for k in range(KT):
                    ex(Hhi[:, k, :], Y[:, k, :], ACT.Copy, "h_hi")

            def o(l, m):
                split_at(UB[l] + ZU + m + 2)

            def router(l):
                act.wait_ge(sem["down_v"], KT * NG[0])
                a, b = PAR["router"]
                ex(RWhi[:, :], par[:, a:b], ACT.Copy, "rwhi_a")
                act.wait_ge(sem["rl_v"], 1)
                ex(RTK[:, 4, :, :], RTK[:, 4, :, :], ACT.Exp, "rexp_a")
                act.wait_ge(sem["rt_p"], 2)
                ex(RG[:, 0:T], M[1][0:8, :], ACT.Copy, "rgt_a")
                ex(RG[:, T:TOK], M[2][0:8, 0:NB], ACT.Copy, "rgt_a")
                for e in range(EXPERTS):
                    act.wait_ge(sem["gt_p"], e + 1)
                    ex(halves(GT[:, e, :]), slot(2 + e % 2), ACT.Copy, "gt_a")

            split_at(0)
            split_at(1)
            act.wait_ge(sem["load_con"], 16)
            STEPS = dict(rows=rows, tq=tq, l2=l2, glog=glog, inv=inv, qe=qe, gst=gst, hn=hn, mbc=mbc, mtok=mtok,
                         mst=mst, mlog=mlog, mout=mout, md=md, lg=lg, lk=lk, ltok=ltok, lst=lst, lsub=lsub,
                         sc=sc, ysp=ysp)

            for l in range(LAYERS):
                for step in ORDER:
                    name, arg = step if isinstance(step, tuple) else (step, None)
                    if name == "z":
                        z(l, arg)
                    elif name == "o":
                        o(l, arg)
                    elif name == "rnm":
                        rn(l, 2 * l)
                    elif name == "rnf":
                        rn(l, 2 * l + 1)
                    elif name == "gout":
                        outs(l, 0, OG)
                    elif name == "lout":
                        outs(l, 2, OL)
                    elif name == "conv":
                        tails(l)
                    elif name in STEPS:
                        STEPS[name](l) if arg is None else STEPS[name](l, arg)
                if l == 1:
                    router(l)
                base = UB[l] + ZU + OU

                def group(e, last):
                    def split_next(i):
                        if last and i + 2 >= EU:
                            split_at(base + e * EU + i + 2) if isinstance(e, int) else None
                            return
                        g = base + i + 2
                        k = GF if 2 * GF <= (i + 2) % EU else KT
                        split(e * EU + g, k, g % SPLIT, g % RAW, e * (16 * EU // RAW) + 16 * (g // RAW + 1))

                    for f in range(GF):
                        act.wait_ge(sem["unit_done"], e * EU + (base + 2 * f + 1))
                        split_next(2 * f)
                        ex(halves(SG[:, f % 2, :]), slot(1 - f % 2), ACT.Silu, "silu_g")
                        split_next(2 * f + 1)
                        act.wait_ge(sem["af_v"], e * GF + (GF * GROUPS_BEFORE[l] + f + 1))
                        ex(Ahi[:, f, :], AF[:, f % 2, :], ACT.Copy, "ahi_a")
                    for m in range(KT):
                        split_next(2 * GF + m)

                if l:
                    act.wait_ge(sem["stored_g"], 2)
                else:
                    act.wait_ge(sem["stored_g"], 1)
                before = dict(count)
                with act.Fori(0, NG[l] - 1) as e:
                    group(e, False)
                looped(before, NG[l] - 1)
                group(NG[l] - 1, True)
            rn(LAYERS, 4)

        @block.vector
        def _(dve):
            def split(g, k, s, raw):
                dve.wait_ge(sem["w_hi"], g + 1)
                inc(dve.tensor_tensor(Wlo[:, s, 0:k * P], Wraw[:, raw, 0:k * P], Whi[:, s, 0:k * P].bitcast(F32),
                                      ALU.subtract), "w_lo")

            def split_at(g):
                if g < UB[1] + UNITS[1]:
                    l = int(g >= UB[1])
                    split(g, kind_of(g - UB[l]), g % SPLIT, g % RAW)

            def tt(out, a, b, op, name="v_ord"):
                return inc(dve.tensor_tensor(out, a, b, op), name)

            def ts(out, a, s1, op, s2=None, op2=ALU.bypass, name="v_ord"):
                if s2 is None:
                    return inc(dve.tensor_scalar(out, a, s1, None, op), name)
                return inc(dve.tensor_scalar(out, a, s1, s2, op, op2), name)

            def stt(out, a, s1, b, op, op2, name="v_ord"):
                return inc(dve.scalar_tensor_tensor(out=out, in0=a, scalar=s1, in1=b, op0=op, op1=op2), name)

            def cp(out, a, name="v_ord"):
                return inc(dve.tensor_copy(out, a), name)

            def done():
                own(dve, "v_ord")

            def z(l, u):
                split_at(UB[l] + u + 2)

            def o(l, m):
                split_at(UB[l] + ZU + m + 2)
                dve.wait_ge(sem["unit_done"], UB[l] + ZU + m + 1)
                tt(halves(X[:, m, :]), slot(m % 2), halves(X[:, m, :]), ALU.add, "wo_add")

            def rn(l, n):
                dve.wait_ge(sem["rs_a"], n + 1)
                dve.wait_ge(sem["load_par"], 16 * min(l + 1, LAYERS))
                col = ("g_mix", "g_ffn")[n % 2] if n < 2 * LAYERS else "g_final"

                def low(k):
                    dve.wait_ge(sem["h_hi"], l * 24 + (0 if n % 2 == 0 else 16) + k + 1)
                    tt(Hlo[:, k, :], TH[:, k % 2, :], Hhi[:, k, :].bitcast(F32), ALU.subtract, "h_lo")

                for k in range(KT):
                    a = PAR[col][0] + k
                    if n == 2 * LAYERS:
                        dst = YO[:, k, :]
                    else:
                        dst = TH[:, k % 2, :]
                        if k >= 2:
                            low(k - 2)
                            own(dve, "h_lo")
                    stt(dst, X[:, k, :], par[:, a:a + 1], RS, ALU.mult, ALU.mult, "h_f")
                if n < 2 * LAYERS:
                    low(KT - 2)
                    low(KT - 1)

            def chunks(ap):
                return ap[:, 0:T].rearrange("p (c t) -> p c t", c=NC_)

            def rows(l):
                n4 = slice(0, 4)
                m = RM[0:4, :]
                W(dve, "z_evac", l, 1)
                W(dve, "rsp_a", l)
                own(dve, "h_lo")
                stt(rf, rf, 0.0, fa, ALU.min, ALU.subtract)
                stt(ra, ra, 0.0, aa, ALU.max, ALU.add)
                ts(rb, rb, 1.0, ALU.add)
                done()
                ts(ra, ra, EA, ALU.mult, -1.0, ALU.mult)
                inc(dve.reciprocal(rb, rb), "v_ord")
                inc(dve.tensor_tensor_scan(fa[:, 0:T], reset[0:4, :], rf[:, 0:T], 0.0, ALU.mult, ALU.add), "v_ord")
                cp(fa[:, T:TOK], rf[:, T:TOK])
                inc(dve.tensor_tensor_scan(m[:, 0:T], rf[:, 0:T], ri[:, 0:T], 0.0, ALU.add, ALU.max), "v_ord")
                tt(t2[:, T:TOK], rf[:, T:TOK], pr("m0", n4), ALU.add)
                done()
                tt(m[:, T:TOK], t2[:, T:TOK], ri[:, T:TOK], ALU.max)
                inc(dve.tensor_tensor_scan(gg[:, 0:T], reset[0:4, :], ra[:, 0:T], 0.0, ALU.mult, ALU.add), "v_ord")
                cp(gg[:, T:TOK], ra[:, T:TOK])
                cp(QB[0:4, :], rb)
                done()
                tt(RA[0:4, :], fa, m, ALU.subtract)
                tt(t2, ri, fa, ALU.subtract)
                ts(QA[64:68, :], gg, -1.0, ALU.mult)
                cp(QB[64:68, :], gg)
                tt(chunks(t4), chunks(gg)[:, :, C - 1:C].broadcast_to([4, NC_, C]), chunks(gg), ALU.subtract)
                done()
                r = RA[0:4, :]
                cp(t1[:, 0:C], r[:, 0:C])
                tt(t1[:, C:T].rearrange("p (c t) -> p c t", t=C), r[:, C:T].rearrange("p (c t) -> p c t", t=C),
                   chunks(m)[:, 0:NC_ - 1, C - 1:C].broadcast_to([4, NC_ - 1, C]), ALU.add)
                tt(t1[:, T:TOK], r[:, T:TOK], pr("m0", n4), ALU.add)
                cp(QA[0:4, :], t2)
                tt(chunks(t3), chunks(t2), chunks(r)[:, :, C - 1:C].broadcast_to([4, NC_, C]), ALU.add)
                tt(t3[:, T:TOK], t2[:, T:TOK], r[:, T:TOK], ALU.add, "rpre_v")
                W(dve, "rex_a", l)
                tt(QB[32:36, :], rb, t5, ALU.mult, "rows_v")

            def conv(l):
                dve.wait_ge(sem["hist_d"], 96 * (l + 1))
                W(dve, "z_evac", l, 7)
                own(dve, "rows_v")
                W(dve, "rex_a", l)
                W(dve, "zero_g", l, 4)
                a = PAR["conv"][0]
                for w in range(KCH):
                    for j in range(6):
                        src, k = CB[:, j, w:w + CV], par[:, a + 4 * j + w:a + 4 * j + w + 1]
                        if w == 0:
                            ts(CY[:, j, :], src, k, ALU.mult, name="conv_v")
                        else:
                            dve.wait_ge(sem["conv_v"], l * 24 + 6 * (w - 1) + j + 1)
                            stt(CY[:, j, :], src, k, CY[:, j, :], ALU.mult, ALU.add, "conv_v")

            def l2(l):
                for i in range(2):
                    W(dve, "rs2_a", l, i + 1)
                    q = CB[:, 2 * i:2 * i + 2, 0:TOK]
                    tt(q, q, LS[:, 2 * i:2 * i + 2, :], ALU.mult, "l2_v")

            def by_head(ap):
                return ap.rearrange("p (h e) -> p h e", h=HEADS)

            def tcol(c, j):
                return TQ[:, c, j, :].rearrange("p (h o) -> p h o", o=1).broadcast_to([P, HEADS, DH])

            def gtok(l):
                W(dve, "tq_a", l)
                for c in range(NC_):
                    W(dve, "gtok_p", l, c + 1)
                    tt(by_head(KD[:, c, :]), by_head(M[c][:, 0:256]), tcol(c, 3), ALU.mult, "gtok_v")
                    tt(by_head(BK[:, c, :]), by_head(M[c][:, 0:256]), tcol(c, 5), ALU.mult, "gtok_v")
                    tt(by_head(BV[:, c, :]), by_head(M[c][:, 256:512]), tcol(c, 4), ALU.mult, "gtok_v")

            def c4(ap):
                return ap.rearrange("p (c t) -> p c t", c=NC_)

            def bc4(ap):
                return ap.rearrange("p (o t) -> p o t", o=1).broadcast_to([P, NC_, P])

            def glog(l, hp):
                for h in range(2):
                    head = 2 * hp + h
                    W(dve, "glog_p", l, head + 1)
                    if hp and h == 0:
                        W(dve, "zt_p", l, 6)
                    tt(EB[:, h, :, :], c4(M[0]), bc4(neg), ALU.add, "eb_v")
                    W(dve, "ebx_a", l, head + 1)
                    tt(PM[:, head, :, :], c4(M[2]), EB[:, h, :, :], ALU.mult, "pm_v")
                    own(dve, "pm_v")
                    tt(EB[:, h, :, :], c4(M[1]), EB[:, h, :, :], ALU.mult)
                    done()
                    tt(AT[:, h, :, :], c4(M[3]), EB[:, h, :, :], ALU.mult, "at_v")

            def eight(ap):
                return ap.rearrange("p h c t -> p (h c) t")

            def inv(l, hp):
                own(dve, "at_v")
                if hp:
                    W(dve, "y_p", l, 6)
                tt(eight(CT), eight(AT), lvl[:, 0:1, :].broadcast_to([P, 8, P]), ALU.mult)
                done()
                stt(eight(XT), eight(CT), -1.0, ident.rearrange("p (o t) -> p o t", o=1).broadcast_to([P, 8, P]),
                    ALU.mult, ALU.add, "xt0_v")
                for v in range(1, 7):
                    if v < 6:
                        W(dve, "z_p", l, 5 * hp + v)
                        x = XM.rearrange("p h c t -> p h (c t)")
                        if v == 1:
                            W(dve, "xm_a", l, hp + 1)
                        else:
                            own(dve, "xu_v")
                        tt(x, x, PS[:, 6:8, :], ALU.subtract, "xu_v")
                    W(dve, "zt_p", l, 6 * hp + v)
                    own(dve, "xt0_v" if v == 1 else "xtu_v")
                    x = XT.rearrange("p h c t -> p h (c t)")
                    tt(x, x, PS[:, 4:6, :], ALU.subtract, "xtu_v")

            def uw(l, hp):
                W(dve, "uw_p", l, hp + 1)
                for h in range(2):
                    a = hp * P + h * DH
                    cp(U[:, :, a:a + DH], M[0].rearrange("p (h c e) -> p h c e", h=2, c=NC_)[:, h, :, :], "uw_v")
                for h in range(2):
                    r = slice(h * DH, (h + 1) * DH)
                    last = dve.tensor_copy(ST[r, 0:NC_, hp, 1, :], c4(M[1 + h])[r])
                inc(last, "uw_v")

            def qe(l):
                W(dve, "qe_a", l)
                W(dve, "uw_p", l, 2)
                tt(QE.rearrange("p h c t -> p h (c t)"), CB[:, 0:2, 0:T], EGB[:, :, 0:T], ALU.mult, "qe_v")

            def carry(l, c, ps, decay, kinds):
                for hp in range(2):
                    for h in range(2):
                        r, e = slice(h * DH, (h + 1) * DH), slice(h * DH, (h + 1) * DH)
                        stt(ST[r, c + 1, hp, 0:kinds, e], ST[r, c, hp, 0:kinds, e],
                            decay[r, hp, c * C + C - 1:c * C + C], ps(hp)[r, :, e], ALU.mult, ALU.add, "st_v")

            def gst(l):
                W(dve, "zero_g", l, 4)
                own(dve, "uw_v")
                own(dve, "qe_v")
                for c in range(NC_):
                    if c:
                        W(dve, "gst_p", l, c)
                        tt(VN[:, c, :], U[:, c, :], M[0][:, 0:256], ALU.subtract, "vn_v")
                    else:
                        cp(VN[:, 0, :], U[:, 0, :], "vn_v")
                    W(dve, "gsd_p", l, c + 1)
                    if c:
                        own(dve, "st_v")
                    carry(l, c, lambda hp: M[1][:, hp * P:(hp + 1) * P].rearrange("p (k e) -> p k e", k=1), EGB, 1)

            def wide(ap):
                return ap.rearrange("p h (b o) -> p h b o", o=1).broadcast_to([P, 2, NB, DH])

            irep4 = irep.rearrange("p (x y e) -> p x y e", x=1, y=1).broadcast_to([P, 2, NB, DH])
            sums = PS[:, 4:6, :].rearrange("p h (b e) -> p h b e", b=NB)

            def sm(i):
                return SM[:, i, :].rearrange("p (h b) -> p h b", h=2)

            def bh(ap):
                return ap.rearrange("p h b e -> p (h b) e")

            def decay_state(l, n, decay):
                dve.wait_ge(sem["state_d"], l * 64 + 16 * n)
                tt(SD, SD, wide(decay), ALU.mult)

            def spread(vec, l, n, first=True):
                tt(DX, wide(vec), irep4, ALU.mult, "dx_v")
                W(dve, "dx_p", l, n)

            def contract(l, n, by, out, name):
                tt(DX, SD, wide(by), ALU.mult, "dx_v")
                W(dve, "dx_p", l, n)
                tt(DX, sums, irep4, ALU.mult)
                done()
                inc(dve.tensor_reduce(out, DX, AX.X, ALU.add), name)

            def gd(l):
                W(dve, "out_p", l, 2)
                q, k, v = (CB[:, 2 * i:2 * i + 2, T:TOK] for i in range(3))
                decay_state(l, 1, EGB[:, :, T:TOK])
                done()
                contract(l, 1, k, sm(0), "v_ord")
                done()
                tt(sm(1), v, sm(0), ALU.subtract)
                W(dve, "beta_p", l)
                done()
                tt(sm(1), sm(1), M[2][:, 0:16].rearrange("p (h b) -> p h b", h=2), ALU.mult)
                done()
                spread(sm(1), l, 2)
                tt(DX, sums, wide(k), ALU.mult)
                done()
                tt(SD, SD, DX, ALU.add)
                done()
                contract(l, 3, q, OG[:, :, T:TOK], "dec_v")

            def hn(l, i):
                o_, sq = ((OG, SQG), (OM, DA), (OL, SQL))[i]
                gate = (GZ, GB[:, 6:8, :], LA[:, 6:8, :])[i]
                y0 = (2, 0, 6)[i]
                W(dve, "hrs_a", l, i + 1)
                if i:
                    W(dve, "gate_a", l, i)
                tt(o_, o_, sq, ALU.mult, "hn_v")
                own(dve, "hn_v")
                for j in range(2):
                    a = PAR[("n_gdn", "n_mlstm", "n_gla")[i]][0] + j
                    stt(Y[:, y0 + j, :], o_[:, j, :], par[:, a:a + 1], gate[:, j, :], ALU.mult, ALU.mult, "hn_v")

            def mtok(l):
                for c in range(NC_):
                    W(dve, "vp_a", l, 8 + 2 * c + 2)
                    tt(by_head(KD[:, c, :]), by_head(M[c][:, 0:256]), tcol(c, 1), ALU.mult, "mkd_v")

            def mst(l):
                W(dve, "kind_g", l)
                W(dve, "mbc_a", l)
                for c in range(NC_):
                    W(dve, "up_p", l, c + 1)
                    own(dve, "st_v")
                    carry(l, c, lambda hp: M[c][:, hp * 256:(hp + 1) * 256].rearrange("p (k e) -> p k e", k=2), WI, 2)

            def mlog(l):
                W(dve, "dec_v", l, 1)
                W(dve, "so_g", l, 1)
                for head in range(HEADS):
                    a = 2 * (head % 2)
                    W(dve, "mlog_p", l, head + 1)
                    tt(EM[:, head % 2, :, :], c4(M[a]), bc4(neg), ALU.add, "em_v")
                    W(dve, "emx_a", l, head + 1)
                    tt(PM[:, head, :, :], c4(M[a + 1]), EM[:, head % 2, :, :], ALU.mult, "mpm_v")
                W(dve, "z_evac", l, 11)
                tt(GB[:, 0:2, 0:T], GB[:, 0:2, 0:T], WI[:, :, 0:T], ALU.mult, "qw_v")

            def mout(l):
                W(dve, "da_a", l)
                tt(DA[:, :, 0:T], DA[:, :, 0:T], EMN[:, :, 0:T], ALU.max)
                done()
                inc(dve.reciprocal(DA[:, :, 0:T], DA[:, :, 0:T]), "v_ord")
                done()
                tt(OM[:, :, 0:T], PS[:, 4:6, :], DA[:, :, 0:T], ALU.mult, "mo_v")

            def md(l):
                q, k, v = (GB[:, 2 * i:2 * i + 2, T:TOK] for i in range(3))
                W(dve, "z_evac", l, 15)
                decay_state(l, 3, WI[:, :, T:TOK])
                tt(sm(1), sm(2), k, ALU.mult)
                tt(NS, NS, WI[:, :, T:TOK], ALU.mult)
                W(dve, "out_p", l, 4)
                spread(v, l, 4)
                done()
                tt(DX, sums, wide(sm(1)), ALU.mult)
                tt(NS, NS, sm(1), ALU.add, "nsn_v")
                own(dve, "nsn_v")
                tt(sm(3), NS, q, ALU.mult, "nq_v")
                done()
                tt(SD, SD, DX, ALU.add)
                done()
                contract(l, 5, q, sm(4), "v_ord")
                W(dve, "nd_a", l)
                tt(sm(5), sm(5), EMN[:, :, T:TOK], ALU.max)
                done()
                inc(dve.reciprocal(sm(5), sm(5)), "v_ord")
                done()
                tt(OM[:, :, T:TOK], sm(4), sm(5), ALU.mult, "dec_v")

            def lg(l):
                W(dve, "lsp_a", l)
                stt(GG, GG, 0.0, EG, ALU.min, ALU.subtract)
                done()
                ts(GG, GG, 1.0 / 16.0, ALU.mult)
                done()
                for hp in range(2):
                    inc(dve.tensor_tensor_scan(EG[:, hp, 0:T], reset, GG[:, hp, 0:T], 0.0, ALU.mult, ALU.add), "v_ord")
                inc(dve.tensor_copy(EG[:, :, T:TOK], GG[:, :, T:TOK]), "lcum_v")

            def pc(ap):
                return ap[:, :, 0:T].rearrange("p h (c t) -> p h c t", c=NC_)

            def lk(l):
                W(dve, "lk_a", l)
                W(dve, "z_evac", l, 21)
                tt(KI[0], KI[0], pc(LA[:, 2:4, :]), ALU.mult, "lke_v")

            def lst(l):
                W(dve, "leg_a", l)
                for c in range(NC_):
                    W(dve, "up_p", l, 4 + c + 1)
                    own(dve, "st_v")
                    carry(l, c, lambda hp: M[c][:, hp * P:(hp + 1) * P].rearrange("p (k e) -> p k e", k=1), GG, 1)

            def lsub(l):
                W(dve, "hn_v", l, 6)
                W(dve, "lcum_v", l)
                g16 = EG[:, :, 0:T].rearrange("p h (i t) -> p h i t", t=SUB)
                q16 = QI[:, :, 0:T].rearrange("p h (i t) -> p h i t", t=SUB)
                ref = g16[:, :, :, SUB // 2 - 1:SUB // 2]
                tt(q16, g16, ref.broadcast_to([P, 2, NC_ * NSUB, SUB]), ALU.subtract, "lsub_v")
                W(dve, "ltok_p", l)
                W(dve, "ki0_g", l)
                for i in range(NSUB):
                    w = (i + 1) * SUB
                    at = i * SUB + SUB // 2 - 1
                    g = pc(EG)
                    tt(KI[i][:, :, :, 0:w], g[:, :, :, at:at + 1].broadcast_to([P, 2, NC_, w]), g[:, :, :, 0:w],
                       ALU.subtract, "lsub_v")
                W(dve, "lsub_a", l, 1)
                tt(QI[:, :, 0:T], QI[:, :, 0:T], LA[:, 0:2, 0:T], ALU.mult, "ki_v")
                for i in range(NSUB):
                    w = (i + 1) * SUB
                    W(dve, "lsub_a", l, i + 2)
                    tt(KI[i][:, :, :, 0:w], KI[i][:, :, :, 0:w], pc(LA[:, 2:4, :])[:, :, :, 0:w], ALU.mult, "ki_v")

            def llog(l):
                W(dve, "so_g", l, 2)
                for head in range(HEADS):
                    W(dve, "llog_p", l, head + 1)
                    tt(PM[:, head, :, :], c4(M[head]), bc4(tri), ALU.mult, "lpm_v")
                own(dve, "ki_v")
                tt(LA[:, 0:2, 0:T], LA[:, 0:2, 0:T], GG[:, :, 0:T], ALU.mult, "lqe_v")

            def ld(l):
                q, k, v = (LA[:, 2 * i:2 * i + 2, T:TOK] for i in range(3))
                decay_state(l, 4, GG[:, :, T:TOK])
                spread(v, l, 6)
                tt(DX, sums, wide(k), ALU.mult)
                done()
                tt(SD, SD, DX, ALU.add)
                done()
                contract(l, 7, q, OL[:, :, T:TOK], "dec_v")

            def sc(l):
                W(dve, "z_evac", l, 31)
                W(dve, "spad_g", l)
                own(dve, "hn_v")
                w3 = SCB[:, :, T + KSC - 1:SW - 1].rearrange("p j (b w) -> p j b w", w=KSC)
                tt(SCB[:, :, KSC - 1:KSC - 1 + T], GB[:, 2:4, 0:T], GB[:, 4:6, 0:T], ALU.mult)
                tt(w3[:, :, :, KSC - 1], GB[:, 2:4, T:TOK], GB[:, 4:6, T:TOK], ALU.mult, "scu_v")
                dve.wait_ge(sem["shist_d"], 32 * (l + 1))
                own(dve, "scu_v")
                a = PAR["sconv"][0]
                for w in range(KSC):
                    if w:
                        done()
                    for j in range(2):
                        src, k = SCB[:, j, w:w + SV], par[:, a + 3 * j + w:a + 3 * j + w + 1]
                        if w == 0:
                            ts(SCY[:, j, :], src, k, ALU.mult)
                        else:
                            stt(SCY[:, j, :], src, k, SCY[:, j, :], ALU.mult, ALU.add)
                done()
                tt(Y[:, 4:6, 0:T], GB[:, 0:2, 0:T], SCY[:, :, 0:T], ALU.mult, "sc_v")
                tt(Y[:, 4:6, T:TOK], GB[:, 0:2, T:TOK], SCY[:, :, T + KSC - 1:SV:KSC], ALU.mult, "sc_v")

            def ysp(l):
                own(dve, "sc_v")
                for k in range(KT):
                    dve.wait_ge(sem["h_hi"], l * 24 + 8 + k + 1)
                    tt(Hlo[:, k, :], Y[:, k, :], Hhi[:, k, :].bitcast(F32), ALU.subtract, "h_lo")

            def router(l):
                a, b = PAR["router"]
                dve.wait_ge(sem["rwhi_a"], 1)
                tt(RWlo[:, :], par[:, a:b], RWhi[:, :].bitcast(F32), ALU.subtract, "rwlo_v")
                L, E1, S1, L2, EX, S2, WT_, G = (RTK[:, i, :, :] for i in range(8))
                inc(dve.memset(RTK[:, :, :, :], 0.0), "v_ord")
                dve.wait_ge(sem["rt_p"], 1)
                done()
                rb_ = PAR["router_b"]
                bias = par[:, rb_[0]:rb_[1]].rearrange("p (o e) -> p o e", o=1)
                tt(L[:, 0:4, :], M[0][:, 0:32].rearrange("p (i e) -> p i e", e=8), bias.broadcast_to([P, 4, 8]), ALU.add)
                tt(L[0:NB, 4:5, :], M[0][0:NB, 32:40].rearrange("p (i e) -> p i e", e=8), bias[0:NB], ALU.add)
                done()
                rev = cn("rev").rearrange("p (o e) -> p o e", o=1).broadcast_to([P, 5, 8])

                def col(i):
                    return RC[:, i, :].rearrange("p (i o) -> p i o", o=1).broadcast_to([P, 5, 8])

                def best(src, out, i):
                    inc(dve.tensor_reduce(RC[:, i, :], src, AX.X, ALU.max), "v_ord")
                    done()
                    tt(E1, src, col(i), ALU.is_equal)
                    done()
                    tt(E1, E1, rev, ALU.mult)
                    done()
                    inc(dve.tensor_reduce(RC[:, 2, :], E1, AX.X, ALU.max), "v_ord")
                    done()
                    tt(out, E1, col(2), ALU.is_equal)
                    done()

                best(L, S1, 0)
                tt(EX, L, col(0), ALU.subtract, "rl_v")
                stt(L2, S1, -1e30, L, ALU.mult, ALU.add)
                done()
                best(L2, S2, 1)
                tt(S1, S1, S2, ALU.add)
                done()
                dve.wait_ge(sem["rexp_a"], 1)
                tt(WT_, S1, EX, ALU.mult)
                done()
                inc(dve.tensor_reduce(RC[:, 3, :], WT_, AX.X, ALU.add), "v_ord")
                done()
                inc(dve.reciprocal(RC[:, 3, :], RC[:, 3, :]), "v_ord")
                done()
                tt(G, WT_, col(3), ALU.mult, "rg_v")

            split_at(0)
            split_at(1)
            dve.wait_ge(sem["load_con"], 16)
            STEPS = dict(rows=rows, conv=conv, l2=l2, gtok=gtok, glog=glog, inv=inv, uw=uw, qe=qe, gst=gst,
                         gd=gd, hn=hn, mtok=mtok, mst=mst, mlog=mlog, mout=mout, md=md, lg=lg, lk=lk, lst=lst,
                         lsub=lsub, llog=llog, ld=ld, sc=sc, ysp=ysp)

            for l in range(LAYERS):
                for step in ORDER:
                    name, arg = step if isinstance(step, tuple) else (step, None)
                    if name == "z":
                        z(l, arg)
                    elif name == "o":
                        o(l, arg)
                    elif name == "rnm":
                        rn(l, 2 * l)
                    elif name == "rnf":
                        rn(l, 2 * l + 1)
                    elif name in STEPS:
                        STEPS[name](l) if arg is None else STEPS[name](l, arg)
                if l == 1:
                    router(l)
                base = UB[l] + ZU + OU

                def group(e, last):
                    def split_next(i):
                        if last and i + 2 >= EU:
                            split_at(base + e * EU + i + 2)
                            return
                        g = base + i + 2
                        split(e * EU + g, GF if 2 * GF <= (i + 2) % EU else KT, g % SPLIT, g % RAW)

                    for f in range(GF):
                        split_next(2 * f)
                        dve.wait_ge(sem["unit_done"], e * EU + (base + 2 * f + 2))
                        dve.wait_ge(sem["silu_g"], e * GF + (GF * GROUPS_BEFORE[l] + f + 1))
                        af = AF[:, f % 2, :]
                        if l == 0:
                            tt(halves(af), slot(2 + f % 2), halves(SG[:, f % 2, :]), ALU.mult, "af_v")
                        else:
                            tt(halves(af), slot(2 + f % 2), halves(SG[:, f % 2, :]), ALU.mult, "m_v")
                            dve.wait_ge(sem["m_v"], e * GF + (f + 1))
                            gt = GT[:, e, :] if isinstance(e, int) else \
                                GT[:, bass.ds(e, 1), :].rearrange("p o t -> p (o t)")
                            tt(af, af, gt, ALU.mult, "af_v")
                        split_next(2 * f + 1)
                        dve.wait_ge(sem["ahi_a"], e * GF + (GF * GROUPS_BEFORE[l] + f + 1))
                        tt(Alo[:, f, :], af, Ahi[:, f, :].bitcast(F32), ALU.subtract, "glu_v")
                    for m in range(KT):
                        dve.wait_ge(sem["unit_done"], e * EU + (base + 2 * GF + m + 1))
                        tt(halves(X[:, m, :]), slot(DOWN_SLOT[m]), halves(X[:, m, :]), ALU.add, "down_v")
                        split_next(2 * GF + m)

                if l:
                    dve.wait_ge(sem["stored_g"], 2)
                else:
                    dve.wait_ge(sem["stored_g"], 1)
                before = dict(count)
                with dve.Fori(0, NG[l] - 1) as e:
                    group(e, False)
                looped(before, NG[l] - 1)
                group(NG[l] - 1, True)
            rn(LAYERS, 4)

        return count


def tiles(w, kt):
    k, m = w.shape[-2:]
    lead = w.shape[:-2]
    w = w.reshape(*lead, kt, P, m // P, P)
    n = len(lead)
    return np.ascontiguousarray(np.moveaxis(w, n + 2, n)).swapaxes(n + 1, n + 2).reshape(*lead, m // P, P, kt * P)


def feature_tiles(a):
    return np.moveaxis(a.reshape(*a.shape[:-1], a.shape[-1] // P, P), (-1, -2), (0, 1))


def lay_out(i):
    f = np.float32
    out = {}
    x = np.concatenate([i["x_prompt"][0], i["x_sample"][:, 0]], 0)
    out["xT"] = np.ascontiguousarray(x.T).reshape(KT, P, TOK)
    w = i["w_in"]
    G = 256
    m0, g0 = 0, 4 * G + 8
    s0 = g0 + 4 * G + 8
    l0 = s0 + 3 * G
    small = np.zeros((LAYERS, D, P), f)
    for at, a, n in ((0, m0 + 4 * G, 4), (32, m0 + 4 * G + 4, 4), (64, g0 + 4 * G, 4), (96, g0 + 4 * G + 4, 4),
                     (4, l0 + 4 * G, 16)):
        small[:, :, at:at + n] = w[:, :, a:a + n]
    z = np.concatenate([small, w[:, :, g0:g0 + 4 * G], w[:, :, m0:m0 + 4 * G], w[:, :, l0:l0 + 4 * G],
                        w[:, :, s0:s0 + 3 * G]], -1)
    out["wz"] = tiles(z, KT)
    out["wo"] = tiles(i["w_out"], KT)
    FE = GF * P
    gate = np.concatenate([i["ffn_w_gate"][0].reshape(D, 2, FE).swapaxes(0, 1), i["moe_w_gate"][0]], 0)
    up = np.concatenate([i["ffn_w_up"][0].reshape(D, 2, FE).swapaxes(0, 1), i["moe_w_up"][0]], 0)
    down = np.concatenate([i["ffn_w_down"][0].reshape(2, FE, D), i["moe_w_down"][0]], 0)
    out["wgu"] = np.stack([tiles(gate, KT), tiles(up, KT)], 2).reshape(GEXP, 2 * GF, P, KT * P)
    out["wd"] = tiles(down, GF)
    out["con"] = constants()
    h = np.arange(EXPERTS)
    out["sel8"] = np.repeat(np.eye(EXPERTS, dtype=f), P, 1)
    par = np.zeros((LAYERS, P, PARW), f)

    def put(name, a, rows=slice(0, P), cols=None):
        s = PAR[name][0] + (0 if cols is None else cols)
        a = a.reshape(LAYERS, a.shape[1], -1)
        par[:, rows, s:s + a.shape[2]] = a

    def cols(a):
        return np.moveaxis(feature_tiles(a), 2, 0)

    put("g_mix", cols(i["g_mix"]))
    put("g_ffn", cols(i["g_ffn"]))
    put("g_final", np.broadcast_to(feature_tiles(i["g_final"]), (LAYERS, P, KT)))
    put("n_mlstm", cols(i["mlstm_norm"]))
    put("n_gdn", cols(i["gdn_norm"]))
    put("n_gla", cols(i["gla_norm"]))
    put("conv", i["gdn_conv_w"].reshape(LAYERS, 6, P, KCH).swapaxes(1, 2))
    put("sconv", i["sc_conv_w"].reshape(LAYERS, 2, P, KSC).swapaxes(1, 2))
    put("gla_b", cols(i["gla_b_gate"]))
    put("gate_b", i["mlstm_b_i"], slice(0, 4))
    put("gate_b", i["mlstm_b_f"], slice(32, 36))
    put("gate_b", i["gdn_dt_bias"], slice(64, 68))
    put("a_log", i["gdn_a_log"], slice(0, 4))
    put("m0", i["state_mlstm_m"].swapaxes(1, 2), slice(0, 4))
    put("wgate", i["gla_w_gate"], slice(100, 116))
    par[1, :, PAR["router"][0]:PAR["router"][1]] = \
        i["moe_w_router"][0].reshape(KT, P, EXPERTS).swapaxes(0, 1).reshape(P, -1)
    par[1, :, PAR["router_b"][0]:PAR["router_b"][1]] = i["moe_b_router"][0][None]
    out["par"] = par

    def state(s):
        s = s.reshape(LAYERS, NB, 2, 2, DH, DH).transpose(0, 3, 4, 2, 1, 5)
        return np.ascontiguousarray(s).reshape(LAYERS, P, 2, NB, DH)

    out["mC"], out["gS"], out["lS"] = (state(i[n]) for n in ("state_mlstm_C", "state_gdn_S", "state_gla_S"))
    n = i["state_mlstm_n"].reshape(LAYERS, NB, 2, 2, DH).transpose(0, 3, 4, 2, 1)
    out["mn"] = np.ascontiguousarray(n).reshape(LAYERS, P, 2, NB)
    c = i["state_gdn_conv"].reshape(LAYERS, NB, KCH - 1, 6, P).transpose(0, 3, 4, 1, 2)
    out["gconv"] = np.ascontiguousarray(c)
    c = i["state_sc_conv"].reshape(LAYERS, NB, KSC - 1, 2, P).transpose(0, 3, 4, 1, 2)
    out["sconv"] = np.ascontiguousarray(c)
    return out


OUTPUTS = dict(y=(KT, P, TOK), mC_p=(LAYERS, P, 2, DH), mC_s=(LAYERS, P, 2, NB, DH), gS_p=(LAYERS, P, 2, DH),
               gS_s=(LAYERS, P, 2, NB, DH), lS_p=(LAYERS, P, 2, DH), lS_s=(LAYERS, P, 2, NB, DH),
               mn=(LAYERS, P, 2, NB + 1), mm=(LAYERS, HEADS, TOK), gtail=(LAYERS, P, 6, 27), stail=(LAYERS, P, 2, 18))


def results(r):
    y = r["y"].reshape(D, TOK).T
    y_p, y_s = y[None, 0:T], y[T:TOK, None]

    def state(s, b):
        s = s.reshape(LAYERS, 2, DH, 2, b, DH).transpose(0, 4, 3, 1, 2, 5)
        return s.reshape(LAYERS, b, HEADS, DH, DH)

    def tail(t, j, w):
        t = t.reshape(LAYERS, P, j, NB + 1, w).transpose(0, 3, 4, 2, 1).reshape(LAYERS, NB + 1, w, j * P)
        return t[:, 0:1], t[:, 1:]

    n = r["mn"].reshape(LAYERS, 2, DH, 2, NB + 1).transpose(0, 4, 3, 1, 2).reshape(LAYERS, NB + 1, HEADS, DH)
    m = r["mm"].transpose(0, 2, 1)
    gt, st = tail(r["gtail"], 6, KCH - 1), tail(r["stail"], 2, KSC - 1)
    out = (y_p, y_s, state(r["mC_p"], 1), state(r["mC_s"], NB), n[:, 0:1], n[:, 1:], m[:, T - 1:T], m[:, T:TOK],
           state(r["gS_p"], 1), state(r["gS_s"], NB), gt[0], gt[1], st[0], st[1],
           state(r["lS_p"], 1), state(r["lS_s"], NB))
    return tuple(np.ascontiguousarray(a) for a in out)


def kernel(**inputs):
    import concourse.bacc as _bacc
    from concourse.bass_utils import run_bass_kernel_spmd as _run

    arrays = lay_out({k: np.asarray(v) for k, v in inputs.items()})
    nc = _bacc.Bacc("TRN2", target_bir_lowering=False, num_devices=1)
    ins = {k: nc.dram_tensor(f"in_{k}", a.shape, F32, kind="ExternalInput").ap() for k, a in arrays.items()}
    outs = {k: nc.dram_tensor(f"out_{k}", s, F32, kind="ExternalOutput").ap() for k, s in OUTPUTS.items()}
    build(nc, ins, outs)
    r = _run(nc, [{f"in_{k}": a for k, a in arrays.items()}], core_ids=[0])
    return results({k: r.results[0][f"out_{k}"] for k in OUTPUTS})
```

```python
from contextlib import ExitStack

import numpy as np

import concourse.bass as bass
from concourse import mybir

F32 = mybir.dt.float32
F32R = mybir.dt.float32r
ALU = mybir.AluOpType
ACT = mybir.ActivationFunctionType
AX = mybir.AxisListType

P = 128
D = 1024
KT = D // P
T, NB = 512, 8
TOK = T + NB
HALF = TOK // 2
LAYERS = 2
HEADS, DH = 4, 64
C = 128
NC_ = T // C
SUB = 32
NSUB = C // SUB
EPS = 1e-6
GEXP, GF = 10, 11
EXPERTS = 8
CAP = 224
ROUNDS = -(-TOK // CAP)
SLOTS = ((0, P), (1, CAP - P))
ZU, OU = 31, 8
EU = 2 * GF + KT
RAW, SPLIT = 3, 2
RAW_E, SPLIT_E = 6, 3
UNITS = [ZU + OU + 2 * EU, ZU + OU + EXPERTS * EU]
KCH, KSC = 4, 3
CW = T + KCH - 1 + NB * KCH + 1
CV = T + KCH - 1 + NB * KCH - KCH + 1
SW = T + KSC - 1 + NB * KSC + 1
SV = T + KSC - 1 + NB * KSC - KSC + 1

PAR = {}
_n = 0
for _name, _w in (("g_mix", 8), ("g_ffn", 8), ("g_final", 8), ("n_mlstm", 2), ("n_gdn", 2), ("n_gla", 2),
                  ("conv", 24), ("sconv", 6), ("gla_b", 2), ("gate_b", 1), ("a_log", 1), ("m0", 8),
                  ("wgate", 256), ("router", 64), ("router_b", 8)):
    PAR[_name] = (_n, _n + _w)
    _n += _w
PARW = _n

CON = {}
_n = 0
for _name, _w in (("ident", 128), ("neg", 128), ("tri", 128), ("lvl", 896), ("bones", 128), ("ones", 256),
                  ("irep", 64), ("sel", 512), ("ehp", 256), ("reset", 512),
                  ("rev", 8), ("eps", 1), ("ln8", 1), ("one", 1), ("valid", 5), ("caps", 4), ("slots", CAP), ("slotp", 2), ("ncap", 8)):
    CON[_name] = (_n, _n + _w)
    _n += _w
CONW = _n


def constants():
    c = np.zeros((P, CONW), np.float32)

    def put(name, a):
        c[:, CON[name][0]:CON[name][1]] = a.reshape(P, -1)

    s, t = np.arange(P)[:, None], np.arange(P)[None, :]
    put("ident", (s == t).astype(np.float32))
    put("neg", np.where(s <= t, 0.0, -1e30).astype(np.float32))
    put("tri", (s <= t).astype(np.float32))
    lv = [((s // (2 * b) == t // (2 * b)) & (s % (2 * b) < b) & (t % (2 * b) >= b)) for b in (1, 2, 4, 8, 16, 32, 64)]
    put("lvl", np.stack(lv, 1).astype(np.float32))
    put("bones", (s // DH == t // DH).astype(np.float32))
    put("ones", np.broadcast_to(np.arange(2 * P) // DH != 2, (P, 2 * P)).astype(np.float32))
    put("irep", (s % DH == np.arange(DH)[None, :]).astype(np.float32))
    h = np.arange(HEADS)[None, :, None]
    put("sel", np.broadcast_to(s[:, :, None] % 32 == h, (P, HEADS, P)).astype(np.float32))
    hp = np.arange(2)[None, :, None]
    put("ehp", (s[:, :, None] % 32 == 2 * hp + t[:, None, :] // DH).astype(np.float32))
    put("reset", np.broadcast_to((np.arange(T) % C != 0)[None, :], (P, T)).astype(np.float32))
    put("rev", np.broadcast_to(np.arange(8, 0, -1, dtype=np.float32)[None, :], (P, 8)))
    put("eps", np.full((P, 1), EPS, np.float32))
    put("ln8", np.full((P, 1), -0.5 * np.log(DH), np.float32))
    put("valid", (np.arange(5)[None, :] * P + s < TOK).astype(np.float32))
    put("caps", np.broadcast_to(CAP * np.arange(4, dtype=np.float32)[None, :], (P, 4)))
    put("slots", np.broadcast_to(np.arange(1, CAP + 1, dtype=np.float32)[None, :], (P, CAP)))
    put("slotp", (s + 1 + P * np.arange(2)[None, :]).astype(np.float32))
    put("ncap", np.where(s == np.arange(8)[None, :], -CAP, 0).astype(np.float32))
    put("one", np.ones((P, 1), np.float32))
    return c


N = dict(
    at_v=4, beta_p=1, conv_v=24, ct_g=24, da_a=1, dec_v=3, dx_p=7, dx_v=7, eb_v=4, ebx_a=4, em_v=4, emx_a=4,
    gate_a=2, glog_p=4, gsd_p=4, gst_p=3, gtok_p=4, gtok_v=12, hn_p=3, hn_v=9, hrs_a=3, hsq_a=3, ki0_g=1,
    ki_v=5, kind_g=1, l2_p=2, l2_v=2, lcum_v=1, leg_a=1, lg_p=1, lk_a=1, lkd_a=4, lke_v=1, llog_p=4, ln2_a=2,
    lpm_v=4, lqe_v=1, lsp_a=1, lsub_a=5, lsub_v=5, ltok_p=4, mbc_a=3, mbc_p=3, mkd_v=4, mlog_p=4, mo_v=1,
    mpm_v=4, mtok_p=4, nd_a=1, nq_p=1, nq_v=1, nsn_v=1, nso_a=3, o_a=4, out_p=6, pm_v=4, qe_a=1, qe_p=1,
    qe_v=1, qw_v=1, rex_a=6, rows_v=1, rpre_v=1, rs2_a=2, rsp_a=2, sc_v=2, scu_v=1, silu_a=3, so_a=6, so_g=3,
    spad_g=2, sq2_a=2, st_v=48, stail_a=2, tail_a=2, tq_a=2, tq_p=2, up_p=8, uw_p=2, uw_v=6, vn_v=4, vp_a=24,
    wo_add=8, xm_a=4, xt0_v=2, xtr_p=4, xtu_v=24, xu_v=20, y_p=24, ys_a=24, z_evac=31, z_p=20, zero_g=4,
    zt_p=24,
)


def build(nc, A, O):
    with ExitStack() as ctx:
        def sb(name, shape, dt=F32, stack=ctx):
            return stack.enter_context(nc.sbuf_tensor("sb_" + name, shape, dt))

        X = sb("x", [P, KT, TOK])
        normed = ExitStack()
        Hhi, Hlo = sb("h_hi", [P, KT, TOK], F32R, normed), sb("h_lo", [P, KT, TOK], F32R, normed)
        normed.close()
        more = ExitStack()
        Whi3, Wlo3 = sb("w_hi3", [P, GF * P], F32R, more), sb("w_lo3", [P, GF * P], F32R, more)
        Wraw3 = sb("w_raw3", [P, RAW_E - RAW, GF * P], stack=more)
        SGG, AFG = sb("sgg", [P, 2, CAP], stack=more), sb("afg", [P, 2, CAP], stack=more)
        rest = sb("rest", [P, 2 * KT * TOK - (RAW_E - RAW + 2) * GF * P - 4 * CAP], stack=more)
        ctx.enter_context(more)
        Wraw = sb("w_raw", [P, RAW, GF * P])
        Whi, Wlo = sb("w_hi", [P, SPLIT, GF * P], F32R), sb("w_lo", [P, SPLIT, GF * P], F32R)
        con = sb("con", [P, CONW])
        par = sb("par", [P, PARW])
        mixers = ExitStack()
        Y = sb("y", [P, KT, TOK], stack=mixers)
        GA = sb("ga", [P, 6 * CW + 2 * TOK], stack=mixers)
        GB = sb("gb", [P, 8, TOK], stack=mixers)
        S = sb("s", [P, 14522], stack=mixers)
        mixers.close()
        ffn = ExitStack()
        Ahi, Alo = sb("a_hi", [P, GF, TOK], F32R, ffn), sb("a_lo", [P, GF, TOK], F32R, ffn)
        SG = sb("silu_g", [P, 2, TOK], stack=ffn)
        AF = sb("act_f", [P, 2, TOK], stack=ffn)
        ffn.close()
        experts = ExitStack()
        HTh, HTl = sb("ht_hi", [P, 5, D], F32R, experts), sb("ht_lo", [P, 5, D], F32R, experts)
        Hgh, Hgl = sb("hg_hi", [P, KT, CAP], F32R, experts), sb("hg_lo", [P, KT, CAP], F32R, experts)
        Agh, Agl = sb("ag_hi", [P, GF, CAP], F32R, experts), sb("ag_lo", [P, GF, CAP], F32R, experts)
        yt = sb("yt", [P, KT * CAP], stack=experts)
        YT = yt[:, :].rearrange("p (k t) -> p k t", k=KT)
        Yhi, Ylo = sb("yg_hi", [P, 2, D], F32R, experts), sb("yg_lo", [P, 2, D], F32R, experts)
        SelG = sb("sel_g", [P, 5, CAP], F32R, experts)
        SelT = sb("sel_t", [P, 2, TOK], F32R, experts)
        KEY, KC = sb("key", [P, 5, 8], stack=experts), sb("key_col", [P, 5], stack=experts)
        KEYT, KTM = (con[r:r + 8, CON["lvl"][0]:CON["lvl"][0] + TOK] for r in (0, 32))
        GH, GE = sb("gate_parts", [P, 5, 8, 2], F32R, experts), sb("gate_e", [P, 5, 2], F32R, experts)
        GC = sb("gate_col", [P, 2], stack=experts)
        NI = sb("turns", [1, 1], mybir.dt.int32, experts)
        RTK = yt[:, 0:320].rearrange("p (a i e) -> p a i e", a=8, i=5)
        RWhi, RWlo = sb("rw_hi", [P, 64], F32R, experts), sb("rw_lo", [P, 64], F32R, experts)
        RC = sb("router_c", [P, 4, 5], stack=experts)
        experts.close()
        PS = ctx.enter_context(nc.psum_tensor("ps", [P, 8, 512], F32))

        sem = {}

        def new(*names):
            for name in names:
                sem[name] = ctx.enter_context(nc.semaphore(name))

        new("a_ord", "af_v", "ahi_a", "at_v", "beta_p", "conv_v", "ct_g", "da_a", "dec_v", "down_v", "dx_p",
            "dx_v", "eb_v", "ebx_a", "em_v", "emx_a", "gate_a", "gc_v", "glog_p", "glu_v", "gsd_p", "gst_p",
            "gtok_p", "gtok_v", "h_f", "h_hi", "h_lo", "hg_p", "hgh_a", "hgl_v", "hist_d", "hn_p", "hn_v", "hrs_a",
            "hsq_a", "ht_p", "hth_a", "htl_v", "kc_v", "key_p", "key_v", "keyt_v", "ki0_g", "ki_v", "kind_g", "kt_a",
            "ktm1_v", "ktm_v", "l2_p", "l2_v", "lcum_v", "leg_a", "lg_p", "lk_a", "lkd_a", "lke_v", "llog_p",
            "ln2_a", "load_con", "load_par", "load_x", "lpm_v", "lqe_v", "lsp_a", "lsub_a", "lsub_v", "ltok_p",
            "mbc_a", "mbc_p", "mkd_v", "mlog_p", "mo_v", "mpm_v", "mtok_p", "nd_a", "nq_p", "nq_v", "nsn_v", "nso_a",
            "o_a", "out_p", "pm_v", "qe_a", "qe_p", "qe_v", "qw_v", "rex_a", "rexp_a", "rl_v", "rows_v", "rpre_v",
            "rs2_a", "rs_a", "rsp_a", "rt_p", "rwlo_v", "saf_v", "sahi_a", "sc_p", "sc_v", "scu_v", "sel_v",
            "selg_v", "selt_v", "sglu_v", "shist_d", "silu_a", "silu_g", "so_a", "so_g", "spad_g", "sq2_a", "sq_a",
            "ssilu_a", "ssq_p", "st_v", "stail_a", "state_d", "stored", "stored_g", "tail_a", "tq_a", "tq_p", "tr_p",
            "turns_v", "unit_done", "up_p", "uw_p", "uw_v", "v_ord", "vn_v", "vp_a", "w_hi", "w_lo", "wo_add",
            "xadd_v", "xm_a", "xt0_v", "xtr_p", "xtu_v", "xu_v", "y_p", "y_stored", "yhi_a", "ylo_v", "ys_a", "yt_a",
            "z_evac", "z_p", "zero_g", "zt_p")
        new(*[f"w_raw{i}" for i in range(RAW_E)])
        count = dict.fromkeys(sem, 0)

        def inc(ins, name):
            ins.then_inc(sem[name], 1)
            count[name] += 1
            return ins

        def own(eng, name):
            if count[name]:
                eng.wait_ge(sem[name], count[name])

        def looped(before, times):
            for name in count:
                count[name] += (times - 1) * (count[name] - before[name])

        def W(eng, name, l, k=None):
            value = l * N[name] + (N[name] if k is None else k)
            if value:
                eng.wait_ge(sem[name], value)

        def cn(name, rows=None):
            a, b = CON[name]
            return con[:, a:b] if rows is None else con[rows, a:b]

        ident, ones, bones, tri, neg = cn("ident"), cn("ones"), cn("bones"), cn("tri"), cn("neg")
        lvl = cn("lvl").rearrange("p (l t) -> p l t", l=7)
        ones, onesh = ones[:, 0:P], [ones[:, DH + DH * h:DH + DH * h + P] for h in range(2)]
        irep = cn("irep")
        reset = cn("reset")
        EPSC, LN8 = cn("eps"), cn("ln8")
        sel = cn("sel").rearrange("p (h m) -> p h m", h=HEADS)
        ehp = cn("ehp").rearrange("p (h m) -> p h m", h=2)

        def pr(name, rows=slice(0, P)):
            a, b = PAR[name]
            return par[rows, a:b]

        def cut(o, *shape):
            n = int(np.prod(shape))
            v = S[:, o:o + n]
            names = "abcde"[:len(shape)]
            if len(shape) == 1:
                return v
            return v.rearrange(f"p ({' '.join(names)}) -> p {' '.join(names)}",
                               **{x: w for x, w in zip(names[1:], shape[1:])})

        VP = cut(0, NC_, HEADS, P)
        ST = cut(2048, NC_ + 1, 2, 2, P)
        KD = cut(4608, NC_, 256)
        PM = cut(5632, HEADS, NC_, P)
        R0 = 7680
        QA, QB, RA = cut(R0 + 4160, TOK), cut(R0 + 4680, TOK), cut(R0 + 5200, TOK)
        RM = cut(R0 + 5720, TOK)
        TQ = cut(R0 + 6240, NC_, 8, 4)
        SM = cut(R0 + 6368, 7, 16)
        TAIL = cut(R0 + 6480, 6, 27)
        STAIL = cut(R0 + 6642, 2, 18)
        SO = cut(R0 + 6678, 2, DH)
        NS = cut(R0 + 6806, 2, NB)
        NSO = cut(R0 + 6822, 2, NB + 1)
        EA, SMZ = cut(R0 + 6840, 1)[0:4], cut(R0 + 6841, 1)
        TN, TH, RS = cut(R0, 2, TOK), cut(R0 + 1040, 2, TOK), cut(R0 + 2080, TOK)
        YO = Y
        ri, rf, ra, rb, fa, aa, _, gg = (GB[0:4, i, :] for i in range(8))
        t1, t2, t3, t4, t5 = (cut(4608 + TOK * i, TOK)[0:4] for i in range(5))
        CB = GA[:, 0:6 * CW].rearrange("p (j w) -> p j w", j=6)
        GZ = GA[:, 6 * CW:].rearrange("p (j w) -> p j w", j=2)
        CY = cut(R0, 6, CV)
        LS = cut(R0, 4, TOK)
        AT, XM, XT, YS = (cut(R0 + 1024 * i, 2, NC_, P) for i in range(4))
        EB = cut(R0 + 3072, 2, NC_, P)
        yflat = Y[:].rearrange("p k t -> p (k t)")

        def ycut(o, *shape):
            n = int(np.prod(shape))
            names = "abcde"[:len(shape)]
            return yflat[:, o:o + n].rearrange(f"p ({' '.join(names)}) -> p {' '.join(names)}",
                                               **{x: w for x, w in zip(names[1:], shape[1:])})
        CT = ycut(0, 2, NC_, P)
        BK, BV = ycut(1040, NC_, 256), ycut(2064, NC_, 256)
        U = ycut(3120, NC_, 256)
        VN = cut(R0, NC_, 256)
        QE = cut(R0 + 1024, 2, NC_, P)
        OG = cut(R0 + 2048, 2, TOK)
        SQG = EGB = cut(R0 + 3088, 2, TOK)
        WI, EMN, OM = cut(R0, 2, TOK), cut(R0 + 1040, 2, TOK), cut(R0 + 2080, 2, TOK)
        DA = Y[:, 4:6, :]
        EM = ycut(3120, 2, NC_, P)
        GG, EG, QI = Y[:, 4:6, :], Y[:, 6:8, :], GB[:, 6:8, :]
        KI = [cut(R0 + 1024 * i, 2, NC_, P) for i in range(NSUB)]
        OL, SQL = cut(R0, 2, TOK), cut(R0 + 1040, 2, TOK)
        LA = GA[:, 0:8 * TOK].rearrange("p (j w) -> p j w", j=8)
        SD, DX = cut(5632, 2, NB, DH), cut(6656, 2, NB, DH)
        SCB = cut(R0, 2, SW)
        SCY = cut(R0 + 2 * SW, 2, SV)

        def halves(ap):
            return ap.rearrange("p (a b) -> p a b", a=2)

        def slot(i):
            return PS[:, 2 * i:2 * i + 2, 0:HALF]

        M = [PS[:, 4 + i, :] for i in range(4)]
        DOWN_SLOT = [0, 3, 1, 2, 1, 2, 0, 3]

        def kind_of(u):
            if u < ZU + OU:
                return KT
            return KT if (u - ZU - OU) % EU < 2 * GF else GF

        UB = [0, UNITS[0]]
        E0 = UB[1] + ZU + OU

        def raw_e(i):
            j = i % RAW_E
            return ((E0 + j) % RAW, Wraw[:, (E0 + j) % RAW, :]) if j < RAW else (j, Wraw3[:, j - RAW, :])

        def raw_loads(it, i):
            j = i % RAW_E
            return it * (EU // RAW_E) + (i // RAW_E + ((E0 + j) // RAW + 1 if j < RAW else 1))

        def split_e(i):
            j = i % SPLIT_E
            return (Whi[:, (E0 + j) % SPLIT, :], Wlo[:, (E0 + j) % SPLIT, :]) if j < SPLIT else (Whi3, Wlo3)
        LAST = sum(UNITS)

        ORDER = (["rnm", ("z", 0), ("z", 1), ("rows", 0), ("z", 2), ("rows", 1), ("z", 3), ("conv", 0), ("z", 4),
                  ("rows", 2), ("conv", 1), ("z", 5), ("conv", 2), ("conv", 3), ("z", 6), ("conv", 4), ("conv", 5),
                  ("z", 7), "tq", ("z", 8), "tails", ("z", 9), "l2q", ("z", 10), "l2", "gtok", ("z", 11),
                  ("glog", 0), ("z", 12), ("glog", 1), ("z", 13), ("inv", 0), ("uw", 0), ("glog", 2), ("z", 14),
                  ("glog", 3), ("z", 15), ("inv", 1), ("uw", 1), "qe", ("z", 16), "gst", "gout", "gd", ("hn", 0),
                  "mbc", ("z", 17), "mtok", ("gate", 1), ("z", 18), "mst", ("z", 19), "mlog", ("z", 20), "mout",
                  ("z", 21), "md", ("z", 22), ("hn", 1), ("z", 23), ("z", 24),
                  "lg", ("z", 25), "lk", "ltok", ("z", 26), "lst", ("gate", 2), "lsub", ("z", 27), "llog", ("z", 28),
                  "lout", ("z", 29), "ld", ("z", 30), ("hn", 2), "sc", "ysp"] + [("o", m) for m in range(OU)] +
                 ["rnf"])

        DENSE = 2

        block = ctx.enter_context(nc.Block())

        @block.sync
        def _(sp):
            for k in range(KT):
                sp.dma_start(X[:, k, :], A["xT"][k]).then_inc(sem["load_x"], 16)

            def load(u, k, src):
                if not isinstance(u, int) or u >= RAW:
                    sp.wait_ge(sem["w_lo"], u - RAW + 1)
                return sp.dma_start(Wraw[:, k[1], 0:k[0] * P], src).then_inc(sem[f"w_raw{k[1]}"], 16)

            for l in range(LAYERS):
                for i in range(ZU):
                    load(UB[l] + i, (KT, (UB[l] + i) % RAW), A["wz"][l, i])
                for i in range(OU):
                    u = UB[l] + ZU + i
                    load(u, (KT, u % RAW), A["wo"][l, i])
                base = UB[l] + ZU + OU

                def group(e, g):
                    for i in range(2 * GF):
                        load(e * EU + (base + i), (KT, (base + i) % RAW), A["wgu"][bass.ds(g, 1), i, :, :]
                             .rearrange("g p n -> (g p) n") if not isinstance(g, int) else A["wgu"][g, i])
                    for i in range(KT):
                        j = base + 2 * GF + i
                        load(e * EU + j, (GF, j % RAW), A["wd"][bass.ds(g, 1), i, :, :]
                             .rearrange("g p n -> (g p) n") if not isinstance(g, int) else A["wd"][g, i])

                if l == 0:
                    with sp.Fori(0, DENSE) as e:
                        group(e, e)
                else:
                    def load_e(it, i, src):
                        if isinstance(it, int) and i < RAW_E:
                            if i < RAW:
                                sp.wait_ge(sem["w_lo"], E0 + i - RAW + 1)
                            elif i == RAW:
                                sp.wait_ge(sem["ht_p"], 5)
                        else:
                            sp.wait_ge(sem["w_lo"], it * EU + (E0 + i - RAW_E + 1))
                        place, dst = raw_e(i)
                        k = KT if i < 2 * GF else GF
                        sp.dma_start(dst[:, 0:k * P], src).then_inc(sem[f"w_raw{place}"], 16)

                    for i in range(EU):
                        load_e(0, i, A["wgu"][DENSE, i] if i < 2 * GF else A["wd"][DENSE, i - 2 * GF])
                    sp.wait_ge(sem["turns_v"], 1)
                    final = sp.value_load(NI[0:1, 0:1], min_val=EXPERTS - 1, max_val=EXPERTS * ROUNDS - 1)
                    with sp.Fori(1, final + 1) as it:
                        g = bass.ds(it % EXPERTS + DENSE, 1)
                        for i in range(EU):
                            src = A["wgu"][g, i, :, :] if i < 2 * GF else A["wd"][g, i - 2 * GF, :, :]
                            load_e(it, i, src.rearrange("g p n -> (g p) n"))
                    for i in range(SPLIT):
                        load_e(final + 1, i, A["wgu"][DENSE, i])
            for k in range(KT):
                sp.wait_ge(sem["h_f"], 8 * 4 + k + 1)
                sp.dma_start(O["y"][k], YO[:, k, :]).then_inc(sem["y_stored"], 16)
            sp.wait_ge(sem["y_stored"], 16 * KT)

        @block.gpsimd
        def _(pool):
            pool.dma_start(con[:, :], A["con"]).then_inc(sem["load_con"], 16)
            stored = [0]

            def store(dst, src):
                pool.dma_start(dst, src).then_inc(sem["stored"], 16)
                stored[0] += 16

            def coupling(l, hp):
                W(pool, "at_v", l, 2 * hp + 2)
                for v in range(1, 7):
                    for h in range(2):
                        if v == 1:
                            W(pool, "xt0_v", l, hp + 1)
                        else:
                            W(pool, "y_p", l, 12 * hp + 2 * (v - 2) + h + 1)
                        inc(pool.tensor_tensor(CT[:, h, :, :], AT[:, h, :, :],
                                               lvl[:, v:v + 1, :].broadcast_to([P, NC_, P]), ALU.mult), "ct_g")

            def state_in(l, i, name):
                W(pool, "out_p", l, 2 * (i + 1))
                if i:
                    W(pool, "hn_v", l, 3 * i)
                pool.dma_start(SD, A[name][l]).then_inc(sem["state_d"], 16)

            def state_out(l, i, name):
                W(pool, "so_a", l, 2 * (i + 1))
                store(O[name + "_p"][l], SO)
                W(pool, "dec_v", l, i + 1)
                store(O[name + "_s"][l], SD)
                pool.wait_ge(sem["stored"], stored[0])
                inc(pool.memset(SMZ, 0.0), "so_g")

            for l in range(LAYERS):
                if l:
                    pool.wait_ge(sem["down_v"], KT * DENSE)
                pool.dma_start(par[:, :], A["par"][l]).then_inc(sem["load_par"], 16)
                inc(pool.memset(S[:, 0:4608], 0.0), "zero_g")
                inc(pool.memset(S[:, R0 + 4160:R0 + 5720], 0.0), "zero_g")
                inc(pool.memset(CB[:, :, 0:KCH - 1], 0.0), "zero_g")
                inc(pool.memset(CB[:, :, CW - 1:CW], 0.0), "zero_g")
                for j in range(6):
                    pool.dma_start(CB[:, j, T + KCH - 1:CW - 1].rearrange("p (b w) -> p b w", w=KCH)[:, :, 0:KCH - 1],
                                   A["gconv"][l, j]).then_inc(sem["hist_d"], 16)
                W(pool, "rows_v", l)
                store(O["mm"][l], RM[0:4, :])
                W(pool, "tail_a", l, 2)
                store(O["gtail"][l], TAIL)
                pool.wait_ge(sem["load_con"], 16)
                coupling(l, 0)
                coupling(l, 1)
                state_in(l, 0, "gS")
                state_out(l, 0, "gS")
                W(pool, "gst_p", l)
                inc(pool.memset(ST[:, :, :, 1, :], 0.0), "kind_g")
                state_in(l, 1, "mC")
                W(pool, "out_p", l, 4)
                pool.dma_start(NS, A["mn"][l]).then_inc(sem["state_d"], 16)
                state_out(l, 1, "mC")
                W(pool, "nso_a", l)
                store(O["mn"][l], NSO)
                W(pool, "ltok_p", l)
                for i in range(NSUB - 1):
                    last = pool.memset(KI[i][:, :, :, (i + 1) * SUB:], 0.0)
                inc(last, "ki0_g")
                state_in(l, 2, "lS")
                state_out(l, 2, "lS")
                W(pool, "hn_v", l, 9)
                inc(pool.memset(SCB[:, :, 0:KSC - 1], 0.0), "spad_g")
                inc(pool.memset(SCB[:, :, SW - 1:SW], 0.0), "spad_g")
                for j in range(2):
                    pool.dma_start(SCB[:, j, T + KSC - 1:SW - 1].rearrange("p (b w) -> p b w", w=KSC)[:, :, 0:KSC - 1],
                                   A["sconv"][l, j]).then_inc(sem["shist_d"], 16)
                W(pool, "stail_a", l)
                store(O["stail"][l], STAIL)
                pool.wait_ge(sem["stored"], stored[0])
                inc(pool.memset(SMZ, 0.0), "stored_g")
            pool.wait_ge(sem["stored"], stored[0])
        @block.tensor
        def _(pe):
            def mm(out, lhsT, rhs, start=True, stop=True):
                return pe.matmul(out, lhsT, rhs, start=start, stop=stop, skip_group_check=True)

            def unit(s, banks, k, hi, lo, last_tile=None, fresh=None):
                for j in range(k):
                    if last_tile is not None and j == k - 1:
                        pe.wait_ge(sem["glu_v"], last_tile)
                    if fresh is not None:
                        pe.wait_ge(sem["h_lo"], fresh + j + 1)
                    for h in range(2):
                        out, t = banks[:, h, :], slice(h * HALF, (h + 1) * HALF)
                        w = slice(j * P, (j + 1) * P)
                        mm(out, Whi[:, s, w], hi[:, j, t], j == 0, False)
                        mm(out, Whi[:, s, w], lo[:, j, t], False, False)
                        last = mm(out, Wlo[:, s, w], hi[:, j, t], False, j == k - 1)
                return last

            def z(l, u):
                if u == 0 and l:
                    pe.wait_ge(sem["down_v"], KT * DENSE)
                if u >= 2:
                    W(pe, "z_evac", l, u - 1)
                g = UB[l] + u
                pe.wait_ge(sem["w_lo"], g + 1)
                inc(unit(g % SPLIT, slot(u % 2), KT, Hhi, Hlo, fresh=None if u else l * 24), "unit_done")

            def o(l, m):
                if m == 0:
                    W(pe, "z_evac", l)
                if m >= 2:
                    W(pe, "wo_add", l, m - 1)
                g = UB[l] + ZU + m
                pe.wait_ge(sem["w_lo"], g + 1)
                inc(unit(g % SPLIT, slot(m % 2), KT, Hhi, Hlo, fresh=None if m else l * 24 + 8), "unit_done")

            def rn(l, n):
                for k in range(KT):
                    pe.wait_ge(sem["sq_a"], n * KT + k + 1)
                    for h in range(2):
                        last = mm(M[h][:, 0:HALF], ones, TN[:, k % 2, h * HALF:(h + 1) * HALF], k == 0, k == KT - 1)
                    inc(last, "ssq_p")

            def tq(l):
                W(pe, "rows_v", l)
                W(pe, "rex_a", l)
                for i, q in enumerate((QA, QB)):
                    for c in range(NC_):
                        last = pe.transpose(M[i][:, c * P:(c + 1) * P], q[:, c * C:(c + 1) * C], ident)
                    inc(last, "tq_p")

            def pair_bc(lo, hi_, rows, at, name):
                for hp in range(2):
                    for h in range(2):
                        last = mm(M[2 * hp + h][:, 0:HALF], ehp[lo:hi_, hp, :], rows[lo:hi_, h * HALF:(h + 1) * HALF])
                inc(last, name)

            def head_sums(src, name):
                for j in range(2):
                    for h in range(2):
                        last = mm(M[2 * j + h][:, 0:HALF], bones, src[:, j, h * HALF:(h + 1) * HALF])
                inc(last, name)

            def l2(l):
                for i in range(2):
                    W(pe, "sq2_a", l, i + 1)
                    if i:
                        W(pe, "ln2_a", l, i)
                    else:
                        W(pe, "tq_a", l)
                    head_sums(LS[:, 2 * i:2 * i + 2, :], "l2_p")

            def tok(l, keys, values, name, free):
                for c in range(NC_):
                    for i, src in enumerate((keys[0], keys[1], values[0], values[1])):
                        last = pe.transpose(M[c][:, i * P:(i + 1) * P], src[:, c * C:(c + 1) * C], ident)
                    inc(last, name)

            def gtok(l):
                W(pe, "l2_v", l)
                W(pe, "silu_a", l)
                tok(l, (CB[:, 2, :], CB[:, 3, :]), (CB[:, 4, :], CB[:, 5, :]), "gtok_p", None)

            def glog(l, head):
                hp, h = head // 2, head % 2
                if head == 0:
                    W(pe, "gtok_v", l)
                elif head == 2:
                    W(pe, "uw_v", l, 3)
                else:
                    W(pe, "at_v", l, head)
                rows = slice(DH * h, DH * h + DH)
                mm(M[0], sel[64:68, head, :], QB[64:68, 0:T])
                mm(M[3], sel[0:4, head, :], QB[0:4, 0:T])
                for c in range(NC_):
                    t = slice(c * C, (c + 1) * C)
                    mm(M[1][:, t], CB[rows, 2 + hp, t], CB[rows, 2 + hp, t])
                    last = mm(M[2][:, t], CB[rows, 2 + hp, t], CB[rows, hp, t])
                inc(last, "glog_p")

            def inv(l, hp):
                W(pe, "xt0_v", l, hp + 1)
                W(pe, "at_v", l, 2 * hp + 2)
                for h in range(2):
                    for c in range(NC_):
                        last = pe.transpose(M[h][:, c * P:(c + 1) * P], XT[:, h, c, :], ident)
                    inc(last, "xtr_p")
                for v in range(1, 7):
                    n = 12 * hp + 2 * (v - 1)
                    for h in range(2):
                        W(pe, "ct_g", l, n + h + 1)
                        if v == 1:
                            W(pe, "xm_a", l, 2 * hp + h + 1)
                        else:
                            W(pe, "xu_v", l, 10 * hp + 2 * (v - 2) + h + 1)
                            W(pe, "xtu_v", l, n - 2 + h + 1)
                        for c in range(NC_):
                            last = mm(M[h][:, c * P:(c + 1) * P], CT[:, h, c, :], XM[:, h, c, :])
                        inc(last, "y_p")
                    if v < 6:
                        for h in range(2):
                            W(pe, "ys_a", l, n + h + 1)
                            for c in range(NC_):
                                last = mm(M[2 + h][:, c * P:(c + 1) * P], XT[:, h, c, :], YS[:, h, c, :])
                            inc(last, "z_p")
                    for h in range(2):
                        W(pe, "ys_a", l, n + h + 1)
                        for c in range(NC_):
                            last = mm(M[h][:, c * P:(c + 1) * P], YS[:, h, c, :], XT[:, h, c, :])
                        inc(last, "zt_p")

            def uw(l, hp):
                W(pe, "xtu_v", l, 12 * hp + 12)
                for h in range(2):
                    for c in range(NC_):
                        a = hp * P + h * DH
                        mm(M[0][:, (h * NC_ + c) * DH:(h * NC_ + c + 1) * DH], XT[:, h, c, :], BV[:, c, a:a + DH])
                        last = mm(M[1 + h][:, c * P:(c + 1) * P], BK[:, c, hp * P:(hp + 1) * P], XT[:, h, c, :])
                inc(last, "uw_p")

            def qe(l):
                W(pe, "uw_v", l)
                pair_bc(96, 100, QB, None, "qe_p")

            def gst(l):
                W(pe, "qe_v", l)
                for c in range(NC_):
                    if c:
                        W(pe, "st_v", l, 4 * c)
                        for hp in range(2):
                            last = mm(M[0][:, hp * P:(hp + 1) * P], ST[:, c, hp, 1, :], ST[:, c, hp, 0, :])
                        inc(last, "gst_p")
                    W(pe, "vn_v", l, c + 1)
                    for hp in range(2):
                        last = mm(M[1][:, hp * P:(hp + 1) * P], KD[:, c, hp * P:(hp + 1) * P],
                                  VN[:, c, hp * P:(hp + 1) * P])
                    inc(last, "gsd_p")

            def outs(l, i, q):
                W(pe, "st_v", l, 16 * (i + 1))
                W(pe, "vp_a", l, 8 * (i + 1))
                for hp in range(2):
                    for c in range(NC_):
                        t = slice(c * P, (c + 1) * P)
                        mm(M[hp][:, t], ST[:, c, hp, 0, :], q[:, hp, t], True, False)
                        for h in range(2):
                            last = mm(M[hp][:, t], VP[:, c, 2 * hp + h, :], PM[:, 2 * hp + h, c, :], False, h == 1)
                    if i == 1:
                        for c in range(NC_):
                            t = slice(c * P, (c + 1) * P)
                            mm(M[2 + hp][:, t], ST[:, c, hp, 1, :], q[:, hp, t], True, False)
                            for h in range(2):
                                last = mm(M[2 + hp][:, t], onesh[h], PM[:, 2 * hp + h, c, :], False, h == 1)
                    inc(last, "out_p")

            def dx(l, n):
                W(pe, "dx_v", l, n)
                for hp in range(2):
                    last = mm(M[hp], bones, DX[:, hp, :, :].rearrange("p b e -> p (b e)"))
                inc(last, "dx_p")

            def gd(l):
                W(pe, "o_a", l, 2)
                for hp in range(2):
                    last = mm(M[2][:, hp * NB:(hp + 1) * NB], ehp[0:4, hp, :], QB[0:4, T:TOK])
                inc(last, "beta_p")
                for n in range(3):
                    dx(l, n + 1)

            def hn(l, i):
                W(pe, "hsq_a", l, i + 1)
                W(pe, "dec_v", l, i + 1)
                head_sums((SQG, DA, SQL)[i], "hn_p")

            def mbc(l):
                W(pe, "hrs_a", l, 1)
                pair_bc(32, 36, RA, None, "mbc_p")
                W(pe, "mbc_a", l, 1)
                pair_bc(64, 68, RA, None, "mbc_p")
                W(pe, "mbc_a", l, 2)
                for hp in range(2):
                    last = mm(M[0][:, hp * NB:(hp + 1) * NB], ehp[32:36, hp, :], QA[32:36, T:TOK])
                inc(last, "mbc_p")

            def mtok(l):
                W(pe, "mbc_a", l)
                W(pe, "z_evac", l, 15)
                tok(l, (GB[:, 2, :], GB[:, 3, :]), (GB[:, 4, :], GB[:, 5, :]), "mtok_p", None)

            def updates(l, i):
                for c in range(NC_):
                    W(pe, ("", "mkd_v", "lkd_a")[i], l, c + 1)
                    W(pe, "vp_a", l, 8 * i + 2 * c + 2)
                    for hp in range(2):
                        k = KD[:, c, hp * P:(hp + 1) * P]
                        a = hp * 256 if i == 1 else hp * P
                        mm(M[c][:, a:a + P], k, VP[:, c, 2 * hp, :], True, False)
                        last = mm(M[c][:, a:a + P], k, VP[:, c, 2 * hp + 1, :], False, True)
                        if i == 1:
                            last = mm(M[c][:, a + P:a + 2 * P], k, ones)
                    inc(last, "up_p")

            def mlog(l):
                W(pe, "st_v", l, 32)
                for head in range(HEADS):
                    hp, h = head // 2, head % 2
                    rows = slice(DH * h, DH * h + DH)
                    if head >= 2:
                        W(pe, "mpm_v", l, head - 1)
                    a = 2 * (head % 2)
                    mm(M[a], sel[0:4, head, :], RA[0:4, 0:T])
                    for c in range(NC_):
                        t = slice(c * C, (c + 1) * C)
                        last = mm(M[a + 1][:, t], GB[rows, 2 + hp, t], GB[rows, hp, t])
                    inc(last, "mlog_p")

            def mout(l):
                W(pe, "mpm_v", l)
                W(pe, "qw_v", l)
                outs(l, 1, GB)

            def md(l):
                W(pe, "mo_v", l)
                dx(l, 4)
                W(pe, "nq_v", l)
                inc(mm(M[2][:, 0:2 * NB], bones, SM[:, 3, :]), "nq_p")
                dx(l, 5)

            def lg(l):
                W(pe, "hrs_a", l, 2)
                for hp in range(2):
                    for h in range(2):
                        a = PAR["wgate"][0] + hp * P
                        last = mm(M[2 * hp + h][:, 0:HALF], par[96:128, a:a + P], RA[96:128, h * HALF:(h + 1) * HALF])
                inc(last, "lg_p")

            def ltok(l):
                W(pe, "lke_v", l)
                W(pe, "z_evac", l, 23)
                tok(l, (KI[0][:, 0, :, :].rearrange("p c t -> p (c t)"), KI[0][:, 1, :, :].rearrange("p c t -> p (c t)")),
                    (LA[:, 4, :], LA[:, 5, :]), "ltok_p", None)

            def llog(l):
                W(pe, "ki_v", l)
                W(pe, "ki0_g", l)
                W(pe, "st_v", l, 48)
                for head in range(HEADS):
                    hp, h = head // 2, head % 2
                    rows = slice(DH * h, DH * h + DH)
                    for c in range(NC_):
                        for i in range(NSUB):
                            t = slice(c * C + i * SUB, c * C + (i + 1) * SUB)
                            last = mm(M[head][:, t], KI[i][rows, hp, c, :], QI[rows, hp, t])
                    inc(last, "llog_p")

            def lout(l):
                W(pe, "lpm_v", l)
                W(pe, "lqe_v", l)
                outs(l, 2, LA)

            def ld(l):
                W(pe, "o_a", l, 4)
                dx(l, 6)
                dx(l, 7)

            def router():
                pe.wait_ge(sem["h_lo"], 48)
                pe.wait_ge(sem["rwlo_v"], 1)
                for i in range(5):
                    n = P if i < 4 else NB
                    t = slice(i * P, i * P + n)
                    for k in range(KT):
                        w = slice(k * 8, k * 8 + 8)
                        out = M[0][0:n, i * 8:i * 8 + 8]
                        mm(out, Hhi[:, k, t], RWhi[:, w], k == 0, False)
                        mm(out, Hlo[:, k, t], RWhi[:, w], False, False)
                        last = mm(out, Hhi[:, k, t], RWlo[:, w], False, k == KT - 1)
                inc(last, "rt_p")
                W(pe, "wo_add", 1)
                for i in range(5):
                    n = P if i < 4 else NB
                    if i == 1:
                        pe.wait_ge(sem["hth_a"], 1)
                        pe.wait_ge(sem["htl_v"], 1)
                    elif i:
                        pe.wait_ge(sem["hth_a"], i)
                        pe.wait_ge(sem["htl_v"], i)
                    for part, h in ((0, Hhi), (1, Hlo)):
                        for k in range(KT):
                            last = pe.transpose(PS[0:n, 2 * part + k // 4, (k % 4) * P:(k % 4) * P + P],
                                                h[:, k, i * P:i * P + n].bitcast(F32), ident)
                    inc(last, "ht_p")
                pe.wait_ge(sem["sel_v"], 1)
                for i in range(5):
                    for j in range(i):
                        mm(M[1][:, i * 8:i * 8 + 8], ones, RTK[:, 2, j, :], j == 0, False)
                    mm(M[1][:, i * 8:i * 8 + 8], tri, RTK[:, 2, i, :], i == 0, True)
                for i in range(5):
                    last = mm(M[2][0:1, 0:8], ones[:, 0:1], RTK[:, 2, i, :], i == 0, i == 4)
                inc(last, "rt_p")
                pe.wait_ge(sem["key_v"], 2)
                for i in range(5):
                    n = P if i < 4 else NB
                    out = M[3][0:8, i * P:i * P + n] if i < 4 else M[2][0:8, 0:NB]
                    last = pe.transpose(out, KEY[0:n, i, :], ident[0:n, 0:n])
                inc(last, "rt_p")

            pe.wait_ge(sem["load_con"], 16)
            STEPS = dict(tq=tq, l2=l2, gtok=gtok, glog=glog, inv=inv, uw=uw, qe=qe, gst=gst, gd=gd, hn=hn,
                         mbc=mbc, mtok=mtok, mlog=mlog, mout=mout, md=md, lg=lg, ltok=ltok, llog=llog,
                         lout=lout, ld=ld)

            for l in range(LAYERS):
                for step in ORDER:
                    name, arg = step if isinstance(step, tuple) else (step, None)
                    if name == "z":
                        z(l, arg)
                    elif name == "o":
                        o(l, arg)
                    elif name == "rnm":
                        rn(l, 2 * l)
                    elif name == "rnf":
                        rn(l, 2 * l + 1)
                    elif name == "gout":
                        W(pe, "pm_v", l)
                        outs(l, 0, QE.rearrange("p h c t -> p h (c t)"))
                    elif name == "mst":
                        updates(l, 1)
                    elif name == "lst":
                        updates(l, 2)
                    elif name in STEPS:
                        STEPS[name](l) if arg is None else STEPS[name](l, arg)
                if l == 1:
                    break
                base = ZU + OU
                W(pe, "wo_add", l)

                def group(e, first):
                    for f in range(GF):
                        if f >= 2:
                            pe.wait_ge(sem["glu_v"], e * GF + (f - 1))
                        elif not first:
                            pe.wait_ge(sem["down_v"], e * KT + (2 * f - 2))
                        for j in range(2):
                            i = 2 * f + j
                            pe.wait_ge(sem["w_lo"], e * EU + (base + i + 1))
                            s = slot((1 - f % 2) if j == 0 else (2 + f % 2))
                            inc(unit((base + i) % SPLIT, s, KT, Hhi, Hlo, fresh=16 if first and i == 0 else None), "unit_done")
                    for m in range(KT):
                        pe.wait_ge(sem["w_lo"], e * EU + (base + 2 * GF + m + 1))
                        if m == 0:
                            pe.wait_ge(sem["glu_v"], e * GF + (GF - 1))
                        elif m >= 4:
                            pe.wait_ge(sem["down_v"], e * KT + (3, 4, 4, 4)[m - 4])
                        inc(unit((base + 2 * GF + m) % SPLIT, slot(DOWN_SLOT[m]), GF, Ahi, Alo,
                                 e * GF + GF if m == 0 else None), "unit_done")

                group(0, True)
                before = dict(count)
                with pe.Fori(1, DENSE) as e:
                    group(e, False)
                looped(before, DENSE - 1)

            router()
            base = UB[1] + ZU + OU

            def narrow(i, out, k, hi, lo, last_tile=None):
                whi, wlo = split_e(i)
                for j in range(k):
                    if last_tile is not None and j == k - 1:
                        pe.wait_ge(sem["sglu_v"], last_tile)
                    w = slice(j * P, (j + 1) * P)
                    mm(out, whi[:, w], hi[:, j, :], j == 0, False)
                    mm(out, whi[:, w], lo[:, j, :], False, False)
                    last = mm(out, wlo[:, w], hi[:, j, :], False, j == k - 1)
                return last

            def gather(it):
                pe.wait_ge(sem["selg_v"], it + 1)
                for k in range(KT):
                    if k >= 2:
                        pe.wait_ge(sem["hgh_a"], it * KT + (k - 1))
                        pe.wait_ge(sem["hgl_v"], it * KT + (k - 1))
                    for part, h in ((0, HTh), (1, HTl)):
                        for i in range(5):
                            n = P if i < 4 else NB
                            last = mm(PS[:, 2 * (k % 2) + part, 0:CAP], h[0:n, i, k * P:(k + 1) * P], SelG[0:n, i, :],
                                      i == 0, i == 4)
                    inc(last, "hg_p")

            def scatter(it, tiles_):
                for m in tiles_:
                    if m == 0:
                        pe.wait_ge(sem["ylo_v"], it * 2 + 2)
                        pe.wait_ge(sem["selt_v"], it * 2 + 2)
                    elif m >= 2:
                        pe.wait_ge(sem["xadd_v"], it * KT + (m - 1))
                    for h in range(2):
                        for st, n in SLOTS:
                            for part, y in ((0, Yhi), (1, Ylo)):
                                last = mm(PS[:, 4 + 2 * (m % 2) + h, 0:HALF], y[0:n, st, m * P:(m + 1) * P],
                                          SelT[0:n, st, h * HALF:(h + 1) * HALF], st == 0 and part == 0,
                                          st == 1 and part == 1)
                    inc(last, "sc_p")

            def turn(it, before=None):
                for f in range(GF):
                    if f == 0:
                        pe.wait_ge(sem["hgh_a"], it * KT + KT)
                        pe.wait_ge(sem["hgl_v"], it * KT + KT)
                    if f >= 2:
                        pe.wait_ge(sem["sglu_v"], it * GF + (f - 1))
                    for j in range(2):
                        i = 2 * f + j
                        pe.wait_ge(sem["w_lo"], it * EU + (base + i + 1))
                        inc(narrow(i, PS[:, 2 * j + f % 2, 0:CAP], KT, Hgh, Hgl), "unit_done")
                    if before is not None and 2 <= f < 6:
                        scatter(before, range(2 * f - 4, 2 * f - 2))
                    if f == 6:
                        pe.wait_ge(sem["ktm_v"], it + 1)
                        if before is not None:
                            pe.wait_ge(sem["xadd_v"], it * KT)
                        for h in range(2):
                            mm(PS[:, 4 + h, 0:HALF], ones[32:40, :], KTM[:, h * HALF:(h + 1) * HALF])
                        for st, n in SLOTS:
                            for t in range(5):
                                r = P if t < 4 else NB
                                last = mm(PS[0:n, 6, 2 * st:2 * st + 2], SelG[0:r, t, st * P:st * P + n],
                                          GE[0:r, t, :], t == 0, t == 4)
                        inc(last, "key_p")
                for m in range(KT):
                    if m == 2:
                        gather(it + 1)
                    pe.wait_ge(sem["w_lo"], it * EU + (base + 2 * GF + m + 1))
                    if m == 0:
                        pe.wait_ge(sem["selt_v"], it * 2 + 2)
                        pe.wait_ge(sem["sglu_v"], it * GF + (GF - 1))
                    elif m >= 2:
                        pe.wait_ge(sem["yt_a"], it * KT + (m - 1))
                    inc(narrow(2 * GF + m, PS[:, 4 + m % 2, 0:CAP], GF, Agh, Agl, it * GF + GF if m == 0 else None),
                        "unit_done")
                pe.wait_ge(sem["gc_v"], it + 1)
                pe.wait_ge(sem["yt_a"], it * KT + KT)
                for st, n in SLOTS:
                    for m in range(KT):
                        last = pe.transpose(PS[0:n, (6 if st == 0 else 4) + m // 4, (m % 4) * P:(m % 4) * P + P],
                                            YT[:, m, st * P:st * P + n], ident)
                    inc(last, "tr_p")

            pe.wait_ge(sem["turns_v"], 1)
            final = pe.value_load(NI[0:1, 0:1], min_val=EXPERTS - 1, max_val=EXPERTS * ROUNDS - 1)
            gather(0)
            turn(0)
            with pe.Fori(0, final) as before:
                turn(before + 1, before)
            scatter(final, range(KT))
            rn(LAYERS, 4)

        @block.scalar
        def _(act):
            def split(g, k, s, raw, value):
                act.wait_ge(sem[f"w_raw{raw}"], value)
                if not isinstance(g, int) or g >= SPLIT:
                    act.wait_ge(sem["unit_done"], g - SPLIT + 1)
                inc(act.activation(Whi[:, s, 0:k * P], Wraw[:, raw, 0:k * P], ACT.Copy), "w_hi")

            def split_at(g):
                if g < UB[1] + UNITS[1]:
                    l = int(g >= UB[1])
                    split(g, kind_of(g - UB[l]), g % SPLIT, g % RAW, 16 * (g // RAW + 1))

            def ex(out, in_, func, name="a_ord", **kw):
                return inc(act.activation(out, in_, func, **kw), name)

            def z(l, u):
                split_at(UB[l] + u + 2)
                act.wait_ge(sem["unit_done"], UB[l] + u + 1)
                ps = slot(u % 2)
                if u == 0:
                    if l:
                        act.wait_ge(sem["down_v"], KT * DENSE)
                    W(act, "zero_g", l, 4)
                    act.wait_ge(sem["load_par"], 16 * (l + 1))
                    act.activation(halves(ri), ps[0:4], ACT.Identity, bias=pr("gate_b", slice(0, 4)))
                    act.activation(halves(rf), ps[32:36], ACT.Identity, bias=pr("gate_b", slice(32, 36)))
                    act.activation(halves(ra), ps[64:68], ACT.Identity, bias=pr("gate_b", slice(64, 68)))
                    act.activation(halves(rb), ps[96:100], ACT.Copy)
                    ex(halves(RA[96:128, :]), ps[0:32], ACT.Copy, "z_evac")
                elif u < 7:
                    j = u - 1
                    act.activation(CB[:, j, 3:3 + HALF], ps[:, 0, :], ACT.Copy)
                    act.activation(CB[:, j, 3 + HALF:3 + T], ps[:, 1, 0:T - HALF], ACT.Copy)
                    ex(CB[:, j, T + KCH - 1:CW - 1].rearrange("p (b w) -> p b w", w=KCH)[:, :, KCH - 1],
                       ps[:, 1, T - HALF:HALF], ACT.Copy, "z_evac")
                elif u < 9:
                    ex(halves(GZ[:, u - 7, :]), ps, ACT.Copy, "z_evac")
                elif u < 17:
                    if u == 9:
                        W(act, "rows_v", l)
                        own(act, "rex_a")
                    ex(halves(GB[:, u - 9, :]), ps, ACT.Copy, "z_evac", scale=DH ** -0.5 if u in (11, 12) else 1.0)
                elif u < 25:
                    if u == 17:
                        W(act, "hn_v", l, 3)
                    ex(halves(LA[:, u - 17, :]), ps, ACT.Copy, "z_evac", scale=DH ** -0.5 if u < 19 else 1.0)
                else:
                    if u == 25:
                        W(act, "hn_v", l, 6)
                    ex(halves(GB[:, u - 25, :]), ps, ACT.Copy, "z_evac")

            def rn(l, n):
                if n == 0:
                    act.wait_ge(sem["load_x"], 16 * KT)
                elif n % 2:
                    W(act, "wo_add", l)
                elif n < 2 * LAYERS:
                    act.wait_ge(sem["down_v"], KT * DENSE)
                for k in range(KT):
                    if k >= 2:
                        act.wait_ge(sem["ssq_p"], n * KT + k - 1)
                    ex(TN[:, k % 2, :], X[:, k, :], ACT.Square, "sq_a")
                act.wait_ge(sem["ssq_p"], n * KT + KT)
                ex(halves(RS), PS[:, 4:6, 0:HALF], ACT.Ln, scale=1.0 / D, bias=EPSC)
                own(act, "a_ord")
                ex(RS, RS, ACT.Exp, "rs_a", scale=-0.5)
                if n < 2 * LAYERS:
                    for k in range(KT):
                        act.wait_ge(sem["h_f"], n * KT + k + 1)
                        if k == 0:
                            act.wait_ge(sem["unit_done"], UB[l] + (0 if n % 2 == 0 else ZU + OU))
                        ex(Hhi[:, k, :], TH[:, k % 2, :], ACT.Copy, "h_hi")

            def rows(l, part):
                if part == 1:
                    return
                if part == 2:
                    W(act, "rpre_v", l)
                    ex(RA[32:36, :], t1, ACT.Exp, "rex_a")
                    ex(RA[64:68, :], RM[0:4, :], ACT.Exp, "rex_a", scale=-1.0)
                    ex(QA[32:36, :], t3, ACT.Exp, "rex_a")
                    ex(QA[96:100, 0:T], t4[:, 0:T], ACT.Exp, "rex_a")
                    ex(t5, gg, ACT.Exp, "rex_a")
                    ex(QB[96:100, :], gg, ACT.Exp, "rex_a")
                    return
                own(act, "z_evac")
                ex(fa, rf, ACT.Abs)
                ex(aa, ra, ACT.Abs)
                own(act, "a_ord")
                ex(fa, fa, ACT.Exp, scale=-1.0)
                ex(aa, aa, ACT.Exp, scale=-1.0)
                ex(rb, rb, ACT.Exp, scale=-1.0)
                ex(EA, pr("a_log", slice(0, 4)), ACT.Exp)
                own(act, "a_ord")
                ex(fa, fa, ACT.Ln, "rsp_a", bias=cn("one", slice(0, 4)))
                ex(aa, aa, ACT.Ln, "rsp_a", bias=cn("one", slice(0, 4)))

            def tq(l):
                for i in range(2):
                    W(act, "tq_p", l, i + 1)
                    ex(TQ[:, :, 4 * i:4 * i + 4, :],
                       M[i].rearrange("p (c j h) -> p c j h", c=NC_, j=4)[:, :, :, 0:4], ACT.Copy, "tq_a")

            def tails(l):
                act.wait_ge(sem["hist_d"], 96 * (l + 1))
                own(act, "z_evac")
                ex(TAIL[:, :, 0:3], CB[:, :, T:T + 3], ACT.Copy, "tail_a")
                for j in range(6):
                    last = act.activation(TAIL[:, j, 3:27].rearrange("p (b w) -> p b w", w=3),
                                          CB[:, j, T + KCH - 1:CW - 1].rearrange("p (b w) -> p b w", w=KCH)[:, :, 1:4],
                                          ACT.Copy)
                inc(last, "tail_a")
                W(act, "conv_v", l)
                own(act, "tail_a")
                ex(CB[:, :, 0:T], CY[:, :, 0:T], ACT.Silu, "silu_a")
                ex(CB[:, :, T:TOK], CY[:, :, T + KCH - 1:CV:KCH], ACT.Silu, "silu_a")
                ex(GZ, GZ, ACT.Silu, "silu_a")

            def l2q(l):
                own(act, "silu_a")
                for i in range(2):
                    ex(LS[:, 2 * i:2 * i + 2, :], CB[:, 2 * i:2 * i + 2, 0:TOK], ACT.Square, "sq2_a")

            def l2(l):
                ls = [LS[:, 2 * i:2 * i + 2, :].rearrange("p j w -> p (j w)") for i in range(2)]
                for i in range(2):
                    W(act, "l2_p", l, i + 1)
                    ex(ls[i].rearrange("p (a b) -> p a b", a=4), PS[:, 4:8, 0:HALF], ACT.Ln, "ln2_a", bias=EPSC)
                own(act, "ln2_a")
                for i in range(2):
                    ex(ls[i], ls[i], ACT.Exp, "rs2_a", scale=-0.5, bias=LN8 if i == 0 else 0.0)

            def glog(l, head):
                W(act, "eb_v", l, head + 1)
                for c in range(NC_):
                    last = act.activation(EB[:, head % 2, c, :], EB[:, head % 2, c, :], ACT.Exp,
                                          bias=TQ[:, c, 2, head:head + 1])
                inc(last, "ebx_a")

            def inv(l, hp):
                for h in range(2):
                    W(act, "xtr_p", l, 2 * hp + h + 1)
                    ex(XM[:, h, :, :].rearrange("p c t -> p (c t)"), M[h], ACT.Copy, "xm_a")
                for v in range(1, 7):
                    n = 12 * hp + 2 * (v - 1)
                    for h in range(2):
                        W(act, "y_p", l, n + h + 1)
                        if v > 1:
                            W(act, "zt_p", l, n - 2 + h + 1)
                        ex(YS[:, h, :, :].rearrange("p c t -> p (c t)"), M[h], ACT.Copy, "ys_a")

            def qe(l):
                W(act, "qe_p", l)
                ex(EGB.rearrange("p j w -> p (j w)").rearrange("p (a b) -> p a b", a=4), PS[:, 4:8, 0:HALF],
                   ACT.Copy, "qe_a")

            def pad_values(l, c, src):
                vp = VP[:, c, :, :].rearrange("p (a b) e -> p a b e", b=2)
                for h in range(2):
                    ex(vp[:, :, h, h * DH:(h + 1) * DH], src[:, :, h, :], ACT.Copy, "vp_a")

            def state_out(l, i):
                W(act, "so_g", l, i)
                for h in range(2):
                    r = slice(h * DH, (h + 1) * DH)
                    ex(SO[r, :, :], ST[r, NC_, :, 0, h * DH:(h + 1) * DH], ACT.Copy, "so_a")

            def gst(l):
                for c in range(NC_):
                    W(act, "vn_v", l, c + 1)
                    pad_values(l, c, VN[:, c, :].rearrange("p (a b e) -> p a b e", a=2, b=2))
                W(act, "st_v", l, 16)
                state_out(l, 0)

            def outs(l, i, o_):
                for hp in range(2):
                    W(act, "out_p", l, 2 * i + hp + 1)
                    ex(o_[:, hp, 0:T], M[hp], ACT.Copy, "o_a")

            def hn(l, i):
                o_, sq = ((OG, SQG), (OM, DA), (OL, SQL))[i]
                W(act, "dec_v", l, i + 1)
                if i != 1:
                    own(act, "o_a")
                ex(sq, o_, ACT.Square, "hsq_a")
                W(act, "hn_p", l, i + 1)
                sf = sq.rearrange("p j w -> p (j w)") if i != 1 else yflat[:, 4 * TOK:6 * TOK]
                ex(sf.rearrange("p (a b) -> p a b", a=4), PS[:, 4:8, 0:HALF], ACT.Ln, scale=1.0 / DH, bias=EPSC)
                own(act, "a_ord")
                ex(sf, sf, ACT.Exp, "hrs_a", scale=-0.5)

            def gate(l, i):
                own(act, "z_evac")
                if i == 1:
                    ex(GB[:, 6:8, :], GB[:, 6:8, :], ACT.Sigmoid, "gate_a")
                else:
                    ex(LA[:, 6:8, :], LA[:, 6:8, :], ACT.Silu, "gate_a")

            def mbc(l):
                W(act, "hn_v", l, 3)
                for i, dst in enumerate((WI, EMN)):
                    W(act, "mbc_p", l, i + 1)
                    ex(dst.rearrange("p j w -> p (j w)").rearrange("p (a b) -> p a b", a=4), PS[:, 4:8, 0:HALF],
                       ACT.Copy, "mbc_a")
                W(act, "mbc_p", l, 3)
                ex(SM[:, 2, :], M[0][:, 0:2 * NB], ACT.Copy, "mbc_a")

            def mtok(l):
                for c in range(NC_):
                    W(act, "mtok_p", l, c + 1)
                    pad_values(l, c, M[c][:, 256:512].rearrange("p (a b e) -> p a b e", a=2, b=2))

            def mst(l):
                W(act, "st_v", l, 32)
                state_out(l, 1)
                if l:
                    act.wait_ge(sem["stored_g"], l)
                for h in range(2):
                    r = slice(h * DH, (h + 1) * DH)
                    ex(NSO[r, :, 0], ST[r, NC_, :, 1, h * DH], ACT.Copy, "nso_a")

            def mlog(l):
                for head in range(HEADS):
                    W(act, "em_v", l, head + 1)
                    for c in range(NC_):
                        last = act.activation(EM[:, head % 2, c, :], EM[:, head % 2, c, :], ACT.Exp,
                                              bias=TQ[:, c, 0, head:head + 1])
                    inc(last, "emx_a")

            def mout(l):
                W(act, "out_p", l, 4)
                ex(DA[:, :, 0:T], PS[:, 6:8, :], ACT.Abs, "da_a")

            def md(l):
                W(act, "nsn_v", l)
                ex(NSO[:, :, 1:9], NS, ACT.Copy, "nso_a")
                W(act, "nq_p", l)
                ex(SM[:, 5, :], M[2][:, 0:2 * NB], ACT.Abs, "nd_a")

            def lg(l):
                W(act, "lg_p", l)
                W(act, "hn_v", l, 6)
                for hp in range(2):
                    a = PAR["gla_b"][0] + hp
                    ex(halves(GG[:, hp, :]), PS[:, 4 + 2 * hp:6 + 2 * hp, 0:HALF], ACT.Identity, bias=par[:, a:a + 1])
                own(act, "a_ord")
                ex(EG, GG, ACT.Abs)
                own(act, "a_ord")
                ex(EG, EG, ACT.Exp, scale=-1.0)
                own(act, "a_ord")
                ex(EG, EG, ACT.Ln, "lsp_a", bias=cn("one"))
                W(act, "lcum_v", l)
                ex(GG, EG, ACT.Exp, "leg_a")

            def lk(l):
                for hp in range(2):
                    for c in range(NC_):
                        e = c * C + C - 1
                        last = act.activation(KI[0][:, hp, c, :], EG[:, hp, c * C:(c + 1) * C], ACT.Exp, scale=-1.0,
                                              bias=EG[:, hp, e:e + 1])
                inc(last, "lk_a")

            def ltok(l):
                for c in range(NC_):
                    W(act, "ltok_p", l, c + 1)
                    ex(KD[:, c, :], M[c][:, 0:256], ACT.Copy, "lkd_a")
                    pad_values(l, c, M[c][:, 256:512].rearrange("p (a b e) -> p a b e", a=2, b=2))

            def lst(l):
                W(act, "st_v", l, 48)
                state_out(l, 2)

            def lsub(l):
                W(act, "lsub_v", l, 1)
                ex(QI[:, :, 0:T], QI[:, :, 0:T], ACT.Exp, "lsub_a")
                for i in range(NSUB):
                    W(act, "lsub_v", l, i + 2)
                    k = KI[i][:, :, :, 0:(i + 1) * SUB]
                    ex(k, k, ACT.Exp, "lsub_a")

            def sc(l):
                W(act, "scu_v", l)
                act.wait_ge(sem["shist_d"], 32 * (l + 1))
                ex(STAIL[:, :, 0:2], SCB[:, :, T:T + 2], ACT.Copy, "stail_a")
                for j in range(2):
                    last = act.activation(STAIL[:, j, 2:18].rearrange("p (b w) -> p b w", w=2),
                                          SCB[:, j, T + KSC - 1:SW - 1].rearrange("p (b w) -> p b w", w=KSC)[:, :, 1:3],
                                          ACT.Copy)
                inc(last, "stail_a")

            def ysp(l):
                act.wait_ge(sem["unit_done"], UB[l] + ZU)
                W(act, "hn_v", l)
                W(act, "sc_v", l)
                for k in range(KT):
                    ex(Hhi[:, k, :], Y[:, k, :], ACT.Copy, "h_hi")

            def o(l, m):
                split_at(UB[l] + ZU + m + 2)

            def router():
                act.wait_ge(sem["down_v"], KT * DENSE)
                act.wait_ge(sem["stored_g"], 2)
                a, b = PAR["router"]
                ex(RWhi[:, :], par[:, a:b], ACT.Copy, "rexp_a")
                for i in range(5):
                    n = P if i < 4 else NB
                    act.wait_ge(sem["ht_p"], i + 1)
                    ex(HTh[0:n, i, :].rearrange("p (a b) -> p a b", a=2), PS[0:n, 0:2, :], ACT.Copy, "hth_a")
                    if i == 1:
                        act.wait_ge(sem["rl_v"], 1)
                        ex(RTK[:, 4, :, :], RTK[:, 4, :, :], ACT.Exp, "rexp_a")
                act.wait_ge(sem["rt_p"], 3)
                ex(KEYT[:, 0:T], M[3][0:8, :], ACT.Copy, "kt_a")
                act.wait_ge(sem["key_v"], 2)
                ex(KEYT[:, T:TOK], M[2][0:8, 0:NB], ACT.Copy, "kt_a")

            split_at(0)
            split_at(1)
            act.wait_ge(sem["load_con"], 16)
            STEPS = dict(rows=rows, tq=tq, tails=tails, l2q=l2q, l2=l2, gate=gate, glog=glog, inv=inv, qe=qe, gst=gst, hn=hn, mbc=mbc, mtok=mtok,
                         mst=mst, mlog=mlog, mout=mout, md=md, lg=lg, lk=lk, ltok=ltok, lst=lst, lsub=lsub,
                         sc=sc, ysp=ysp)

            for l in range(LAYERS):
                for step in ORDER:
                    name, arg = step if isinstance(step, tuple) else (step, None)
                    if name == "z":
                        z(l, arg)
                    elif name == "o":
                        o(l, arg)
                    elif name == "rnm":
                        rn(l, 2 * l)
                    elif name == "rnf":
                        rn(l, 2 * l + 1)
                    elif name == "gout":
                        outs(l, 0, OG)
                    elif name == "lout":
                        outs(l, 2, OL)
                    elif name in STEPS:
                        STEPS[name](l) if arg is None else STEPS[name](l, arg)
                if l == 1:
                    break
                base = ZU + OU
                act.wait_ge(sem["stored_g"], 1)

                def group(e, last):
                    def split_next(i):
                        if last and i + 2 >= EU:
                            split_at(base + e * EU + i + 2)
                            return
                        g = base + i + 2
                        k = GF if 2 * GF <= (i + 2) % EU else KT
                        split(e * EU + g, k, g % SPLIT, g % RAW, e * (16 * EU // RAW) + 16 * (g // RAW + 1))

                    for f in range(GF):
                        act.wait_ge(sem["unit_done"], e * EU + (base + 2 * f + 1))
                        split_next(2 * f)
                        ex(halves(SG[:, f % 2, :]), slot(1 - f % 2), ACT.Silu, "silu_g")
                        split_next(2 * f + 1)
                        act.wait_ge(sem["af_v"], e * GF + (f + 1))
                        ex(Ahi[:, f, :], AF[:, f % 2, :], ACT.Copy, "ahi_a")
                    for m in range(KT):
                        split_next(2 * GF + m)

                before = dict(count)
                with act.Fori(0, DENSE - 1) as e:
                    group(e, False)
                looped(before, DENSE - 1)
                group(DENSE - 1, True)

            router()
            base = UB[1] + ZU + OU

            def split_turn(it, i):
                i += 2
                n = (GF if 2 * GF <= i % EU else KT) * P
                place, raw = raw_e(i)
                act.wait_ge(sem[f"w_raw{place}"], 16 * raw_loads(it, i))
                act.wait_ge(sem["unit_done"], it * EU + (base + i - SPLIT_E + 1))
                inc(act.activation(split_e(i)[0][:, 0:n], raw[:, 0:n], ACT.Copy), "w_hi")

            def gathered(it):
                for k in range(KT):
                    act.wait_ge(sem["hg_p"], it * KT + (k + 1))
                    ex(Hgh[:, k, :], PS[:, 2 * (k % 2), 0:CAP], ACT.Copy, "hgh_a")

            def turn(it):
                for f in range(GF):
                    split_turn(it, 2 * f)
                    act.wait_ge(sem["unit_done"], it * EU + (base + 2 * f + 1))
                    ex(SGG[:, f % 2, :], PS[:, f % 2, 0:CAP], ACT.Silu, "ssilu_a")
                    split_turn(it, 2 * f + 1)
                    act.wait_ge(sem["saf_v"], it * GF + (f + 1))
                    ex(Agh[:, f, :], AFG[:, f % 2, :], ACT.Copy, "sahi_a")
                for m in range(KT):
                    if m == 2:
                        gathered(it + 1)
                    split_turn(it, 2 * GF + m)
                    act.wait_ge(sem["unit_done"], it * EU + (base + 2 * GF + m + 1))
                    ex(YT[:, m, :], PS[:, 4 + m % 2, 0:CAP], ACT.Copy, "yt_a")
                for st, n in SLOTS:
                    act.wait_ge(sem["tr_p"], it * 2 + (st + 1))
                    b = 6 if st == 0 else 4
                    ex(Yhi[0:n, st, :].rearrange("p (a b) -> p a b", a=2), PS[0:n, b:b + 2, :], ACT.Copy, "yhi_a",
                       scale=GC[0:n, st:st + 1])

            act.wait_ge(sem["turns_v"], 1)
            final = act.value_load(NI[0:1, 0:1], min_val=EXPERTS - 1, max_val=EXPERTS * ROUNDS - 1)
            gathered(0)
            with act.Fori(0, final + 1) as it:
                turn(it)
            act.wait_ge(sem["xadd_v"], final * KT + KT)
            rn(LAYERS, 4)

        @block.vector
        def _(dve):
            def split(g, k, s, raw):
                dve.wait_ge(sem["w_hi"], g + 1)
                inc(dve.tensor_tensor(Wlo[:, s, 0:k * P], Wraw[:, raw, 0:k * P], Whi[:, s, 0:k * P].bitcast(F32),
                                      ALU.subtract), "w_lo")

            def split_at(g):
                if g < UB[1] + UNITS[1]:
                    l = int(g >= UB[1])
                    split(g, kind_of(g - UB[l]), g % SPLIT, g % RAW)

            def tt(out, a, b, op, name="v_ord"):
                return inc(dve.tensor_tensor(out, a, b, op), name)

            def ts(out, a, s1, op, s2=None, op2=ALU.bypass, name="v_ord"):
                if s2 is None:
                    return inc(dve.tensor_scalar(out, a, s1, None, op), name)
                return inc(dve.tensor_scalar(out, a, s1, s2, op, op2), name)

            def stt(out, a, s1, b, op, op2, name="v_ord"):
                return inc(dve.scalar_tensor_tensor(out=out, in0=a, scalar=s1, in1=b, op0=op, op1=op2), name)

            def cp(out, a, name="v_ord"):
                return inc(dve.tensor_copy(out, a), name)

            def done():
                own(dve, "v_ord")

            def z(l, u):
                split_at(UB[l] + u + 2)

            def o(l, m):
                split_at(UB[l] + ZU + m + 2)
                dve.wait_ge(sem["unit_done"], UB[l] + ZU + m + 1)
                tt(halves(X[:, m, :]), slot(m % 2), halves(X[:, m, :]), ALU.add, "wo_add")

            def rn(l, n):
                dve.wait_ge(sem["rs_a"], n + 1)
                dve.wait_ge(sem["load_par"], 16 * min(l + 1, LAYERS))
                col = ("g_mix", "g_ffn")[n % 2] if n < 2 * LAYERS else "g_final"

                def low(k):
                    dve.wait_ge(sem["h_hi"], l * 24 + (0 if n % 2 == 0 else 16) + k + 1)
                    tt(Hlo[:, k, :], TH[:, k % 2, :], Hhi[:, k, :].bitcast(F32), ALU.subtract, "h_lo")

                for k in range(KT):
                    a = PAR[col][0] + k
                    if n == 2 * LAYERS:
                        dst = YO[:, k, :]
                    else:
                        dst = TH[:, k % 2, :]
                        if k >= 2:
                            low(k - 2)
                            own(dve, "h_lo")
                    stt(dst, X[:, k, :], par[:, a:a + 1], RS, ALU.mult, ALU.mult, "h_f")
                if n < 2 * LAYERS:
                    low(KT - 2)
                    low(KT - 1)

            def chunks(ap):
                return ap[:, 0:T].rearrange("p (c t) -> p c t", c=NC_)

            def rows(l, part):
                if part == 2:
                    W(dve, "rex_a", l)
                    tt(QB[32:36, :], rb, t5, ALU.mult, "rows_v")
                    return
                n4 = slice(0, 4)
                m = RM[0:4, :]
                r = RA[0:4, :]
                if part == 1:
                    tt(r, fa, m, ALU.subtract)
                    tt(t2, ri, fa, ALU.subtract)
                    ts(QA[64:68, :], gg, -1.0, ALU.mult)
                    cp(QB[64:68, :], gg)
                    tt(chunks(t4), chunks(gg)[:, :, C - 1:C].broadcast_to([4, NC_, C]), chunks(gg), ALU.subtract)
                    done()
                    cp(t1[:, 0:C], r[:, 0:C])
                    tt(t1[:, C:T].rearrange("p (c t) -> p c t", t=C), r[:, C:T].rearrange("p (c t) -> p c t", t=C),
                       chunks(m)[:, 0:NC_ - 1, C - 1:C].broadcast_to([4, NC_ - 1, C]), ALU.add)
                    tt(t1[:, T:TOK], r[:, T:TOK], pr("m0", n4), ALU.add)
                    cp(QA[0:4, :], t2)
                    tt(chunks(t3), chunks(t2), chunks(r)[:, :, C - 1:C].broadcast_to([4, NC_, C]), ALU.add)
                    tt(t3[:, T:TOK], t2[:, T:TOK], r[:, T:TOK], ALU.add, "rpre_v")
                    return
                W(dve, "z_evac", l, 1)
                W(dve, "rsp_a", l)
                own(dve, "h_lo")
                stt(rf, rf, 0.0, fa, ALU.min, ALU.subtract)
                stt(ra, ra, 0.0, aa, ALU.max, ALU.add)
                ts(rb, rb, 1.0, ALU.add)
                done()
                ts(ra, ra, EA, ALU.mult, -1.0, ALU.mult)
                inc(dve.reciprocal(rb, rb), "v_ord")
                inc(dve.tensor_tensor_scan(fa[:, 0:T], reset[0:4, :], rf[:, 0:T], 0.0, ALU.mult, ALU.add), "v_ord")
                cp(fa[:, T:TOK], rf[:, T:TOK])
                inc(dve.tensor_tensor_scan(m[:, 0:T], rf[:, 0:T], ri[:, 0:T], 0.0, ALU.add, ALU.max), "v_ord")
                tt(t2[:, T:TOK], rf[:, T:TOK], pr("m0", n4), ALU.add)
                done()
                tt(m[:, T:TOK], t2[:, T:TOK], ri[:, T:TOK], ALU.max)
                inc(dve.tensor_tensor_scan(gg[:, 0:T], reset[0:4, :], ra[:, 0:T], 0.0, ALU.mult, ALU.add), "v_ord")
                cp(gg[:, T:TOK], ra[:, T:TOK])
                cp(QB[0:4, :], rb)
                done()

            def conv(l, j):
                dve.wait_ge(sem["hist_d"], 96 * (l + 1))
                W(dve, "z_evac", l, j + 2)
                W(dve, "zero_g", l, 4)
                a = PAR["conv"][0]
                for w in range(KCH):
                    src, k = CB[:, j, w:w + CV], par[:, a + 4 * j + w:a + 4 * j + w + 1]
                    if w == 0:
                        ts(CY[:, j, :], src, k, ALU.mult, name="conv_v")
                    else:
                        dve.wait_ge(sem["conv_v"], l * 24 + 4 * j + w)
                        stt(CY[:, j, :], src, k, CY[:, j, :], ALU.mult, ALU.add, "conv_v")

            def l2(l):
                for i in range(2):
                    W(dve, "rs2_a", l, i + 1)
                    q = CB[:, 2 * i:2 * i + 2, 0:TOK]
                    tt(q, q, LS[:, 2 * i:2 * i + 2, :], ALU.mult, "l2_v")

            def by_head(ap):
                return ap.rearrange("p (h e) -> p h e", h=HEADS)

            def tcol(c, j):
                return TQ[:, c, j, :].rearrange("p (h o) -> p h o", o=1).broadcast_to([P, HEADS, DH])

            def gtok(l):
                W(dve, "tq_a", l)
                for c in range(NC_):
                    W(dve, "gtok_p", l, c + 1)
                    tt(by_head(KD[:, c, :]), by_head(M[c][:, 0:256]), tcol(c, 3), ALU.mult, "gtok_v")
                    tt(by_head(BK[:, c, :]), by_head(M[c][:, 0:256]), tcol(c, 5), ALU.mult, "gtok_v")
                    tt(by_head(BV[:, c, :]), by_head(M[c][:, 256:512]), tcol(c, 4), ALU.mult, "gtok_v")

            def c4(ap):
                return ap.rearrange("p (c t) -> p c t", c=NC_)

            def bc4(ap):
                return ap.rearrange("p (o t) -> p o t", o=1).broadcast_to([P, NC_, P])

            def glog(l, head):
                h = head % 2
                W(dve, "glog_p", l, head + 1)
                if head == 2:
                    W(dve, "zt_p", l, 12)
                tt(EB[:, h, :, :], c4(M[0]), bc4(neg), ALU.add, "eb_v")
                W(dve, "ebx_a", l, head + 1)
                tt(PM[:, head, :, :], c4(M[2]), EB[:, h, :, :], ALU.mult, "pm_v")
                own(dve, "pm_v")
                tt(EB[:, h, :, :], c4(M[1]), EB[:, h, :, :], ALU.mult)
                done()
                tt(AT[:, h, :, :], c4(M[3]), EB[:, h, :, :], ALU.mult, "at_v")

            def eight(ap):
                return ap.rearrange("p h c t -> p (h c) t")

            def inv(l, hp):
                own(dve, "at_v")
                if hp:
                    W(dve, "y_p", l, 12)
                tt(eight(CT), eight(AT), lvl[:, 0:1, :].broadcast_to([P, 8, P]), ALU.mult)
                done()
                stt(eight(XT), eight(CT), -1.0, ident.rearrange("p (o t) -> p o t", o=1).broadcast_to([P, 8, P]),
                    ALU.mult, ALU.add, "xt0_v")
                for v in range(1, 7):
                    if v < 6:
                        for h in range(2):
                            n = 10 * hp + 2 * (v - 1) + h
                            W(dve, "z_p", l, n + 1)
                            if v == 1:
                                W(dve, "xm_a", l, 2 * hp + h + 1)
                            else:
                                W(dve, "xu_v", l, n - 1)
                            x = XM[:, h, :, :].rearrange("p c t -> p (c t)")
                            tt(x, x, M[2 + h], ALU.subtract, "xu_v")
                    for h in range(2):
                        n = 12 * hp + 2 * (v - 1) + h
                        W(dve, "zt_p", l, n + 1)
                        if v == 1:
                            W(dve, "xt0_v", l, hp + 1)
                        else:
                            W(dve, "xtu_v", l, n - 1)
                        x = XT[:, h, :, :].rearrange("p c t -> p (c t)")
                        tt(x, x, M[h], ALU.subtract, "xtu_v")

            def uw(l, hp):
                W(dve, "uw_p", l, hp + 1)
                for h in range(2):
                    a = hp * P + h * DH
                    cp(U[:, :, a:a + DH], M[0].rearrange("p (h c e) -> p h c e", h=2, c=NC_)[:, h, :, :], "uw_v")
                for h in range(2):
                    r = slice(h * DH, (h + 1) * DH)
                    last = dve.tensor_copy(ST[r, 0:NC_, hp, 1, :], c4(M[1 + h])[r])
                inc(last, "uw_v")

            def qe(l):
                W(dve, "qe_a", l)
                W(dve, "uw_p", l, 2)
                tt(QE.rearrange("p h c t -> p h (c t)"), CB[:, 0:2, 0:T], EGB[:, :, 0:T], ALU.mult, "qe_v")

            def carry(l, c, ps, decay, kinds):
                for hp in range(2):
                    for h in range(2):
                        r, e = slice(h * DH, (h + 1) * DH), slice(h * DH, (h + 1) * DH)
                        stt(ST[r, c + 1, hp, 0:kinds, e], ST[r, c, hp, 0:kinds, e],
                            decay[r, hp, c * C + C - 1:c * C + C], ps(hp)[r, :, e], ALU.mult, ALU.add, "st_v")

            def gst(l):
                W(dve, "zero_g", l, 4)
                own(dve, "uw_v")
                own(dve, "qe_v")
                for c in range(NC_):
                    if c:
                        W(dve, "gst_p", l, c)
                        tt(VN[:, c, :], U[:, c, :], M[0][:, 0:256], ALU.subtract, "vn_v")
                    else:
                        cp(VN[:, 0, :], U[:, 0, :], "vn_v")
                    W(dve, "gsd_p", l, c + 1)
                    if c:
                        own(dve, "st_v")
                    carry(l, c, lambda hp: M[1][:, hp * P:(hp + 1) * P].rearrange("p (k e) -> p k e", k=1), EGB, 1)

            def wide(ap):
                return ap.rearrange("p h (b o) -> p h b o", o=1).broadcast_to([P, 2, NB, DH])

            irep4 = irep.rearrange("p (x y e) -> p x y e", x=1, y=1).broadcast_to([P, 2, NB, DH])
            sums = PS[:, 4:6, :].rearrange("p h (b e) -> p h b e", b=NB)

            def sm(i):
                return SM[:, i, :].rearrange("p (h b) -> p h b", h=2)

            def bh(ap):
                return ap.rearrange("p h b e -> p (h b) e")

            def decay_state(l, n, decay):
                dve.wait_ge(sem["state_d"], l * 64 + 16 * n)
                tt(SD, SD, wide(decay), ALU.mult)

            def spread(vec, l, n, first=True):
                tt(DX, wide(vec), irep4, ALU.mult, "dx_v")
                W(dve, "dx_p", l, n)

            def contract(l, n, by, out, name):
                tt(DX, SD, wide(by), ALU.mult, "dx_v")
                W(dve, "dx_p", l, n)
                tt(DX, sums, irep4, ALU.mult)
                done()
                inc(dve.tensor_reduce(out, DX, AX.X, ALU.add), name)

            def gd(l):
                W(dve, "out_p", l, 2)
                q, k, v = (CB[:, 2 * i:2 * i + 2, T:TOK] for i in range(3))
                decay_state(l, 1, EGB[:, :, T:TOK])
                done()
                contract(l, 1, k, sm(0), "v_ord")
                done()
                tt(sm(1), v, sm(0), ALU.subtract)
                W(dve, "beta_p", l)
                done()
                tt(sm(1), sm(1), M[2][:, 0:16].rearrange("p (h b) -> p h b", h=2), ALU.mult)
                done()
                spread(sm(1), l, 2)
                tt(DX, sums, wide(k), ALU.mult)
                done()
                tt(SD, SD, DX, ALU.add)
                done()
                contract(l, 3, q, OG[:, :, T:TOK], "dec_v")

            def hn(l, i):
                o_, sq = ((OG, SQG), (OM, DA), (OL, SQL))[i]
                gate = (GZ, GB[:, 6:8, :], LA[:, 6:8, :])[i]
                y0 = (2, 0, 6)[i]
                W(dve, "hrs_a", l, i + 1)
                if i:
                    W(dve, "gate_a", l, i)
                tt(o_, o_, sq, ALU.mult, "hn_v")
                own(dve, "hn_v")
                for j in range(2):
                    a = PAR[("n_gdn", "n_mlstm", "n_gla")[i]][0] + j
                    stt(Y[:, y0 + j, :], o_[:, j, :], par[:, a:a + 1], gate[:, j, :], ALU.mult, ALU.mult, "hn_v")

            def mtok(l):
                for c in range(NC_):
                    W(dve, "vp_a", l, 8 + 2 * c + 2)
                    tt(by_head(KD[:, c, :]), by_head(M[c][:, 0:256]), tcol(c, 1), ALU.mult, "mkd_v")

            def mst(l):
                W(dve, "kind_g", l)
                W(dve, "mbc_a", l)
                for c in range(NC_):
                    W(dve, "up_p", l, c + 1)
                    own(dve, "st_v")
                    carry(l, c, lambda hp: M[c][:, hp * 256:(hp + 1) * 256].rearrange("p (k e) -> p k e", k=2), WI, 2)

            def mlog(l):
                W(dve, "dec_v", l, 1)
                W(dve, "so_g", l, 1)
                for head in range(HEADS):
                    a = 2 * (head % 2)
                    W(dve, "mlog_p", l, head + 1)
                    tt(EM[:, head % 2, :, :], c4(M[a]), bc4(neg), ALU.add, "em_v")
                    W(dve, "emx_a", l, head + 1)
                    tt(PM[:, head, :, :], c4(M[a + 1]), EM[:, head % 2, :, :], ALU.mult, "mpm_v")
                W(dve, "z_evac", l, 11)
                tt(GB[:, 0:2, 0:T], GB[:, 0:2, 0:T], WI[:, :, 0:T], ALU.mult, "qw_v")

            def mout(l):
                W(dve, "da_a", l)
                tt(DA[:, :, 0:T], DA[:, :, 0:T], EMN[:, :, 0:T], ALU.max)
                done()
                inc(dve.reciprocal(DA[:, :, 0:T], DA[:, :, 0:T]), "v_ord")
                done()
                tt(OM[:, :, 0:T], PS[:, 4:6, :], DA[:, :, 0:T], ALU.mult, "mo_v")

            def md(l):
                q, k, v = (GB[:, 2 * i:2 * i + 2, T:TOK] for i in range(3))
                W(dve, "z_evac", l, 15)
                decay_state(l, 3, WI[:, :, T:TOK])
                tt(sm(1), sm(2), k, ALU.mult)
                tt(NS, NS, WI[:, :, T:TOK], ALU.mult)
                W(dve, "out_p", l, 4)
                spread(v, l, 4)
                done()
                tt(DX, sums, wide(sm(1)), ALU.mult)
                tt(NS, NS, sm(1), ALU.add, "nsn_v")
                own(dve, "nsn_v")
                tt(sm(3), NS, q, ALU.mult, "nq_v")
                done()
                tt(SD, SD, DX, ALU.add)
                done()
                contract(l, 5, q, sm(4), "v_ord")
                W(dve, "nd_a", l)
                tt(sm(5), sm(5), EMN[:, :, T:TOK], ALU.max)
                done()
                inc(dve.reciprocal(sm(5), sm(5)), "v_ord")
                done()
                tt(OM[:, :, T:TOK], sm(4), sm(5), ALU.mult, "dec_v")

            def lg(l):
                W(dve, "lsp_a", l)
                stt(GG, GG, 0.0, EG, ALU.min, ALU.subtract)
                done()
                ts(GG, GG, 1.0 / 16.0, ALU.mult)
                done()
                for hp in range(2):
                    inc(dve.tensor_tensor_scan(EG[:, hp, 0:T], reset, GG[:, hp, 0:T], 0.0, ALU.mult, ALU.add), "v_ord")
                inc(dve.tensor_copy(EG[:, :, T:TOK], GG[:, :, T:TOK]), "lcum_v")

            def pc(ap):
                return ap[:, :, 0:T].rearrange("p h (c t) -> p h c t", c=NC_)

            def lk(l):
                W(dve, "lk_a", l)
                W(dve, "z_evac", l, 21)
                tt(KI[0], KI[0], pc(LA[:, 2:4, :]), ALU.mult, "lke_v")

            def lst(l):
                W(dve, "leg_a", l)
                for c in range(NC_):
                    W(dve, "up_p", l, 4 + c + 1)
                    own(dve, "st_v")
                    carry(l, c, lambda hp: M[c][:, hp * P:(hp + 1) * P].rearrange("p (k e) -> p k e", k=1), GG, 1)

            def lsub(l):
                W(dve, "hn_v", l, 6)
                W(dve, "lcum_v", l)
                g16 = EG[:, :, 0:T].rearrange("p h (i t) -> p h i t", t=SUB)
                q16 = QI[:, :, 0:T].rearrange("p h (i t) -> p h i t", t=SUB)
                ref = g16[:, :, :, SUB // 2 - 1:SUB // 2]
                tt(q16, g16, ref.broadcast_to([P, 2, NC_ * NSUB, SUB]), ALU.subtract, "lsub_v")
                W(dve, "ltok_p", l)
                W(dve, "ki0_g", l)
                for i in range(NSUB):
                    w = (i + 1) * SUB
                    at = i * SUB + SUB // 2 - 1
                    g = pc(EG)
                    tt(KI[i][:, :, :, 0:w], g[:, :, :, at:at + 1].broadcast_to([P, 2, NC_, w]), g[:, :, :, 0:w],
                       ALU.subtract, "lsub_v")
                W(dve, "lsub_a", l, 1)
                tt(QI[:, :, 0:T], QI[:, :, 0:T], LA[:, 0:2, 0:T], ALU.mult, "ki_v")
                for i in range(NSUB):
                    w = (i + 1) * SUB
                    W(dve, "lsub_a", l, i + 2)
                    tt(KI[i][:, :, :, 0:w], KI[i][:, :, :, 0:w], pc(LA[:, 2:4, :])[:, :, :, 0:w], ALU.mult, "ki_v")

            def llog(l):
                W(dve, "so_g", l, 2)
                for head in range(HEADS):
                    W(dve, "llog_p", l, head + 1)
                    tt(PM[:, head, :, :], c4(M[head]), bc4(tri), ALU.mult, "lpm_v")
                own(dve, "ki_v")
                tt(LA[:, 0:2, 0:T], LA[:, 0:2, 0:T], GG[:, :, 0:T], ALU.mult, "lqe_v")

            def ld(l):
                q, k, v = (LA[:, 2 * i:2 * i + 2, T:TOK] for i in range(3))
                decay_state(l, 4, GG[:, :, T:TOK])
                spread(v, l, 6)
                tt(DX, sums, wide(k), ALU.mult)
                done()
                tt(SD, SD, DX, ALU.add)
                done()
                contract(l, 7, q, OL[:, :, T:TOK], "dec_v")

            def sc(l):
                W(dve, "z_evac", l, 31)
                W(dve, "spad_g", l)
                own(dve, "hn_v")
                w3 = SCB[:, :, T + KSC - 1:SW - 1].rearrange("p j (b w) -> p j b w", w=KSC)
                tt(SCB[:, :, KSC - 1:KSC - 1 + T], GB[:, 2:4, 0:T], GB[:, 4:6, 0:T], ALU.mult)
                tt(w3[:, :, :, KSC - 1], GB[:, 2:4, T:TOK], GB[:, 4:6, T:TOK], ALU.mult, "scu_v")
                dve.wait_ge(sem["shist_d"], 32 * (l + 1))
                own(dve, "scu_v")
                a = PAR["sconv"][0]
                for w in range(KSC):
                    if w:
                        done()
                    for j in range(2):
                        src, k = SCB[:, j, w:w + SV], par[:, a + 3 * j + w:a + 3 * j + w + 1]
                        if w == 0:
                            ts(SCY[:, j, :], src, k, ALU.mult)
                        else:
                            stt(SCY[:, j, :], src, k, SCY[:, j, :], ALU.mult, ALU.add)
                done()
                tt(Y[:, 4:6, 0:T], GB[:, 0:2, 0:T], SCY[:, :, 0:T], ALU.mult, "sc_v")
                tt(Y[:, 4:6, T:TOK], GB[:, 0:2, T:TOK], SCY[:, :, T + KSC - 1:SV:KSC], ALU.mult, "sc_v")

            def ysp(l):
                own(dve, "sc_v")
                for k in range(KT):
                    dve.wait_ge(sem["h_hi"], l * 24 + 8 + k + 1)
                    tt(Hlo[:, k, :], Y[:, k, :], Hhi[:, k, :].bitcast(F32), ALU.subtract, "h_lo")

            def router():
                a, b = PAR["router"]
                dve.wait_ge(sem["rexp_a"], 1)
                tt(RWlo[:, :], par[:, a:b], RWhi[:, :].bitcast(F32), ALU.subtract, "rwlo_v")
                L, E1, S1, L2, EX, S2, WT_, G = (RTK[:, i, :, :] for i in range(8))
                inc(dve.memset(RTK[:, :, :, :], 0.0), "v_ord")
                dve.wait_ge(sem["rt_p"], 1)
                done()
                rb_ = PAR["router_b"]
                bias = par[:, rb_[0]:rb_[1]].rearrange("p (o e) -> p o e", o=1)
                tt(L[:, 0:4, :], M[0][:, 0:32].rearrange("p (i e) -> p i e", e=8), bias.broadcast_to([P, 4, 8]), ALU.add)
                tt(L[0:NB, 4:5, :], M[0][0:NB, 32:40].rearrange("p (i e) -> p i e", e=8), bias[0:NB], ALU.add)
                done()
                rev = cn("rev").rearrange("p (o e) -> p o e", o=1).broadcast_to([P, 5, 8])

                def col(i):
                    return RC[:, i, :].rearrange("p (i o) -> p i o", o=1).broadcast_to([P, 5, 8])

                def best(src, out, i):
                    inc(dve.tensor_reduce(RC[:, i, :], src, AX.X, ALU.max), "v_ord")
                    done()
                    tt(E1, src, col(i), ALU.is_equal)
                    done()
                    tt(E1, E1, rev, ALU.mult)
                    done()
                    inc(dve.tensor_reduce(RC[:, 2, :], E1, AX.X, ALU.max), "v_ord")
                    done()
                    tt(out, E1, col(2), ALU.is_equal)
                    done()
                best(L, S1, 0)
                tt(EX, L, col(0), ALU.subtract, "rl_v")
                for i in range(5):
                    low_tokens(i)
                stt(L2, S1, -1e30, L, ALU.mult, ALU.add)
                done()
                best(L2, S2, 1)
                tt(S1, S1, S2, ALU.add)
                done()
                tt(S1, S1, cn("valid").rearrange("p (i o) -> p i o", o=1).broadcast_to([P, 5, 8]), ALU.mult, "sel_v")
                own(dve, "sel_v")
                dve.wait_ge(sem["rexp_a"], 2)
                tt(WT_, S1, EX, ALU.mult)
                done()
                inc(dve.tensor_reduce(RC[:, 3, :], WT_, AX.X, ALU.add), "v_ord")
                done()
                ts(RC[:, 3, :], RC[:, 3, :], 1e-30, ALU.max)
                done()
                inc(dve.reciprocal(RC[:, 3, :], RC[:, 3, :]), "v_ord")
                done()
                tt(G, WT_, col(3), ALU.mult)
                done()
                cp(GH[:, :, :, 0], G)
                done()
                tt(GH[:, :, :, 1], G, GH[:, :, :, 0].bitcast(F32), ALU.subtract)
                dve.wait_ge(sem["rt_p"], 2)
                tt(KEY[:, :, :], M[1][:, 0:40].rearrange("p (i e) -> p i e", e=8), S1, ALU.mult, "key_v")
                inc(dve.tensor_reduce(RC[0:1, 0, 0:1], M[2][0:1, 0:8], AX.X, ALU.max), "key_v")
                own(dve, "key_v")
                ts(RC[0:1, 1, 0:4], cn("caps", slice(0, 1)), RC[0:1, 0, 0:1], ALU.is_lt)
                done()
                inc(dve.tensor_reduce(RC[0:1, 2, 0:1], RC[0:1, 1, 0:4], AX.X, ALU.add), "v_ord")
                done()
                ts(NI[0:1, 0:1], RC[0:1, 2, 0:1], float(EXPERTS), ALU.mult, -1.0, ALU.add, name="turns_v")

            def low_tokens(i):
                n = P if i < 4 else NB
                dve.wait_ge(sem["ht_p"], i + 1)
                inc(dve.tensor_copy(HTl[0:n, i, :].rearrange("p (a b) -> p a b", a=2), PS[0:n, 2:4, :]), "htl_v")

            split_at(0)
            split_at(1)
            dve.wait_ge(sem["load_con"], 16)
            STEPS = dict(rows=rows, conv=conv, l2=l2, gtok=gtok, glog=glog, inv=inv, uw=uw, qe=qe, gst=gst,
                         gd=gd, hn=hn, mtok=mtok, mst=mst, mlog=mlog, mout=mout, md=md, lg=lg, lk=lk, lst=lst,
                         lsub=lsub, llog=llog, ld=ld, sc=sc, ysp=ysp)

            for l in range(LAYERS):
                for step in ORDER:
                    name, arg = step if isinstance(step, tuple) else (step, None)
                    if name == "z":
                        z(l, arg)
                    elif name == "o":
                        o(l, arg)
                    elif name == "rnm":
                        rn(l, 2 * l)
                    elif name == "rnf":
                        rn(l, 2 * l + 1)
                    elif name in STEPS:
                        STEPS[name](l) if arg is None else STEPS[name](l, arg)
                if l == 1:
                    break
                base = ZU + OU
                dve.wait_ge(sem["stored_g"], 1)

                def group(e, last):
                    def split_next(i):
                        if last and i + 2 >= EU:
                            split_at(base + e * EU + i + 2)
                            return
                        g = base + i + 2
                        split(e * EU + g, GF if 2 * GF <= (i + 2) % EU else KT, g % SPLIT, g % RAW)

                    for f in range(GF):
                        split_next(2 * f)
                        dve.wait_ge(sem["unit_done"], e * EU + (base + 2 * f + 2))
                        dve.wait_ge(sem["silu_g"], e * GF + (f + 1))
                        af = AF[:, f % 2, :]
                        tt(halves(af), slot(2 + f % 2), halves(SG[:, f % 2, :]), ALU.mult, "af_v")
                        split_next(2 * f + 1)
                        dve.wait_ge(sem["ahi_a"], e * GF + (f + 1))
                        tt(Alo[:, f, :], af, Ahi[:, f, :].bitcast(F32), ALU.subtract, "glu_v")
                    for m in range(KT):
                        dve.wait_ge(sem["unit_done"], e * EU + (base + 2 * GF + m + 1))
                        tt(halves(X[:, m, :]), slot(DOWN_SLOT[m]), halves(X[:, m, :]), ALU.add, "down_v")
                        split_next(2 * GF + m)

                before = dict(count)
                with dve.Fori(0, DENSE - 1) as e:
                    group(e, False)
                looped(before, DENSE - 1)
                group(DENSE - 1, True)

            router()
            base = UB[1] + ZU + OU

            def split_turn(it, i):
                i += 2
                n = (GF if 2 * GF <= i % EU else KT) * P
                hi, lo = split_e(i)
                dve.wait_ge(sem["w_hi"], it * EU + (base + i + 1))
                inc(dve.tensor_tensor(lo[:, 0:n], raw_e(i)[1][:, 0:n], hi[:, 0:n].bitcast(F32), ALU.subtract), "w_lo")

            def expert(ap, e):
                return ap[:, :, e:e + 1] if isinstance(e, int) else ap[:, :, bass.ds(e, 1)]

            def select(e, it):
                cp(KC[:, :].rearrange("p (i o) -> p i o", o=1), expert(KEY, e), "kc_v")
                dve.wait_ge(sem["kc_v"], it + 1)
                for i in range(5):
                    ts(SelG[:, i, :], cn("slots"), KC[:, i:i + 1], ALU.is_equal, name="keyt_v")
                ts(expert(KEY, e), expert(KEY, e), float(-CAP), ALU.add, name="selg_v")

            def keys(e, it):
                col_ = ident[0:8, e:e + 1] if isinstance(e, int) else ident[0:8, bass.ds(e, 1)]
                dve.wait_ge(sem["selt_v"], 2 * it) if not isinstance(it, int) or it else None
                ts(KTM, KEYT, col_, ALU.mult, name="ktm1_v")
                neg_ = cn("ncap", slice(0, 8))
                neg_ = neg_[:, e:e + 1] if isinstance(e, int) else neg_[:, bass.ds(e, 1)]
                dve.wait_ge(sem["ktm1_v"], it + 1)
                ts(KEYT, KEYT, neg_, ALU.add, name="keyt_v")
                g = GH[:, :, e, :] if isinstance(e, int) else \
                    GH[:, :, bass.ds(e, 1), :].rearrange("p i o w -> p i (o w)")
                cp(GE[:, :, :], g.bitcast(F32), "ktm_v")

            def gathered(it):
                for k in range(KT):
                    dve.wait_ge(sem["hg_p"], it * KT + (k + 1))
                    cp(Hgl[:, k, :], PS[:, 2 * (k % 2) + 1, 0:CAP], "hgl_v")

            def add(it, tiles_):
                for m in tiles_:
                    dve.wait_ge(sem["sc_p"], it * KT + (m + 1))
                    tt(halves(X[:, m, :]), slot(2 + m % 2), halves(X[:, m, :]), ALU.add, "xadd_v")

            def turn(it, before=None):
                e = it if isinstance(it, int) else it % EXPERTS
                e1 = it + 1 if isinstance(it, int) else (it + 1) % EXPERTS
                for f in range(GF):
                    split_turn(it, 2 * f)
                    dve.wait_ge(sem["unit_done"], it * EU + (base + 2 * f + 2))
                    dve.wait_ge(sem["ssilu_a"], it * GF + (f + 1))
                    af = AFG[:, f % 2, :]
                    tt(af, PS[:, 2 + f % 2, 0:CAP], SGG[:, f % 2, :], ALU.mult, "saf_v")
                    split_turn(it, 2 * f + 1)
                    dve.wait_ge(sem["sahi_a"], it * GF + (f + 1))
                    tt(Agl[:, f, :], af, Agh[:, f, :].bitcast(F32), ALU.subtract, "sglu_v")
                    if before is not None and 2 <= f < 6:
                        add(before, range(2 * f - 4, 2 * f - 2))
                    if f == 4:
                        keys(e, it)
                    if f == 7:
                        dve.wait_ge(sem["key_p"], it + 1)
                        if before is not None:
                            dve.wait_ge(sem["sc_p"], it * KT)
                        for st, n in SLOTS:
                            ts(halves(SelT[0:n, st, :]), PS[0:n, 4:6, 0:HALF], cn("slotp", slice(0, n))[:, st:st + 1],
                               ALU.is_equal, name="selt_v")
                        for st, n in SLOTS:
                            last = dve.tensor_reduce(GC[0:n, st:st + 1], PS[0:n, 6, 2 * st:2 * st + 2], AX.X, ALU.add)
                        inc(last, "gc_v")
                    if f == 8:
                        select(e1, it + 1)
                for m in range(KT):
                    if m == 2:
                        gathered(it + 1)
                    split_turn(it, 2 * GF + m)
                for st, n in SLOTS:
                    dve.wait_ge(sem["yhi_a"], it * 2 + (st + 1))
                    b = 6 if st == 0 else 4
                    stt(Ylo[0:n, st, :].rearrange("p (a b) -> p a b", a=2), PS[0:n, b:b + 2, :], GC[0:n, st:st + 1],
                        Yhi[0:n, st, :].rearrange("p (a b) -> p a b", a=2).bitcast(F32), ALU.mult, ALU.subtract, "ylo_v")

            own(dve, "turns_v")
            own(dve, "v_ord")
            final = dve.value_load(NI[0:1, 0:1], min_val=EXPERTS - 1, max_val=EXPERTS * ROUNDS - 1)
            dve.wait_ge(sem["kt_a"], 2)
            select(0, 0)
            gathered(0)
            turn(0)
            with dve.Fori(0, final) as before:
                turn(before + 1, before)
            add(final, range(KT))
            rn(LAYERS, 4)

        return count


def tiles(w, kt):
    k, m = w.shape[-2:]
    lead = w.shape[:-2]
    w = w.reshape(*lead, kt, P, m // P, P)
    n = len(lead)
    return np.ascontiguousarray(np.moveaxis(w, n + 2, n)).swapaxes(n + 1, n + 2).reshape(*lead, m // P, P, kt * P)


def feature_tiles(a):
    return np.moveaxis(a.reshape(*a.shape[:-1], a.shape[-1] // P, P), (-1, -2), (0, 1))


def lay_out(i):
    f = np.float32
    out = {}
    x = np.concatenate([i["x_prompt"][0], i["x_sample"][:, 0]], 0)
    out["xT"] = np.ascontiguousarray(x.T).reshape(KT, P, TOK)
    w = i["w_in"]
    G = 256
    m0, g0 = 0, 4 * G + 8
    s0 = g0 + 4 * G + 8
    l0 = s0 + 3 * G
    small = np.zeros((LAYERS, D, P), f)
    for at, a, n in ((0, m0 + 4 * G, 4), (32, m0 + 4 * G + 4, 4), (64, g0 + 4 * G, 4), (96, g0 + 4 * G + 4, 4),
                     (4, l0 + 4 * G, 16)):
        small[:, :, at:at + n] = w[:, :, a:a + n]
    z = np.concatenate([small, w[:, :, g0:g0 + 4 * G], w[:, :, m0:m0 + 4 * G], w[:, :, l0:l0 + 4 * G],
                        w[:, :, s0:s0 + 3 * G]], -1)
    out["wz"] = tiles(z, KT)
    out["wo"] = tiles(i["w_out"], KT)
    FE = GF * P
    gate = np.concatenate([i["ffn_w_gate"][0].reshape(D, 2, FE).swapaxes(0, 1), i["moe_w_gate"][0]], 0)
    up = np.concatenate([i["ffn_w_up"][0].reshape(D, 2, FE).swapaxes(0, 1), i["moe_w_up"][0]], 0)
    down = np.concatenate([i["ffn_w_down"][0].reshape(2, FE, D), i["moe_w_down"][0]], 0)
    out["wgu"] = np.stack([tiles(gate, KT), tiles(up, KT)], 2).reshape(GEXP, 2 * GF, P, KT * P)
    out["wd"] = tiles(down, GF)
    out["con"] = constants()
    par = np.zeros((LAYERS, P, PARW), f)

    def put(name, a, rows=slice(0, P), cols=None):
        s = PAR[name][0] + (0 if cols is None else cols)
        a = a.reshape(LAYERS, a.shape[1], -1)
        par[:, rows, s:s + a.shape[2]] = a

    def cols(a):
        return np.moveaxis(feature_tiles(a), 2, 0)

    put("g_mix", cols(i["g_mix"]))
    put("g_ffn", cols(i["g_ffn"]))
    put("g_final", np.broadcast_to(feature_tiles(i["g_final"]), (LAYERS, P, KT)))
    put("n_mlstm", cols(i["mlstm_norm"]))
    put("n_gdn", cols(i["gdn_norm"]))
    put("n_gla", cols(i["gla_norm"]))
    put("conv", i["gdn_conv_w"].reshape(LAYERS, 6, P, KCH).swapaxes(1, 2))
    put("sconv", i["sc_conv_w"].reshape(LAYERS, 2, P, KSC).swapaxes(1, 2))
    put("gla_b", cols(i["gla_b_gate"]))
    put("gate_b", i["mlstm_b_i"], slice(0, 4))
    put("gate_b", i["mlstm_b_f"], slice(32, 36))
    put("gate_b", i["gdn_dt_bias"], slice(64, 68))
    put("a_log", i["gdn_a_log"], slice(0, 4))
    put("m0", i["state_mlstm_m"].swapaxes(1, 2), slice(0, 4))
    put("wgate", i["gla_w_gate"], slice(100, 116))
    par[1, :, PAR["router"][0]:PAR["router"][1]] = \
        i["moe_w_router"][0].reshape(KT, P, EXPERTS).swapaxes(0, 1).reshape(P, -1)
    par[1, :, PAR["router_b"][0]:PAR["router_b"][1]] = i["moe_b_router"][0][None]
    out["par"] = par

    def state(s):
        s = s.reshape(LAYERS, NB, 2, 2, DH, DH).transpose(0, 3, 4, 2, 1, 5)
        return np.ascontiguousarray(s).reshape(LAYERS, P, 2, NB, DH)

    out["mC"], out["gS"], out["lS"] = (state(i[n]) for n in ("state_mlstm_C", "state_gdn_S", "state_gla_S"))
    n = i["state_mlstm_n"].reshape(LAYERS, NB, 2, 2, DH).transpose(0, 3, 4, 2, 1)
    out["mn"] = np.ascontiguousarray(n).reshape(LAYERS, P, 2, NB)
    c = i["state_gdn_conv"].reshape(LAYERS, NB, KCH - 1, 6, P).transpose(0, 3, 4, 1, 2)
    out["gconv"] = np.ascontiguousarray(c)
    c = i["state_sc_conv"].reshape(LAYERS, NB, KSC - 1, 2, P).transpose(0, 3, 4, 1, 2)
    out["sconv"] = np.ascontiguousarray(c)
    return out


OUTPUTS = dict(y=(KT, P, TOK), mC_p=(LAYERS, P, 2, DH), mC_s=(LAYERS, P, 2, NB, DH), gS_p=(LAYERS, P, 2, DH),
               gS_s=(LAYERS, P, 2, NB, DH), lS_p=(LAYERS, P, 2, DH), lS_s=(LAYERS, P, 2, NB, DH),
               mn=(LAYERS, P, 2, NB + 1), mm=(LAYERS, HEADS, TOK), gtail=(LAYERS, P, 6, 27), stail=(LAYERS, P, 2, 18))


def results(r):
    y = r["y"].reshape(D, TOK).T
    y_p, y_s = y[None, 0:T], y[T:TOK, None]

    def state(s, b):
        s = s.reshape(LAYERS, 2, DH, 2, b, DH).transpose(0, 4, 3, 1, 2, 5)
        return s.reshape(LAYERS, b, HEADS, DH, DH)

    def tail(t, j, w):
        t = t.reshape(LAYERS, P, j, NB + 1, w).transpose(0, 3, 4, 2, 1).reshape(LAYERS, NB + 1, w, j * P)
        return t[:, 0:1], t[:, 1:]

    n = r["mn"].reshape(LAYERS, 2, DH, 2, NB + 1).transpose(0, 4, 3, 1, 2).reshape(LAYERS, NB + 1, HEADS, DH)
    m = r["mm"].transpose(0, 2, 1)
    gt, st = tail(r["gtail"], 6, KCH - 1), tail(r["stail"], 2, KSC - 1)
    out = (y_p, y_s, state(r["mC_p"], 1), state(r["mC_s"], NB), n[:, 0:1], n[:, 1:], m[:, T - 1:T], m[:, T:TOK],
           state(r["gS_p"], 1), state(r["gS_s"], NB), gt[0], gt[1], st[0], st[1],
           state(r["lS_p"], 1), state(r["lS_s"], NB))
    return tuple(np.ascontiguousarray(a) for a in out)


def kernel(**inputs):
    import concourse.bacc as _bacc
    from concourse.bass_utils import run_bass_kernel_spmd as _run

    arrays = lay_out({k: np.asarray(v) for k, v in inputs.items()})
    nc = _bacc.Bacc("TRN2", target_bir_lowering=False, num_devices=1)
    ins = {k: nc.dram_tensor(f"in_{k}", a.shape, F32, kind="ExternalInput").ap() for k, a in arrays.items()}
    outs = {k: nc.dram_tensor(f"out_{k}", s, F32, kind="ExternalOutput").ap() for k, s in OUTPUTS.items()}
    build(nc, ins, outs)
    r = _run(nc, [{f"in_{k}": a for k, a in arrays.items()}], core_ids=[0])
    return results({k: r.results[0][f"out_{k}"] for k in OUTPUTS})
```
